# Optimizing a Trainium2 kernel written in Bass

```python
import math
import jax
import jax.numpy as jnp
from jax import lax
import numpy as np

D_MODEL = 1024
BATCH = 1
SEQ = 512
DEPTH = 2

HEAD_DIM = 64
MLA_HEADS = 8
MLA_NOPE = 64
MLA_ROPE = 32
MLA_V = 64
MLA_Q_LORA = 384
MLA_KV_LORA = 256
ROPE_THETA = 10000.0
MOBA_HEADS = 8
MOBA_BLOCK = 256
MOBA_TOPK = 3
MOBA_QCHUNK = 32
SB_HEADS = 16
Q_BLOCK = 128
NUM_BUCKETS = 32
MAX_DISTANCE = 128
RMS_EPS = 1e-6
D_FF = -(-8 * D_MODEL // (3 * 256)) * 256
N_EVEN = (DEPTH + 1) // 2
N_ODD = DEPTH // 2
AB_IN = MLA_Q_LORA + MLA_KV_LORA + MLA_ROPE + 3 * MOBA_HEADS * HEAD_DIM
AB_OUT = MLA_HEADS * MLA_V + MOBA_HEADS * HEAD_DIM
SB_WIDTH = SB_HEADS * HEAD_DIM

kernel_name = 'hybrid_mla_moba_stickbreaking'

def rmsnorm(x, g):
    xf = x.astype(jnp.float32)
    y = xf * lax.rsqrt(jnp.mean(xf * xf, axis=-1, keepdims=True) + RMS_EPS)
    return (y * g.astype(jnp.float32)).astype(x.dtype)

def rope(x, pos):
    half = x.shape[-1] // 2
    inv_freq = ROPE_THETA ** (-jnp.arange(half, dtype=jnp.float32) / half)
    ang = pos.astype(jnp.float32)[:, None] * inv_freq[None, :]
    cos, sin = jnp.cos(ang), jnp.sin(ang)
    x1 = x[..., :half].astype(jnp.float32)
    x2 = x[..., half:].astype(jnp.float32)
    return jnp.concatenate([x1 * cos - x2 * sin, x1 * sin + x2 * cos], axis=-1).astype(x.dtype)

def t5_bucket(rel):
    max_exact = NUM_BUCKETS // 2
    rel = jnp.maximum(rel, 0)
    large = max_exact + (jnp.log(jnp.maximum(rel, max_exact).astype(jnp.float32) / max_exact)
                         / math.log(MAX_DISTANCE / max_exact) * (NUM_BUCKETS - max_exact)).astype(jnp.int32)
    large = jnp.minimum(large, NUM_BUCKETS - 1)
    return jnp.where(rel < max_exact, rel, large)

def mla_attention(c_q, c_kv, k_rope_in, q_norm_g, w_uq, kv_norm_g, w_ukv, pos):
    B, S, _ = c_q.shape
    q = jnp.einsum('bsr,rhd->bhsd', rmsnorm(c_q, q_norm_g),
                   w_uq.reshape(MLA_Q_LORA, MLA_HEADS, MLA_NOPE + MLA_ROPE))
    q_nope = q[..., :MLA_NOPE]
    q_rope = rope(q[..., MLA_NOPE:], pos)
    kv = jnp.einsum('bsr,rhd->bhsd', rmsnorm(c_kv, kv_norm_g),
                    w_ukv.reshape(MLA_KV_LORA, MLA_HEADS, MLA_NOPE + MLA_V))
    k_nope, v = kv[..., :MLA_NOPE], kv[..., MLA_NOPE:]
    k_rope = rope(k_rope_in, pos)
    scale = (MLA_NOPE + MLA_ROPE) ** -0.5
    n_blk = S // Q_BLOCK
    qn = q_nope.reshape(B, MLA_HEADS, n_blk, Q_BLOCK, MLA_NOPE).transpose(2, 0, 1, 3, 4)
    qr = q_rope.reshape(B, MLA_HEADS, n_blk, Q_BLOCK, MLA_ROPE).transpose(2, 0, 1, 3, 4)
    kpos = jnp.arange(S)

    def block(args):
        i, qn_b, qr_b = args
        logits = (jnp.einsum('bhqd,bhkd->bhqk', qn_b, k_nope)
                  + jnp.einsum('bhqd,bkd->bhqk', qr_b, k_rope)).astype(jnp.float32) * scale
        qpos = i * Q_BLOCK + jnp.arange(Q_BLOCK)
        logits = jnp.where(kpos[None, :] <= qpos[:, None], logits, -jnp.inf)
        p = jax.nn.softmax(logits, axis=-1).astype(v.dtype)
        return jnp.einsum('bhqk,bhkd->bhqd', p, v)

    out = lax.map(block, (jnp.arange(n_blk), qn, qr))
    return out.transpose(1, 0, 3, 2, 4).reshape(B, S, MLA_HEADS * MLA_V)

def moba_attention(q, k, v, rel_bias):
    B, H, S, d = q.shape
    nb = -(-S // MOBA_BLOCK)
    pad = nb * MOBA_BLOCK - S
    kp = jnp.pad(k, ((0, 0), (0, 0), (0, pad), (0, 0)))
    vp = jnp.pad(v, ((0, 0), (0, 0), (0, pad), (0, 0)))
    kb = kp.reshape(B, H, nb, MOBA_BLOCK, d)
    vb = vp.reshape(B, H, nb, MOBA_BLOCK, d)
    kbar = jnp.mean(kb.astype(jnp.float32), axis=3).astype(k.dtype)
    kk = min(MOBA_TOPK, max(nb - 1, 1))
    scale = d ** -0.5
    n_chunk = S // MOBA_QCHUNK
    qc_all = q.reshape(B, H, n_chunk, MOBA_QCHUNK, d).transpose(2, 0, 1, 3, 4)
    b_idx = jnp.arange(B)[:, None, None, None]
    h_idx = jnp.arange(H)[None, :, None, None]
    bias_t = rel_bias.T
    offs = jnp.arange(MOBA_BLOCK)

    def chunk(args):
        i, q_c = args
        qpos = i * MOBA_QCHUNK + jnp.arange(MOBA_QCHUNK)
        own = (i * MOBA_QCHUNK) // MOBA_BLOCK
        gate = jnp.einsum('bhqd,bhnd->bhqn', q_c, kbar).astype(jnp.float32)
        gate = jnp.where(jnp.arange(nb) < own, gate, -jnp.inf)
        _, idx = lax.top_k(gate, kk)
        valid = idx < own
        kg = kb[b_idx, h_idx, idx]
        vg = vb[b_idx, h_idx, idx]
        rel_sel = qpos[None, None, :, None, None] - (idx[..., None] * MOBA_BLOCK + offs)
        bias_sel = bias_t[h_idx[..., None], t5_bucket(rel_sel)].astype(jnp.float32)
        l_sel = jnp.einsum('bhqd,bhqknd->bhqkn', q_c, kg).astype(jnp.float32) * scale + bias_sel
        l_sel = jnp.where(valid[..., None], l_sel, -jnp.inf)
        k_own = lax.dynamic_slice_in_dim(kp, own * MOBA_BLOCK, MOBA_BLOCK, axis=2)
        v_own = lax.dynamic_slice_in_dim(vp, own * MOBA_BLOCK, MOBA_BLOCK, axis=2)
        rel_own = qpos[:, None] - (own * MOBA_BLOCK + offs)[None, :]
        bias_own = jnp.transpose(rel_bias[t5_bucket(rel_own)], (2, 0, 1)).astype(jnp.float32)
        l_own = jnp.einsum('bhqd,bhnd->bhqn', q_c, k_own).astype(jnp.float32) * scale + bias_own
        l_own = jnp.where(rel_own >= 0, l_own, -jnp.inf)
        logits = jnp.concatenate([l_sel.reshape(B, H, MOBA_QCHUNK, kk * MOBA_BLOCK), l_own], axis=-1)
        p = jax.nn.softmax(logits, axis=-1).astype(v.dtype)
        p_sel = p[..., :kk * MOBA_BLOCK].reshape(B, H, MOBA_QCHUNK, kk, MOBA_BLOCK)
        p_own = p[..., kk * MOBA_BLOCK:]
        return (jnp.einsum('bhqkn,bhqknd->bhqd', p_sel, vg)
                + jnp.einsum('bhqn,bhnd->bhqd', p_own, v_own))

    out = lax.map(chunk, (jnp.arange(n_chunk), qc_all))
    return out.transpose(1, 0, 3, 2, 4).reshape(B, S, H * d)

def stick_breaking_attention(q, k, v):
    B, H, S, d = q.shape
    scale = d ** -0.5
    n_blk = S // Q_BLOCK
    qb = q.reshape(B, H, n_blk, Q_BLOCK, d).transpose(2, 0, 1, 3, 4)
    kpos = jnp.arange(S)

    def block(args):
        i, q_b = args
        qpos = i * Q_BLOCK + jnp.arange(Q_BLOCK)
        strict = kpos[None, :] < qpos[:, None]
        z = jnp.einsum('bhqd,bhkd->bhqk', q_b, k).astype(jnp.float32) * scale
        log_beta = jax.nn.log_sigmoid(z)
        log_1m = jnp.where(strict, jax.nn.log_sigmoid(-z), 0.0)
        acc = lax.cumsum(log_1m, axis=3, reverse=True) - log_1m
        w = jnp.where(strict, jnp.exp(log_beta + acc), 0.0)
        return jnp.einsum('bhqk,bhkd->bhqd', w.astype(v.dtype), v)

    out = lax.map(block, (jnp.arange(n_blk), qb))
    return out.transpose(1, 0, 3, 2, 4).reshape(B, S, H * d)

def setup_inputs(seed: int = 0) -> dict:
    key = jax.random.key(seed)
    ks = jax.random.split(key, 17)

    def nrm(k, shape, fan_in):
        return jax.random.normal(k, shape, jnp.float32) * (fan_in ** -0.5)

    def gain(k, shape):
        return 1.0 + 0.05 * jax.random.normal(k, shape, jnp.float32)

    return {
        'x': jax.random.normal(ks[0], (BATCH, SEQ, D_MODEL), jnp.float32),
        'mix_pre_g': gain(ks[1], (DEPTH, D_MODEL)),
        'mix_post_g': gain(ks[2], (DEPTH, D_MODEL)),
        'ffn_pre_g': gain(ks[3], (DEPTH, D_MODEL)),
        'ffn_post_g': gain(ks[4], (DEPTH, D_MODEL)),
        'ab_w_in': nrm(ks[5], (N_EVEN, D_MODEL, AB_IN), D_MODEL),
        'mla_q_norm_g': gain(ks[6], (N_EVEN, MLA_Q_LORA)),
        'mla_w_uq': nrm(ks[7], (N_EVEN, MLA_Q_LORA, MLA_HEADS * (MLA_NOPE + MLA_ROPE)), MLA_Q_LORA),
        'mla_kv_norm_g': gain(ks[8], (N_EVEN, MLA_KV_LORA)),
        'mla_w_ukv': nrm(ks[9], (N_EVEN, MLA_KV_LORA, MLA_HEADS * (MLA_NOPE + MLA_V)), MLA_KV_LORA),
        'ab_w_out': nrm(ks[10], (N_EVEN, AB_OUT, D_MODEL), AB_OUT),
        'rel_bias': 0.5 * jax.random.normal(ks[11], (NUM_BUCKETS, MOBA_HEADS), jnp.float32),
        'sb_w_qkv': nrm(ks[12], (N_ODD, D_MODEL, 3 * SB_WIDTH), D_MODEL),
        'sb_w_out': nrm(ks[13], (N_ODD, SB_WIDTH, D_MODEL), SB_WIDTH),
        'ffn_w_gate_up': nrm(ks[14], (DEPTH, D_MODEL, 2 * D_FF), D_MODEL),
        'ffn_w_down': nrm(ks[15], (DEPTH, D_FF, D_MODEL), D_FF),
    }

def reference(x, mix_pre_g, mix_post_g, ffn_pre_g, ffn_post_g, ab_w_in, mla_q_norm_g, mla_w_uq,
              mla_kv_norm_g, mla_w_ukv, ab_w_out, rel_bias, sb_w_qkv, sb_w_out, ffn_w_gate_up, ffn_w_down):
    B, S, _ = x.shape
    pos = jnp.arange(S)
    o1 = MLA_Q_LORA
    o2 = o1 + MLA_KV_LORA
    o3 = o2 + MLA_ROPE
    h = x
    for layer in range(DEPTH):
        u = rmsnorm(h, mix_pre_g[layer])
        if layer % 2 == 0:
            e = layer // 2
            proj = u @ ab_w_in[e]
            mla_out = mla_attention(proj[..., :o1], proj[..., o1:o2], proj[..., o2:o3],
                                    mla_q_norm_g[e], mla_w_uq[e], mla_kv_norm_g[e], mla_w_ukv[e], pos)
            qkv = proj[..., o3:].reshape(B, S, 3, MOBA_HEADS, HEAD_DIM).transpose(2, 0, 3, 1, 4)
            moba_out = moba_attention(qkv[0], qkv[1], qkv[2], rel_bias)
            mixed = jnp.concatenate([mla_out, moba_out], axis=-1) @ ab_w_out[e]
        else:
            o = layer // 2
            qkv = (u @ sb_w_qkv[o]).reshape(B, S, 3, SB_HEADS, HEAD_DIM).transpose(2, 0, 3, 1, 4)
            mixed = stick_breaking_attention(qkv[0], qkv[1], qkv[2]) @ sb_w_out[o]
        h = h + rmsnorm(mixed, mix_post_g[layer])
        u = rmsnorm(h, ffn_pre_g[layer])
        gu = u @ ffn_w_gate_up[layer]
        f = (jax.nn.silu(gu[..., :D_FF]) * gu[..., D_FF:]) @ ffn_w_down[layer]
        h = h + rmsnorm(f, ffn_post_g[layer])
    return h


_drawn_inputs = setup_inputs


def setup_inputs(seed=0):
    import zlib

    import numpy as np

    out = dict(_drawn_inputs(seed))
    spreads = {}
    factors = {}
    for name, (base, spread) in spreads.items():
        noise = np.random.default_rng([zlib.crc32(name.encode()), seed]).standard_normal(out[name].shape)
        drawn = base * np.exp(spread * noise) if base else spread * noise
        out[name] = jnp.asarray(drawn.astype(out[name].dtype))
    for name, factor in factors.items():
        out[name] = (out[name] * factor).astype(out[name].dtype)
    return out
```

```python
import math
from contextlib import ExitStack

import numpy as np

import concourse.bass as bass
from concourse import mybir

F32 = mybir.dt.float32
F32R = mybir.dt.float32r
BF16 = mybir.dt.bfloat16
ALU = mybir.AluOpType
ACT = mybir.ActivationFunctionType

P = 128
T = 512
TT = T // P
D = 1024
KD = D // P
FF = 2816
KF = FF // P
EPS = 1e-6
NEG = -1e30
HD = 64
ROPE = 32
QL, KVL = 384, 256
KQ, KKV = QL // P, KVL // P
MLA_QH = HD + ROPE
MLA_SCALE = float(MLA_QH) ** -0.5
SCALE = float(HD) ** -0.5
THETA = 10000.0
NBUCKET, MAXDIST = 32, 128
O1, O2, O3 = QL, QL + KVL, QL + KVL + ROPE
MLA_PAIRS, MOBA_PAIRS, SB_PAIRS = 4, 4, 8
NH0 = 2 * (MLA_PAIRS + MOBA_PAIRS)
NH1 = 2 * SB_PAIRS

ROW_AT = {3: 0, 2: 512, 0: 896, 1: 1024}
COL_AT = {0: 0, 1: 512, 3: 896, 2: 1024}
CW = 1280

NSLOT = 3
AHEAD = 2
CH_IN = 0
CH_MLA = CH_IN + 6
CH_MOBA = CH_MLA + 2 * MLA_PAIRS
CH_OUT0 = CH_MOBA + 3 * MOBA_PAIRS
CH_GU0 = CH_OUT0 + KD
CH_DN0 = CH_GU0 + 2 * KF
CH_SB = CH_DN0 + 3 * KD
CH_OUT1 = CH_SB + 3 * SB_PAIRS
CH_GU1 = CH_OUT1 + KD
CH_DN1 = CH_GU1 + 2 * KF
CH_END = CH_DN1 + 3 * KD
DN_PARTS = ((0, 8), (8, 7), (15, 7))

G_MIX_PRE, G_MIX_POST, G_FFN_PRE, G_FFN_POST, G_Q, G_KV, G_ROWS = 0, 16, 32, 48, 64, 67, 69


def rope_tables():
    half = ROPE // 2
    inv = (np.float32(THETA) ** (-np.arange(half, dtype=np.float32) / np.float32(half))).astype(np.float32)
    ang = np.arange(T, dtype=np.float32)[None, :] * inv[:, None]
    cos, sin = np.cos(ang).astype(np.float32), np.sin(ang).astype(np.float32)
    return np.stack([np.concatenate([cos, cos]), np.concatenate([-sin, sin])])


def bucket_onehot():
    rel = 511 - np.arange(640)
    exact = NBUCKET // 2
    big = exact + (np.log(np.maximum(rel, exact).astype(np.float32) / np.float32(exact))
                   / np.float32(math.log(MAXDIST / exact)) * (NBUCKET - exact)).astype(np.int32)
    bucket = np.where(np.maximum(rel, 0) < exact, np.maximum(rel, 0), np.minimum(big, NBUCKET - 1))
    hot = (bucket[None, :] == np.arange(NBUCKET + 1)[:, None]) & (rel >= 0)[None, :]
    hot[NBUCKET] = rel < 0
    return hot.astype(np.float32)


class Chunk:

    def __init__(self, c0, i=0, per=0):
        assert per % NSLOT == 0
        self.c0, self.i, self.per = c0, i, per
        self.slot = c0 % NSLOT
        self.turn = c0 // NSLOT + i * (per // NSLOT)
        self.n = c0 + i * per

    def later(self, k):
        return Chunk(self.c0 + k, self.i, self.per)


def layer0_items():
    groups = []
    for p in range(MLA_PAIRS):
        cq, ck = CH_MLA + 2 * p, CH_MLA + 2 * p + 1
        groups.append([("mq", p, 0, cq, True, False), ("mq", p, 1, cq, False, True),
                       ("mk", p, 0, ck, True, False), ("mk", p, 1, ck, False, False),
                       ("mv", p, 0, ck, False, True), ("vt", p, 0, None, False, False)])
    for m in range(MOBA_PAIRS):
        p, c = MLA_PAIRS + m, CH_MOBA + 3 * m
        groups.append([("bq", p, 0, c, True, True), ("bk", p, 0, c + 1, True, True),
                       ("bv", p, 0, c + 2, True, True), ("vt", p, 0, None, False, False)])
    return groups


def bass_hybrid_two_layers(nc, x, mix_pre_g, mix_post_g, ffn_pre_g, ffn_post_g, ab_w_in,
                           mla_q_norm_g, mla_w_uq, mla_kv_norm_g, mla_w_ukv, ab_w_out, rel_bias,
                           sb_w_qkv, sb_w_out, ffn_w_gate_up, ffn_w_down, out):
    onehot_d = nc.inline_tensor(bucket_onehot(), name="bucket_onehot").ap()
    rope_d = nc.inline_tensor(rope_tables(), name="rope_tables").ap()
    bias_t = nc.dram_tensor("bias_by_distance", [8, P, 640], F32, kind="Internal")

    groups = layer0_items()
    items = [it for g in groups for it in g]
    order = {it[:3]: n for n, it in enumerate(items)}
    split_order = {}
    for it in items:
        if it[0] not in ("mv", "bv"):
            split_order[it[:3]] = len(split_order)
    inner_order = {}
    for it in items:
        if not it[5]:
            inner_order[it[:3]] = len(inner_order)

    def slots_of_step(hh):
        p, e = hh // 2, hh % 2
        if p + 1 >= len(groups):
            return [None] * 3
        g = groups[p + 1]
        if len(g) == 6:
            return g[0:3] if e == 0 else g[3:6]
        return [g[0], None, g[1]] if e == 0 else [g[2], None, g[3]]

    ctx = ExitStack()
    with ctx:
        def sem(name):
            return ctx.enter_context(nc.semaphore(name))

        def sb(stack, name, shape, dt=F32):
            return stack.enter_context(nc.sbuf_tensor(name, shape, dt))

        hT = sb(ctx, "residual", [P, KD, T])
        uh = sb(ctx, "u_hi", [P, KD, T], F32R)
        with ExitStack() as s:
            F = sb(s, "block_out", [P, KD, T])
        ul = sb(ctx, "u_lo", [P, KD, T], F32R)
        raw = sb(ctx, "w_raw", [P, NSLOT, 1024])
        wh = sb(ctx, "w_hi", [P, NSLOT, 1024], F32R)
        wl = sb(ctx, "w_lo", [P, NSLOT, 1024], F32R)
        ident = sb(ctx, "ident", [P, P])
        ones = sb(ctx, "ones", [P, P])
        tri_f = sb(ctx, "tri_f", [P, P])
        negtri = sb(ctx, "negtri", [P, P], F32R)
        negones = sb(ctx, "negones", [P, P], F32R)
        identb = sb(ctx, "identb", [P, P], BF16)
        big = sb(ctx, "big", [P, P], BF16)
        gains = sb(ctx, "gains", [P, G_ROWS])
        r_pre = sb(ctx, "r_pre", [P, T])
        r_post = sb(ctx, "r_post", [P, T])
        acc = sb(ctx, "sq_sum", [P, T])
        sqt = sb(ctx, "sq_tile", [P, T])
        diag = sb(ctx, "diag", [P, TT, P])
        tf = sb(ctx, "tf", [P, 2, T])
        rms = sb(ctx, "rms", [P, TT])
        rinv = sb(ctx, "rinv", [P, TT])
        ssx = sb(ctx, "ssx", [P, TT])
        eps_t = sb(ctx, "eps", [P, 1])
        with ExitStack() as at0:
            vh = sb(at0, "v_hi", [P, 2, TT, 192], F32R)
            vl = sb(at0, "v_lo", [P, 2, TT, 192], F32R)
            oAh = sb(at0, "oA_hi", [P, 4, T], F32R)
            oAl = sb(at0, "oA_lo", [P, 4, T], F32R)
            s_sb = sb(at0, "logits", [P, CW])
            pth = sb(at0, "probsT_hi", [P, CW], F32R)
            ptl = sb(at0, "probsT_lo", [P, CW], F32R)
            mx = sb(at0, "row_max", [P, TT])
            nmx = sb(at0, "neg_max", [P, TT])
            den = sb(at0, "den", [P, TT])
            rden = sb(at0, "rden", [P, TT])
            with ExitStack() as s:
                xt = sb(s, "x_tokens", [P, TT, D])
                junk = sb(s, "x_squares", [P, D])
                graw = sb(s, "gain_rows", [G_ROWS, P])
            with ExitStack() as s:
                sb(s, "below_x", [P, TT * D + D + P])
                hot = sb(s, "onehot", [NBUCKET + 1, 640])
                rb = sb(s, "rel_bias_rows", [NBUCKET + 1, 8])
                brow = sb(s, "bias_rows", [8, 640])
            with ExitStack() as s:
                mq = [sb(s, f"mla_{n}", [P, 3, T], F32R) for n in ("q_hi", "q_lo", "k_hi", "k_lo")]
                cqh = sb(s, "cq_hi", [P, KQ, T], F32R)
                cql = sb(s, "cq_lo", [P, KQ, T], F32R)
                ckh = sb(s, "ckv_hi", [P, KKV, T], F32R)
                ckl = sb(s, "ckv_lo", [P, KKV, T], F32R)
                cs = sb(s, "cos_sin", [P, 2, T])
                cmask = sb(s, "causal", [P, T])
                r_q = sb(s, "r_q", [P, T])
                r_kv = sb(s, "r_kv", [P, T])
                rt = sb(s, "rope_tmp", [P, 2, T])
            with ExitStack() as s:
                oBh = sb(s, "oB_hi", [P, 4, T], F32R)
                oBl = sb(s, "oB_lo", [P, 4, T], F32R)
                bias = sb(s, "bias", [P, 2, T])
                sb(s, "below_moba_qk", [P, 2, T])
                bq = [sb(s, f"moba_{n}", [P, 2, T], F32R) for n in ("q_hi", "q_lo", "k_hi", "k_lo")]
        with ExitStack() as s:
            hidh = sb(s, "hidden_hi", [P, KF, T], F32R)
            hidl = sb(s, "hidden_lo", [P, KF, T], F32R)
            gs = sb(s, "gate", [P, 3, T])
            us = sb(s, "up", [P, 3, T])
        with ExitStack() as s:
            ot = sb(s, "out_tiles", [P, KD, T])
        with ExitStack() as s:
            sv = [sb(s, f"sb_{n}", [P, 2, TT, 192], F32R) for n in ("v_hi", "v_lo")]
            soh = sb(s, "so_hi", [P, KD, T], F32R)
            sol = sb(s, "so_lo", [P, KD, T], F32R)
            sq = [sb(s, f"sb_{n}", [P, 2, T], F32R) for n in ("q_hi", "q_lo", "k_hi", "k_lo")]
            lsp = sb(s, "softplus", [P, CW])
            nsh = sb(s, "nsp_hi", [P, CW], F32R)
            nsl = sb(s, "nsp_lo", [P, CW], F32R)
            wf = sb(s, "stick", [P, CW])
            swh = sb(s, "stick_hi", [P, 2, CW], F32R)
            swl = sb(s, "stick_lo", [P, 2, CW], F32R)

        ps = ctx.enter_context(nc.psum_tensor("banks", [P, 8, T], F32))

        def bank(b):
            return ps[:, b, :]

        def banks(b):
            return ps[:, b:b + 3, :].rearrange("p b n -> p (b n)")

        SC, PT, O_BANK, P_BANK = banks(0), banks(3), 6, 7
        ZB = [banks(0), banks(3)]
        oh = [oAh[:, n, :] for n in range(4)] + [oBh[:, n, :] for n in range(4)]
        ol = [oAl[:, n, :] for n in range(4)] + [oBl[:, n, :] for n in range(4)]

        raw_in = [sem(f"raw_in{n}") for n in range(NSLOT)]
        ukv_in = [sem(f"ukv_in{n}") for n in range(2)]
        w_hi, w_lo, w_used = sem("w_hi_done"), sem("w_lo_done"), sem("w_used")
        consts_ready = sem("consts_ready")
        tri_ready = sem("tri_ready")
        tri_r_ready = sem("tri_rounded")
        x_in = [sem(f"x_in{n}") for n in range(TT)]
        gains_in, tables_in, bias_in_sbuf = sem("gains_in"), sem("tables_in"), sem("bias_tables_in")
        gains_tr, gains_ready = sem("gains_transposed"), sem("gains_ready")
        x_tr, h_ready = sem("x_transposed"), sem("h_copied")
        uh_ready, u_ready = sem("u_hi_ready"), sem("u_ready")
        ssx_ready = sem("x_square_sums")
        st_sum, st_rms, st_rinv = sem("stat_sums"), sem("stat_rms"), sem("stat_rinv")
        st_diag, st_bc, st_r = sem("stat_diag"), sem("stat_spread"), sem("stat_r_ready")
        sq_ready, sq_added = sem("squares_ready"), sem("squares_added")
        in_scaled = sem("latent_scaled")
        lat_hi, lat_ready = sem("latent_hi"), sem("latent_ready")
        brow_mm, brow_sb, brow_out = sem("bias_rows_mm"), sem("bias_rows_sbuf"), sem("bias_rows_dram")
        bias_in = [sem(f"bias_in{n}") for n in range(2)]
        pj_mm, pj_read, pj_hi, pj_lo = sem("proj_product"), sem("proj_bank_read"), sem("proj_hi"), sem("proj_lo")
        rp_sw, rp_cos, rp_sin, rp_done = sem("rope_swapped"), sem("rope_cos"), sem("rope_sin"), sem("rope_done")
        kr_hi, kr_lo = sem("k_rope_hi"), sem("k_rope_lo")
        sc_done, sc_read, mx_neg = sem("scores_done"), sem("scores_read"), sem("max_negated")
        e_done, den_inv, p_done = sem("exp_done"), sem("den_inverted"), sem("probs_done")
        pt_done, pt_hi, pt_lo = sem("probsT_done"), sem("probsT_hi_done"), sem("probsT_lo_done")
        pv_done, o_hi, o_lo = sem("pv_done"), sem("o_hi_done"), sem("o_lo_done")
        f_read = sem("f_read")
        res_t, res_h = sem("branch_scaled"), sem("residual_added")
        gu_read = sem("gate_up_read")
        silu_done, act_mul = sem("silu_done"), sem("hidden_done")
        hid_hi, hid_lo = sem("hidden_hi_done"), sem("hidden_lo_done")
        v0_ready, v1_ready = sem("v_pad_ready"), sem("v1_pad_ready")
        qj_mm, qj_read, qj_hi, qj_lo = sem("sb_product"), sem("sb_bank_read"), sem("sb_hi"), sem("sb_lo")
        z_done, z_min, z_exp, z_ln = sem("z_done"), sem("z_clamped"), sem("z_exp"), sem("z_ln")
        ns_f, ns_hi, ns_lo = sem("softplus_ready"), sem("softplus_hi"), sem("softplus_lo")
        c_done, w_exp, sw_hi, sw_lo = sem("stick_sums"), sem("stick_exp"), sem("stick_hi"), sem("stick_lo")
        sv_done, so_hi_s, so_lo_s = sem("sb_pv_done"), sem("sb_o_hi"), sem("sb_o_lo")
        y_tr, y_sb, y_out = sem("y_transposed"), sem("y_sbuf"), sem("y_out")


        def load(sp, c, src, kt, cols, stride=None):
            if c.c0 >= NSLOT:
                sp.wait_ge(w_lo, c.n - NSLOT + 1)
            stride = stride or cols
            dst = raw[:, c.slot, 0:kt * stride].rearrange("p (k n) -> p k n", k=kt)[:, :, 0:cols]
            sp.dma_start(dst, src.rearrange("(k p) n -> p k n", p=P)).then_inc(raw_in[c.slot], 16)

        def ukv(c):
            p, j = (c - CH_MLA) // 2, (c - CH_MLA) % 2
            return (ukv_in[p % 2], 48 * (p // 2 + 1)) if 0 <= p < MLA_PAIRS and j == 1 else None

        def split_hi(act, c, also=None):
            if c.c0 >= CH_END:
                return
            if also:
                act.wait_ge(*also)
            act.wait_ge(raw_in[c.slot], 16 * (c.turn + 1))
            if c.c0 >= NSLOT:
                act.wait_ge(w_used, c.n - NSLOT + 1)
            act.activation(wh[:, c.slot, :], raw[:, c.slot, :], ACT.Copy).then_inc(w_hi, 1)

        def split_lo(dve, c):
            if c.c0 >= CH_END:
                return
            dve.wait_ge(w_hi, c.n + 1)
            dve.tensor_tensor(wl[:, c.slot, :], raw[:, c.slot, :], wh[:, c.slot, :].bitcast(F32),
                              ALU.subtract).then_inc(w_lo, 1)

        def mm3(o, lh, ll, rh, rl, start, stop):
            nc.tensor.matmul(o, lh, rh, start=start, stop=False, skip_group_check=True)
            nc.tensor.matmul(o, lh, rl, start=False, stop=False, skip_group_check=True)
            return nc.tensor.matmul(o, ll, rh, start=False, stop=stop, skip_group_check=True)

        def project(pe, o, c, kt, stride, at, m, xh, xl, first=0, total=None, x_ready=None):
            total = total or kt
            for k in range(kt):
                if x_ready:
                    pe.wait_ge(x_ready[0], x_ready[1] + k + 1)
                s = slice(k * stride + at, k * stride + at + m)
                last = mm3(o, wh[:, c.slot, s], wl[:, c.slot, s], xh[:, first + k, :], xl[:, first + k, :],
                           start=(first + k == 0), stop=(first + k == total - 1))
            return last

        def stat_pe(pe, k, b, adds=None):
            if adds is not None:
                pe.wait_ge(sq_added, adds)
                for t in range(TT):
                    last = nc.tensor.matmul(bank(b)[:, t:t + 1], acc[:, t * P:(t + 1) * P], ones[:, 0:1],
                                            start=True, stop=True)
                last.then_inc(st_sum, 1)

        def stat_pe_spread(pe, k, b):
            pe.wait_ge(st_diag, k + 1)
            nc.tensor.matmul(bank(b), ones[:, :], diag[:, :, :].rearrange("p t n -> p (t n)"),
                             start=True, stop=True).then_inc(st_bc, 1)

        def stat_act(act, k, src, width):
            if src is None:
                act.wait_ge(ssx_ready, TT)
                src = ssx[:, :]
            else:
                act.wait_ge(st_sum, k)
            act.activation(rms[:, :], src, ACT.Sqrt, bias=eps_t[:, 0:1], scale=1.0 / width).then_inc(st_rms, 1)

        def stat_dve(dve, k, b, dst):
            dve.wait_ge(st_rms, k + 1)
            nc.vector.reciprocal(rinv[:, :], rms[:, :]).then_inc(st_rinv, 1)
            dve.wait_ge(st_rinv, k + 1)
            if k:
                dve.wait_ge(st_bc, k)
            for t in range(TT):
                last = nc.vector.tensor_scalar(diag[:, t, :], ident[:, :], rinv[:, t:t + 1], None, ALU.mult)
            last.then_inc(st_diag, 1)
            dve.wait_ge(st_bc, k + 1)
            nc.vector.tensor_copy(dst[:, :], bank(b)).then_inc(st_r, 1)

        def square(act, src, n, k):
            if n == 0:
                if k > 1:
                    act.wait_ge(st_sum, k - 1)
                act.activation(acc[:, :], src, ACT.Square).then_inc(sq_ready, 1)
            else:
                if AD0[k] + n > 1:
                    act.wait_ge(sq_added, AD0[k] + n - 1)
                act.activation(sqt[:, :], src, ACT.Square).then_inc(sq_ready, 1)

        def add_squares(pool, n, k):
            pool.wait_ge(sq_ready, SQ0[k] + n + 1)
            if n > 1:
                pool.wait_ge(sq_added, AD0[k] + n - 1)
            nc.gpsimd.tensor_tensor(acc[:, :], acc[:, :], sqt[:, :], ALU.add).then_inc(sq_added, 1)

        N_X, N_CQ, N_CKV, N_POST_A0, N_FFN0, N_POST_F0, N_SB, N_POST_A1, N_FFN1, N_POST_F1 = range(10)
        tiles_of = [0, KQ, KKV] + [KD] * 7
        posts = (N_POST_A0, N_POST_F0, N_POST_A1, N_POST_F1)
        SQ0 = [sum(t for j, t in enumerate(tiles_of[:k]) if j not in posts) for k in range(10)]
        AD0 = [sum(t - 1 for t in tiles_of[1:k]) for k in range(11)]

        def f_pe(pe, chunks, fn, n, operands, f0, b):
            if not (f0 == 0 and n is not None and isinstance(n, int) and n < 2):
                pe.wait_ge(f_read, fn * KD + n - 1)
            at = 0
            total = sum(kt for _, kt in chunks)
            for c, kt in chunks:
                pe.wait_ge(w_lo, c.n + 1)
                for k in range(kt):
                    s = slice(k * P, (k + 1) * P)
                    xh, xl = operands(pe, at)
                    last = mm3(bank(b), wh[:, c.slot, s], wl[:, c.slot, s], xh, xl,
                               start=(at == 0), stop=(at == total - 1))
                    at += 1
                last.then_inc(w_used, 1)

        def f_act(act, last_chunk, b, n, first, k):
            act.wait_ge(w_used, last_chunk.n + 1)
            act.activation(F[:, n, :] if isinstance(n, int) else F[:, bass.ds(n, 1), :], bank(b), ACT.Copy)
            if first:
                act.wait_ge(st_sum, k - 1)
                act.activation(acc[:, :], bank(b), ACT.Square).then_inc(f_read, 1)
            else:
                act.wait_ge(sq_added, AD0[k] + n - 1)
                act.activation(sqt[:, :], bank(b), ACT.Square).then_inc(f_read, 1)

        def f_pool(pool, fn, n, k):
            pool.wait_ge(f_read, fn * KD + n + 1)
            if isinstance(n, int) and n == 1:
                pass
            else:
                pool.wait_ge(sq_added, AD0[k] + n - 1)
            nc.gpsimd.tensor_tensor(acc[:, :], acc[:, :], sqt[:, :], ALU.add).then_inc(sq_added, 1)

        def out_sp(sp, ch, w):
            for n in range(KD):
                load(sp, Chunk(ch + n), w[:, n * P:(n + 1) * P], KD, P)

        def out_pe(pe, ch, fn, o_at, o_ready):
            def operands(pe, k):
                return o_at(k)
            pe.wait_ge(*o_ready)
            for n in range(KD):
                f_pe(pe, [(Chunk(ch + n), KD)], fn, n, operands, fn if n >= 2 else 0, 6 + n % 2)

        def out_act(act, ch, k):
            for n in range(KD):
                split_hi(act, Chunk(ch + n + AHEAD))
                f_act(act, Chunk(ch + n), 6 + n % 2, n, n == 0, k)

        def out_dve(dve, ch):
            for n in range(KD):
                split_lo(dve, Chunk(ch + n + AHEAD))

        def f_adds(pool, fn, k):
            for n in range(1, KD):
                f_pool(pool, fn, n, k)

        def res_sp(sp):
            pass

        def res_dve_branch(dve, r, n, g_post):
            if n >= 2:
                dve.wait_ge(res_h, KD * r + n - 1)
            nc.vector.scalar_tensor_tensor(tf[:, n % 2, :], F[:, n, :], gains[:, g_post + n:g_post + n + 1],
                                           r_post[:, :], ALU.mult, ALU.mult).then_inc(res_t, 1)

        def res_dve(dve, r, k, g_post, g_pre):
            stat_dve(dve, k, 0, r_post)
            dve.wait_ge(st_r, k + 1)
            for n in range(KD + 1):
                if n < KD:
                    res_dve_branch(dve, r, n, g_post)
                if n and g_pre is not None:
                    m = n - 1
                    dve.wait_ge(uh_ready, KD * (r + 1) + m + 1)
                    nc.vector.scalar_tensor_tensor(ul[:, m, :], hT[:, m, :], gains[:, g_pre + m:g_pre + m + 1],
                                                   uh[:, m, :].bitcast(F32), ALU.mult, ALU.subtract)\
                        .then_inc(u_ready, 1)

        def res_act(act, r, k, g_pre):
            for n in range(KD):
                act.wait_ge(res_h, KD * r + n + 1)
                act.activation(uh[:, n, :], hT[:, n, :], ACT.Copy, scale=gains[:, g_pre + n:g_pre + n + 1])\
                    .then_inc(uh_ready, 1)
                square(act, hT[:, n, :], n, k + 1)

        def res_pool(pool, r, k, more):
            for n in range(KD):
                pool.wait_ge(res_t, KD * r + n + 1)
                nc.gpsimd.tensor_tensor(hT[:, n, :], hT[:, n, :], tf[:, n % 2, :], ALU.add).then_inc(res_h, 1)
                if more and n > 1:
                    add_squares(pool, n - 1, k + 1)
            if more:
                add_squares(pool, KD - 1, k + 1)

        def gu_chunk(ch, n0, i=0):
            return Chunk(ch + 2 * n0, i, 6)

        def gu_sp(sp, ch, w):
            def tile(n0, i):
                c = gu_chunk(ch, n0, i)
                for half in range(2):
                    at = half * FF + n0 * P
                    src = w[:, at:at + P] if isinstance(i, int) and i == 0 else w[:, bass.ds(i * (3 * P) + at, P)]
                    load(sp, c.later(half), src, KD, P)
            tile(0, 0)
            with sp.Fori(0, (KF - 1) // 3) as i:
                for b in range(1, 4):
                    tile(b, i)

        def gu_pe(pe, ch, l, k):
            def tile(n0, i, k_outer=False):
                c, b = gu_chunk(ch, n0, i), 2 * (n0 % 3)
                for half in range(2):
                    cc = c.later(half)
                    pe.wait_ge(w_lo, cc.n + 1)
                    if n0 or not isinstance(i, int):
                        if n0 == 3 or not isinstance(i, int):
                            pe.wait_ge(gu_read, base_wait(l, n0, i, half))
                    project(pe, bank(b + half), cc, KD, P, 0, P, uh, ul,
                            x_ready=(u_ready, KD * (2 * l + 1)) if n0 == 0 else None).then_inc(w_used, 1)

            def base_wait(l, n0, i, half):
                return 2 * KF * l + 2 * (n0 - 3) + half + 1 + i * 6

            tile(0, 0)
            stat_pe(pe, k, 6, AD0[k + 1])
            stat_pe_spread(pe, k, 6)
            for n0 in (1, 2, 3):
                tile(n0, 0)
            with pe.Fori(1, (KF - 1) // 3) as i:
                for b in range(1, 4):
                    tile(b, i)

        def gu_act(act, ch, l, k):
            def hi(n0, i):
                act.wait_ge(act_mul, KF * l + n0 + i * 3 + 1)
                o = hidh[:, n0, :] if isinstance(i, int) else hidh[:, bass.ds(i * 3 + n0, 1), :]
                act.activation(o, us[:, n0 % 3, :], ACT.Copy).then_inc(hid_hi, 1)

            def tile(n0, i, first=False):
                c = gu_chunk(ch, n0, i)
                split_hi(act, c.later(AHEAD))
                split_hi(act, c.later(AHEAD + 1))
                if first:
                    stat_act(act, k, bank(6)[:, 0:TT], D)
                else:
                    hi(n0 - 1, i)
                act.wait_ge(gu_read, 2 * KF * l + 2 * n0 + i * 6 + 1)
                act.activation(gs[:, n0 % 3, :], gs[:, n0 % 3, :], ACT.Silu).then_inc(silu_done, 1)

            tile(0, 0, True)
            with act.Fori(0, (KF - 1) // 3) as i:
                for b in range(1, 4):
                    tile(b, i)
            hi(KF - 1, 0)

        def gu_pool(pool, l):
            def tile(n0, i):
                pool.wait_ge(silu_done, KF * l + n0 + i * 3 + 1)
                pool.wait_ge(gu_read, 2 * KF * l + 2 * n0 + i * 6 + 2)
                nc.gpsimd.tensor_tensor(us[:, n0 % 3, :], us[:, n0 % 3, :], gs[:, n0 % 3, :], ALU.mult)\
                    .then_inc(act_mul, 1)
            tile(0, 0)
            with pool.Fori(0, (KF - 1) // 3) as i:
                for b in range(1, 4):
                    tile(b, i)

        def gu_dve(dve, ch, l, k):
            def lo(n0, i):
                dve.wait_ge(hid_hi, KF * l + n0 + i * 3 + 1)
                o = hidl[:, n0, :] if isinstance(i, int) else hidl[:, bass.ds(i * 3 + n0, 1), :]
                h = hidh[:, n0, :] if isinstance(i, int) else hidh[:, bass.ds(i * 3 + n0, 1), :]
                nc.vector.tensor_tensor(o, us[:, n0 % 3, :], h.bitcast(F32), ALU.subtract).then_inc(hid_lo, 1)

            def tile(n0, i, first=False):
                c, b = gu_chunk(ch, n0, i), n0 % 3
                split_lo(dve, c.later(AHEAD))
                if first:
                    split_lo(dve, c.later(AHEAD + 1))
                    stat_dve(dve, k, 6, r_pre)
                    dve.wait_ge(st_r, k + 1)
                dve.wait_ge(w_used, c.n + 1)
                nc.vector.tensor_tensor(gs[:, b, :], bank(2 * b), r_pre[:, :], ALU.mult).then_inc(gu_read, 1)
                if not first:
                    split_lo(dve, c.later(AHEAD + 1))
                dve.wait_ge(w_used, c.n + 2)
                nc.vector.tensor_tensor(us[:, b, :], bank(2 * b + 1), r_pre[:, :], ALU.mult).then_inc(gu_read, 1)
                if not first:
                    lo(n0 - 1, i)

            tile(0, 0, True)
            with dve.Fori(0, (KF - 1) // 3) as i:
                for b in range(1, 4):
                    tile(b, i)
            lo(KF - 1, 0)

        def dn_chunks(ch, n0, i=0):
            return [(Chunk(ch + 3 * n0 + j, i, 6), kt) for j, (_, kt) in enumerate(DN_PARTS)]

        DN_TURNS = (KD - 2) // 2

        def dn_sp(sp, ch, w):
            def tile(n0, i):
                for (c, kt), (k0, _) in zip(dn_chunks(ch, n0, i), DN_PARTS):
                    rows = w[k0 * P:(k0 + kt) * P, :]
                    src = rows[:, n0 * P:(n0 + 1) * P] if isinstance(i, int) else rows[:, bass.ds(i * (2 * P) + n0 * P, P)]
                    load(sp, c, src, kt, P)
            with sp.Fori(0, DN_TURNS) as i:
                tile(0, i)
                tile(1, i)
            tile(KD - 2, 0)
            tile(KD - 1, 0)

        def dn_pe(pe, ch, fn, l):
            def operands(ready):
                def at(pe, k):
                    if ready:
                        pe.wait_ge(hid_lo, KF * l + k + 1)
                    return hidh[:, k, :], hidl[:, k, :]
                return at

            def tile(n0, i, first=False):
                f_pe(pe, dn_chunks(ch, n0, i), fn, n0 + i * 2, operands(first), 1, 6 + n0 % 2)
            tile(0, 0, True)
            tile(1, 0)
            with pe.Fori(1, DN_TURNS) as i:
                tile(0, i)
                tile(1, i)
            tile(KD - 2, 0)
            tile(KD - 1, 0)

        def dn_act(act, ch, k):
            def tile(n0, i, first=False):
                c = Chunk(ch + 3 * n0, i, 6)
                for j in range(3):
                    split_hi(act, c.later(AHEAD + j))
                f_act(act, c.later(2), 6 + n0 % 2, n0 + i * 2, first, k)
            tile(0, 0, True)
            tile(1, 0)
            with act.Fori(1, DN_TURNS) as i:
                tile(0, i)
                tile(1, i)
            tile(KD - 2, 0)
            tile(KD - 1, 0)

        def dn_dve(dve, ch):
            def tile(n0, i):
                c = Chunk(ch + 3 * n0, i, 6)
                for j in range(3):
                    split_lo(dve, c.later(AHEAD + j))
            with dve.Fori(0, DN_TURNS) as i:
                tile(0, i)
                tile(1, i)
            tile(KD - 2, 0)
            tile(KD - 1, 0)

        IN_TILES = [(0, P), (P, P), (2 * P, P), (O1, P), (O1 + P, P), (O2 - HD, MLA_QH)]
        lat_gain = [G_Q, G_Q + 1, G_Q + 2, G_KV, G_KV + 1]
        lat_dst = [(cqh, cql, 0), (cqh, cql, 1), (cqh, cql, 2), (ckh, ckl, 0), (ckh, ckl, 1)]
        lat_norm = [(N_CQ, 0), (N_CQ, 1), (N_CQ, 2), (N_CKV, 0), (N_CKV, 1)]

        def rope_dve(dve, n):
            pass

        ROPE_ROWS = slice(HD, HD + ROPE)

        def rope_rows_dve(dve, b, number, scaled):
            dve.wait_ge(*scaled)
            nc.vector.stream_shuffle(rt[ROPE_ROWS, 0, :], tf[ROPE_ROWS, b, :],
                                     [(j + ROPE // 2) % ROPE for j in range(ROPE)]).then_inc(rp_sw, 1)
            dve.wait_ge(rp_sw, number + 1)
            nc.vector.tensor_tensor(rt[ROPE_ROWS, 0, :], rt[ROPE_ROWS, 0, :], cs[ROPE_ROWS, 1, :], ALU.mult)\
                .then_inc(rp_sin, 1)
            dve.wait_ge(rp_sin, number + 1)
            dve.wait_ge(rp_cos, number + 1)
            nc.vector.tensor_tensor(tf[ROPE_ROWS, b, :], rt[ROPE_ROWS, 0, :], rt[ROPE_ROWS, 1, :], ALU.add)\
                .then_inc(rp_done, 1)

        def rope_rows_pool(pool, b, number, scaled):
            pool.wait_ge(*scaled)
            if number:
                pool.wait_ge(rp_done, number)
            nc.gpsimd.tensor_tensor(rt[ROPE_ROWS, 1, :], tf[ROPE_ROWS, b, :], cs[ROPE_ROWS, 0, :], ALU.mult)\
                .then_inc(rp_cos, 1)

        def item_done(eng, it):
            if it[5]:
                eng.wait_ge(w_used, it[3] + 1)
            else:
                eng.wait_ge(pj_mm, inner_order[it[:3]] + 1)

        def head_of(it):
            return 2 * it[1] + it[2]

        def item_pe(pe, it):
            if it is None:
                return
            kind, p, e, c, first, last = it
            n = order[it[:3]]
            c = Chunk(c) if c is not None else None
            if n:
                pe.wait_ge(pj_read, n)
            if first:
                pe.wait_ge(w_lo, c.n + 1)
            b = bank(P_BANK)
            if kind == "mq":
                mm = project(pe, b[0:MLA_QH, :], c, KQ, 2 * MLA_QH, e * MLA_QH, MLA_QH, cqh, cql)
            elif kind == "mk":
                mm = project(pe, b[0:HD, :], c, KKV, P, e * HD, HD, ckh, ckl)
            elif kind == "mv":
                mm = project(pe, b, c, KKV, P, KKV * P, P, ckh, ckl)
            elif kind == "vt":
                tb = n_tf(it) % 2
                for t in range(TT):
                    mm = nc.tensor.transpose(b[:, t * P:(t + 1) * P], tf[:, tb, t * P:(t + 1) * P], ident[:, :])
            else:
                mm = project(pe, b, c, KD, P, 0, P, uh, ul)
            mm.then_inc(w_used if last else pj_mm, 1)

        tf_of = {}
        for it in items:
            if it[0] != "vt":
                tf_of[it[:3]] = len(tf_of) + KQ + KKV + 1

        def n_tf(it):
            if it[0] == "vt":
                return tf_of[("mv" if it[1] < MLA_PAIRS else "bv", it[1], 0)]
            return tf_of[it[:3]]

        def v_views(v, buf):
            return v[:, buf, :, 0:HD], v[:, buf, :, 2 * HD:3 * HD]

        def qk_dst(it):
            kind, p, e = it[:3]
            if kind[0] == "m":
                j = 0 if kind == "mq" else 2
                rows = slice(0, MLA_QH) if kind == "mq" else slice(0, HD)
                return [mq[j + a][rows, head_of(it) % 3, :] for a in range(2)], rows
            j = 0 if kind == "bq" else 2
            return [bq[j + a][:, p % 2, :] for a in range(2)], slice(0, P)

        def buffer_free(eng, it):
            kind, p, e = it[:3]
            if kind[0] == "m":
                h = head_of(it)
                if h >= 3 and kind in ("mq", "mk"):
                    eng.wait_ge(sc_done, 3 * (h - 2))
            elif kind in ("bq", "bk"):
                eng.wait_ge(sc_done, 3 * 2 * max(p - 1, MLA_PAIRS))
            if kind == "vt" and p >= 2:
                eng.wait_ge(pv_done, 2 * (p - 1))

        def item_act(act, it):
            if it is None:
                return
            kind, p, e, c, first, last = it
            if first:
                split_hi(act, Chunk(c + AHEAD), ukv(c + AHEAD))
            if kind in ("mv", "bv"):
                return
            buffer_free(act, it)
            if kind == "vt":
                item_done(act, it)
                if p == 0:
                    act.wait_ge(v0_ready, 1)
                src = bank(P_BANK).rearrange("p (t h n) -> p t h n", t=TT, h=2)
                a, b = v_views(vh, p % 2)
                act.activation(a, src[:, :, 0, :], ACT.Copy)
                act.activation(b, src[:, :, 1, :], ACT.Copy).then_inc(pj_hi, 1)
                return
            (hi, _), rows = qk_dst(it)
            if kind == "mq":
                act.wait_ge(rp_done, head_of(it) + 2)
            else:
                act.wait_ge(pj_read, order[it[:3]] + 1)
            act.activation(hi, tf[rows, n_tf(it) % 2, :], ACT.Copy).then_inc(pj_hi, 1)

        def item_dve(dve, it):
            if it is None:
                return
            kind, p, e, c, first, last = it
            if first:
                split_lo(dve, Chunk(c + AHEAD))
            n = order[it[:3]]
            tb = n_tf(it) % 2
            if kind == "vt":
                dve.wait_ge(pj_hi, split_order[it[:3]] + 1)
                src = bank(P_BANK).rearrange("p (t h n) -> p t h n", t=TT, h=2)
                for x in range(2):
                    ins = nc.vector.tensor_tensor(v_views(vl, p % 2)[x], src[:, :, x, :],
                                                  v_views(vh, p % 2)[x].bitcast(F32), ALU.subtract)
                ins.then_inc(pj_read, 1)
                return
            item_done(dve, it)
            if kind[0] == "m":
                rows = slice(0, {"mq": MLA_QH, "mk": HD, "mv": P}[kind])
                r = r_q if kind == "mq" else r_kv
                scale = MLA_SCALE if kind == "mq" else 1.0
            else:
                rows, r, scale = slice(0, P), r_pre, SCALE if kind == "bq" else 1.0
            vt_before = [i for i in items[:n] if i[0] == "vt"]
            if vt_before:
                dve.wait_ge(pj_mm, inner_order[vt_before[-1][:3]] + 1)
            nc.vector.scalar_tensor_tensor(tf[rows, tb, :], bank(P_BANK)[rows, :], scale, r[rows, :],
                                           ALU.mult, ALU.mult).then_inc(pj_read, 1)
            if kind in ("mv", "bv"):
                return
            if kind == "mq":
                rope_rows_dve(dve, tb, head_of(it) + 1, (pj_read, n + 1))
            (hi, lo), rows = qk_dst(it)
            dve.wait_ge(pj_hi, split_order[it[:3]] + 1)
            nc.vector.tensor_tensor(lo, tf[rows, tb, :], hi.bitcast(F32), ALU.subtract).then_inc(pj_lo, 1)

        def item_pool(pool, it):
            if it is not None and it[0] == "mq":
                rope_rows_pool(pool, n_tf(it) % 2, head_of(it) + 1, (pj_read, order[it[:3]] + 1))

        lo_order = {}
        for it in items:
            if it[0] in ("mq", "mk", "bq", "bk"):
                lo_order[it[:3]] = len(lo_order)

        def scores_pe(pe, hh):
            p, e = hh // 2, hh % 2
            pe.wait_ge(pj_lo, 1 + max(lo_order[("mk", p, e)], lo_order[("mq", p, e)]) if p < MLA_PAIRS
                       else 1 + lo_order[("bk", p, 0)])
            if hh == 0:
                pe.wait_ge(kr_lo, 1)
            if hh:
                pe.wait_ge(sc_read, hh)
            if p < MLA_PAIRS:
                rows, b, (qh, ql, kh, kl) = slice(0, MLA_QH), hh % 3, mq
            else:
                rows, b, (qh, ql, kh, kl) = slice(HD * e, HD * e + HD), p % 2, bq
            for i in (3, 1, 2, 0):
                w, at, q = P * (i + 1), ROW_AT[i], slice(i * P, (i + 1) * P)
                mm = mm3(SC[:, at:at + w], qh[rows, b, q], ql[rows, b, q], kh[rows, b, 0:w], kl[rows, b, 0:w],
                         start=(i != 0), stop=True)
                if i != 2:
                    mm.then_inc(sc_done, 1)

        def scores_dve(dve, hh):
            if hh >= 1:
                dve.wait_ge(pt_done, hh)
            if hh < 2 * MLA_PAIRS:
                add = cmask[:, :]
                if hh == 0:
                    dve.wait_ge(v0_ready, 2)
            else:
                m = hh - 2 * MLA_PAIRS
                dve.wait_ge(bias_in[m % 2], 16 * (m // 2 + 1))
                add = bias[:, m % 2, :]
            for x, i in enumerate((3, 1, 2, 0)):
                w, at = P * (i + 1), ROW_AT[i]
                if x < 3:
                    dve.wait_ge(sc_done, 3 * hh + x + 1)
                ins = nc.vector.tensor_tensor_reduce(s_sb[:, at:at + w], SC[:, at:at + w], add[:, T - w:T], 1.0,
                                                     -3.0e38, ALU.add, ALU.max, mx[:, i:i + 1])
            ins.then_inc(sc_read, 1)
            dve.wait_ge(sc_read, hh + 1)
            nc.vector.tensor_scalar(nmx[:, :], mx[:, :], -1.0, None, ALU.mult).then_inc(mx_neg, 1)

        def exp_act(act, hh):
            act.wait_ge(mx_neg, hh + 1)
            for i in (3, 1, 2, 0):
                w, at = P * (i + 1), ROW_AT[i]
                ins = act.activation(s_sb[:, at:at + w], s_sb[:, at:at + w], ACT.Exp, bias=nmx[:, i:i + 1],
                                     accum_out=den[:, i:i + 1])
            ins.then_inc(e_done, 1)

        def den_dve(dve, hh):
            dve.wait_ge(e_done, hh + 1)
            nc.vector.reciprocal(rden[:, :], den[:, :]).then_inc(den_inv, 1)
            dve.wait_ge(den_inv, hh + 1)
            for i in (3, 1, 2, 0):
                w, at = P * (i + 1), ROW_AT[i]
                ins = nc.vector.tensor_scalar(s_sb[:, at:at + w], s_sb[:, at:at + w], rden[:, i:i + 1], None,
                                              ALU.mult)
            ins.then_inc(p_done, 1)

        def probs_pe(pe, hh):
            pe.wait_ge(p_done, hh + 1)
            if hh:
                pe.wait_ge(pt_lo, hh)
            for j in range(TT):
                for i in range(j, TT):
                    mm = nc.tensor.transpose(PT[:, COL_AT[j] + (i - j) * P:COL_AT[j] + (i - j + 1) * P],
                                             s_sb[:, ROW_AT[i] + j * P:ROW_AT[i] + (j + 1) * P], ident[:, :])
            mm.then_inc(pt_done, 1)

        def probs_act(act, hh):
            act.wait_ge(pt_done, hh + 1)
            if hh:
                act.wait_ge(pv_done, hh)
            act.activation(pth[:, :], PT[:, 0:CW], ACT.Copy).then_inc(pt_hi, 1)

        def probs_dve(dve, hh):
            dve.wait_ge(pt_hi, hh + 1)
            nc.vector.tensor_tensor(ptl[:, :], PT[:, 0:CW], pth[:, :].bitcast(F32), ALU.subtract)\
                .then_inc(pt_lo, 1)

        def values(out_bank, v, buf, e, xh, xl, at0):
            for j in range(TT):
                w, at, cols = T - P * j, COL_AT[j] + at0, slice(HD * e, HD * e + P)
                mm = mm3(out_bank[:, P * j:T], v[0][:, buf, j, cols], v[1][:, buf, j, cols],
                         xh[:, at:at + w], xl[:, at:at + w], start=(e == 0 and j == 0), stop=(e == 1 and j == TT - 1))
            return mm

        def pv_pe(pe, hh):
            p, e = hh // 2, hh % 2
            pe.wait_ge(pt_lo, hh + 1)
            if e == 0:
                pe.wait_ge(pj_read, order[("vt", p, 0)] + 1)
                if p:
                    pe.wait_ge(o_lo, p)
            values(bank(O_BANK), (vh, vl), p % 2, e, pth, ptl, 0).then_inc(pv_done, 1)

        def o_act(act, p):
            act.wait_ge(pv_done, 2 * p + 2)
            act.activation(oh[p], bank(O_BANK), ACT.Copy).then_inc(o_hi, 1)

        def o_dve(dve, p):
            dve.wait_ge(o_hi, p + 1)
            nc.vector.tensor_tensor(ol[p], bank(O_BANK), oh[p].bitcast(F32), ALU.subtract).then_inc(o_lo, 1)

        def sb_item_pe(pe, p, par, j):
            first = isinstance(p, int) and p == 0 and j == 0
            if not first:
                pe.wait_ge(qj_read, p * 4 + j)
            if j < 3:
                c = sb_chunk(p, j)
                pe.wait_ge(w_lo, c.n + 1)
                x_ready = (u_ready, KD * 2) if first else None
                project(pe, bank(P_BANK), c, KD, P, 0, P, uh, ul, x_ready=x_ready).then_inc(w_used, 1)
            else:
                tb = tf_sb(par, 2)
                for t in range(TT):
                    mm = nc.tensor.transpose(bank(P_BANK)[:, t * P:(t + 1) * P], tf[:, tb, t * P:(t + 1) * P],
                                             ident[:, :])
                mm.then_inc(qj_mm, 1)

        def tf_sb(par, j):
            return (par * 3 + j) % 2

        def sb_chunk(p, j):
            c = Chunk(CH_SB + j)
            c.turn, c.n = c.turn + p, c.n + p * 3
            return c

        def sb_later(p, j, k):
            c = Chunk(CH_SB + j + k)
            c.turn, c.n = c.turn + p, c.n + p * 3
            return c

        def sb_item_act(act, p, par, j):
            if j < 3:
                split_hi(act, sb_later(p, j, AHEAD))
            if j == 2:
                return
            if j == 3:
                act.wait_ge(qj_mm, p + 1)
                if not isinstance(p, int) or p >= 2:
                    act.wait_ge(sv_done, 2 * p - 2)
                elif p == 0:
                    act.wait_ge(v1_ready, 1)
                src = bank(P_BANK).rearrange("p (t h n) -> p t h n", t=TT, h=2)
                a, b = v_views(sv[0], par)
                act.activation(a, src[:, :, 0, :], ACT.Copy)
                act.activation(b, src[:, :, 1, :], ACT.Copy).then_inc(qj_hi, 1)
                return
            act.wait_ge(qj_read, p * 4 + j + 1)
            if not isinstance(p, int) or p >= 2:
                act.wait_ge(z_done, 2 * p - 2)
            act.activation(sq[2 * j][:, par, :], tf[:, tf_sb(par, j), :], ACT.Copy).then_inc(qj_hi, 1)

        def sb_item_dve(dve, p, par, j, k_stat=None):
            if j < 3:
                split_lo(dve, sb_later(p, j, AHEAD))
                if k_stat is not None:
                    stat_dve(dve, k_stat, 0, r_pre)
                    dve.wait_ge(st_r, k_stat + 1)
                dve.wait_ge(w_used, sb_chunk(p, j).n + 1)
                if not (isinstance(p, int) and p == 0):
                    dve.wait_ge(qj_mm, p)
                nc.vector.scalar_tensor_tensor(tf[:, tf_sb(par, j), :], bank(P_BANK), -SCALE if j == 0 else 1.0,
                                               r_pre[:, :], ALU.mult, ALU.mult).then_inc(qj_read, 1)
                if j == 2:
                    return
                dve.wait_ge(qj_hi, p * 3 + j + 1)
                nc.vector.tensor_tensor(sq[2 * j + 1][:, par, :], tf[:, tf_sb(par, j), :],
                                        sq[2 * j][:, par, :].bitcast(F32), ALU.subtract).then_inc(qj_lo, 1)
                return
            dve.wait_ge(qj_hi, p * 3 + 3)
            src = bank(P_BANK).rearrange("p (t h n) -> p t h n", t=TT, h=2)
            for x in range(2):
                ins = nc.vector.tensor_tensor(v_views(sv[1], par)[x], src[:, :, x, :],
                                              v_views(sv[0], par)[x].bitcast(F32), ALU.subtract)
            ins.then_inc(qj_read, 1)

        def z_pe(pe, p, par, e, first=False):
            hh = p * 2 + e
            pe.wait_ge(qj_lo, p * 2 + 2)
            if not (isinstance(p, int) and hh < 2):
                pe.wait_ge(w_exp, hh - 1)
            rows = slice(HD * e, HD * e + HD)
            Z = ZB[e]
            for j in (0, 1, 3, 2):
                w, at = T - P * j, COL_AT[j]
                k = slice(j * P, (j + 1) * P)
                mm3(Z[:, at:at + w], sq[2][rows, par, k], sq[3][rows, par, k],
                    sq[0][rows, par, P * j:T], sq[1][rows, par, P * j:T], start=(j != 3), stop=False)
                mm = nc.tensor.matmul(Z[:, at:at + P], identb[:, :], big[:, :], start=False, stop=False,
                                      skip_group_check=True)
            mm.then_inc(z_done, 1)

        def z_dve_clamp(dve, p, e):
            dve.wait_ge(z_done, p * 2 + e + 1)
            if not (isinstance(p, int) and p * 2 + e == 0):
                dve.wait_ge(ns_lo, p * 2 + e)
            nc.vector.tensor_scalar(lsp[:, :], ZB[e][:, 0:CW], -40.0, None, ALU.max).then_inc(z_min, 1)

        def z_act(act, p, e):
            hh = p * 2 + e
            act.wait_ge(z_min, hh + 1)
            act.activation(lsp[:, :], lsp[:, :], ACT.Exp, scale=-1.0).then_inc(z_exp, 1)
            act.wait_ge(z_exp, hh + 1)
            act.activation(lsp[:, :], lsp[:, :], ACT.Ln, bias=1.0).then_inc(z_ln, 1)

        def z_dve(dve, p, e):
            hh = p * 2 + e
            dve.wait_ge(z_ln, hh + 1)
            nc.vector.scalar_tensor_tensor(lsp[:, :], lsp[:, :], -1.0, ZB[e][:, 0:CW], ALU.mult, ALU.min)\
                .then_inc(ns_f, 1)

        def ns_act(act, p, e, first=False):
            hh = p * 2 + e
            act.wait_ge(ns_f, hh + 1)
            if not first:
                act.wait_ge(c_done, hh)
            act.activation(nsh[:, :], lsp[:, :], ACT.Copy).then_inc(ns_hi, 1)

        def ns_dve(dve, p, e):
            dve.wait_ge(ns_hi, p * 2 + e + 1)
            nc.vector.tensor_tensor(nsl[:, :], lsp[:, :], nsh[:, :].bitcast(F32), ALU.subtract).then_inc(ns_lo, 1)

        def c_pe(pe, p, e):
            hh = p * 2 + e
            pe.wait_ge(ns_lo, hh + 1)
            Z = ZB[e]
            for j in range(TT):
                for jj in range(j, TT):
                    at, w = COL_AT[j] + (jj - j) * P, T - P * jj
                    lt = negtri if jj == j else negones
                    for n in (nsh, nsl):
                        mm = nc.tensor.matmul(Z[:, at:at + w], lt[:, :], n[:, COL_AT[jj]:COL_AT[jj] + w],
                                              start=False, stop=False, skip_group_check=True)
            mm.then_inc(c_done, 1)

        def w_act(act, p, e, first=False):
            hh = p * 2 + e
            act.wait_ge(c_done, hh + 1)
            if not first:
                act.wait_ge(sw_lo, hh)
            act.activation(wf[:, :], ZB[e][:, 0:CW], ACT.Exp, scale=-1.0).then_inc(w_exp, 1)

        def w_dve(dve, p, e, first=False):
            hh = p * 2 + e
            dve.wait_ge(w_exp, hh + 1)
            if not first:
                dve.wait_ge(sv_done, hh - 1)
            nc.vector.tensor_copy(swh[:, e, :], wf[:, :]).then_inc(sw_hi, 1)

        def w_pool(pool, p, e):
            pool.wait_ge(sw_hi, p * 2 + e + 1)
            nc.gpsimd.tensor_tensor(swl[:, e, :], wf[:, :], swh[:, e, :].bitcast(F32), ALU.subtract)\
                .then_inc(sw_lo, 1)

        def sb_pv_pe(pe, p, par, e):
            hh = p * 2 + e
            pe.wait_ge(sw_lo, hh + 1)
            if e == 0:
                pe.wait_ge(qj_read, p * 4 + 4)
                if not (isinstance(p, int) and p == 0):
                    pe.wait_ge(so_lo_s, p)
            values(bank(O_BANK), sv, par, e, swh[:, e, :], swl[:, e, :], 0).then_inc(sv_done, 1)

        def sb_o_act(act, p):
            act.wait_ge(sv_done, p * 2 + 2)
            o = soh[:, p, :] if isinstance(p, int) else soh[:, bass.ds(p, 1), :]
            act.activation(o, bank(O_BANK), ACT.Copy).then_inc(so_hi_s, 1)

        def sb_o_dve(dve, p):
            dve.wait_ge(so_hi_s, p + 1)
            h = soh[:, p, :] if isinstance(p, int) else soh[:, bass.ds(p, 1), :]
            o = sol[:, p, :] if isinstance(p, int) else sol[:, bass.ds(p, 1), :]
            nc.vector.tensor_tensor(o, bank(O_BANK), h.bitcast(F32), ALU.subtract).then_inc(so_lo_s, 1)

        def sb_pair_pe(pe, p, par, first=False, last=False):
            q = 1 - par
            if not last:
                sb_item_pe(pe, p + 1, q, 0)
            z_pe(pe, p, par, 1)
            c_pe(pe, p, 0)
            if not last:
                sb_item_pe(pe, p + 1, q, 1)
            if not first:
                sb_pv_pe(pe, p - 1, q, 1)
            if not last:
                sb_item_pe(pe, p + 1, q, 2)
                z_pe(pe, p + 1, q, 0)
            c_pe(pe, p, 1)
            if not last:
                sb_item_pe(pe, p + 1, q, 3)
            sb_pv_pe(pe, p, par, 0)

        def sb_pair_act(act, p, par, first=False, last=False):
            q = 1 - par
            if not last:
                sb_item_act(act, p + 1, q, 0)
            z_act(act, p, 1)
            ns_act(act, p, 1)
            w_act(act, p, 0, first)
            if not last:
                sb_item_act(act, p + 1, q, 1)
            if not first:
                sb_o_act(act, p - 1)
            if not last:
                sb_item_act(act, p + 1, q, 2)
                z_act(act, p + 1, 0)
                ns_act(act, p + 1, 0)
            w_act(act, p, 1)
            if not last:
                sb_item_act(act, p + 1, q, 3)

        def sb_pair_dve(dve, p, par, first=False, last=False):
            q = 1 - par
            if not last:
                sb_item_dve(dve, p + 1, q, 0)
            z_dve_clamp(dve, p, 1)
            z_dve(dve, p, 1)
            ns_dve(dve, p, 1)
            if not last:
                sb_item_dve(dve, p + 1, q, 1)
            w_dve(dve, p, 0, first)
            if not first:
                sb_o_dve(dve, p - 1)
            if not last:
                sb_item_dve(dve, p + 1, q, 2)
                z_dve_clamp(dve, p + 1, 0)
                z_dve(dve, p + 1, 0)
                ns_dve(dve, p + 1, 0)
                sb_item_dve(dve, p + 1, q, 3)
            w_dve(dve, p, 1, first)

        def sb_turns(eng, pair):
            pair(eng, 0, 0, first=True)
            with eng.Fori(0, (SB_PAIRS - 2) // 2) as i:
                pair(eng, i * 2 + 1, 1)
                pair(eng, i * 2 + 2, 0)
            pair(eng, SB_PAIRS - 1, 1, last=True)

        block = ctx.enter_context(nc.Block())

        @block.sync
        def _(sp):
            for v, (g, r0, n) in enumerate(((mix_pre_g, G_MIX_PRE, 16), (mix_post_g, G_MIX_POST, 16),
                                            (ffn_pre_g, G_FFN_PRE, 16), (ffn_post_g, G_FFN_POST, 16),
                                            (mla_q_norm_g, G_Q, KQ), (mla_kv_norm_g, G_KV, KKV))):
                sp.dma_start(graw[r0:r0 + n, :], g.rearrange("l (k p) -> (l k) p", p=P)).then_inc(gains_in, 16)
            for t in range(TT):
                sp.dma_start(xt[:, t, :], x[0, t * P:(t + 1) * P, :]).then_inc(x_in[t], 16)
            for n, (at, cols) in enumerate(IN_TILES):
                load(sp, Chunk(CH_IN + n), ab_w_in[0][:, at:at + cols], KD, cols, P)
                if n == 2:
                    sp.dma_start(hot[:, :], onehot_d).then_inc(bias_in_sbuf, 16)
                    sp.dma_start(rb[0:NBUCKET, :], rel_bias).then_inc(bias_in_sbuf, 16)
            sp.wait_ge(brow_sb, 1)
            sp.dma_start(bias_t.ap(), brow[:, :].unsqueeze(1).to_broadcast([8, P, 640])).then_inc(brow_out, 16)
            sp.wait_ge(brow_out, 16)
            sp.wait_ge(h_ready, KD)
            sp.wait_ge(ssx_ready, TT)
            sp.dma_start(cs[ROPE_ROWS, :, :], rope_d.rearrange("a r t -> r a t")).then_inc(tables_in, 16)
            for p in range(MLA_PAIRS):
                load(sp, Chunk(CH_MLA + 2 * p), mla_w_uq[0][:, 2 * p * MLA_QH:2 * (p + 1) * MLA_QH], KQ, 2 * MLA_QH)
                c = Chunk(CH_MLA + 2 * p + 1)
                sp.wait_ge(w_lo, c.n - NSLOT + 1)
                for kv in range(2):
                    for h in range(2):
                        at = (2 * p + h) * 2 * HD + kv * HD
                        dst = raw[:, c.slot, kv * KKV * P:(kv + 1) * KKV * P].rearrange("p (k h n) -> p k h n", k=KKV, h=2)
                        sp.dma_start(dst[:, :, h, :], mla_w_ukv[0][:, at:at + HD].rearrange("(k p) n -> p k n", p=P))\
                            .then_inc(ukv_in[p % 2] if 2 * kv + h < 3 else raw_in[c.slot], 16)
            for m in range(MOBA_PAIRS):
                for j in range(3):
                    load(sp, Chunk(CH_MOBA + 3 * m + j),
                         ab_w_in[0][:, O3 + 512 * j + P * m:O3 + 512 * j + P * (m + 1)], KD, P)
            out_sp(sp, CH_OUT0, ab_w_out[0])
            gu_sp(sp, CH_GU0, ffn_w_gate_up[0])
            dn_sp(sp, CH_DN0, ffn_w_down[0])
            with sp.Fori(0, SB_PAIRS) as p:
                for j in range(3):
                    load(sp, sb_chunk(p, j), sb_w_qkv[0][:, bass.ds(p * P + D * j, P)], KD, P)
            out_sp(sp, CH_OUT1, sb_w_out[0])
            gu_sp(sp, CH_GU1, ffn_w_gate_up[1])
            dn_sp(sp, CH_DN1, ffn_w_down[1])
            y = out[0].rearrange("(t p) d -> p t d", p=P)
            for n in range(KD):
                sp.wait_ge(y_sb, n + 1)
                sp.dma_start(y[:, :, n * P:(n + 1) * P], ot[:, n, :].rearrange("p (t d) -> p t d", t=TT))\
                    .then_inc(y_out, 16)
            sp.wait_ge(y_out, 16 * KD)
            sp.wait_ge(brow_out, 16)

        @block.gpsimd
        def _(pool):
            nc.gpsimd.memset(ones[:, :], 1.0).then_inc(tri_ready, 1)
            pool.wait_ge(tri_ready, 1)
            nc.gpsimd.memset(eps_t[:, :], EPS).then_inc(tri_ready, 1)
            pool.wait_ge(tri_ready, 2)
            nc.gpsimd.memset(rb[NBUCKET:NBUCKET + 1, :], NEG).then_inc(tri_ready, 1)
            pool.wait_ge(tri_ready, 3)
            nc.gpsimd.affine_select(out=ident[:, :], in_=ones[:, :], compare_op=ALU.is_equal, fill=0.0, base=0,
                                    pattern=[[-1, P]], channel_multiplier=1).then_inc(consts_ready, 1)
            nc.gpsimd.affine_select(out=tri_f[:, :], in_=ones[:, :], compare_op=ALU.is_ge, fill=0.0, base=0,
                                    pattern=[[-1, P]], channel_multiplier=1).then_inc(consts_ready, 1)
            pool.wait_ge(consts_ready, 2)
            for v in (vh, vl):
                nc.gpsimd.memset(v[:, :, :, HD:2 * HD].bitcast(F32), 0.0)
            pool.wait_ge(h_ready, KD)
            pool.wait_ge(ssx_ready, TT)
            pool.wait_ge(brow_out, 16)
            nc.gpsimd.memset(cmask[:, :], 0.0).then_inc(v0_ready, 1)
            pool.wait_ge(v0_ready, 1)
            nc.gpsimd.affine_select(out=cmask[:, :], in_=cmask[:, :], compare_op=ALU.is_ge, fill=NEG, base=T - P,
                                    pattern=[[-1, T]], channel_multiplier=1).then_inc(v0_ready, 1)
            for n in (1, 2):
                add_squares(pool, n, N_CQ)
            add_squares(pool, 1, N_CKV)
            pool.wait_ge(tables_in, 16)
            pool.wait_ge(sq_added, AD0[N_CKV + 1])
            rope_rows_pool(pool, 1, 0, (in_scaled, 6))
            for g in groups[0:1]:
                for it in g:
                    item_pool(pool, it)

            def load_bias(m):
                if m >= 2:
                    pool.wait_ge(sc_read, 2 * MLA_PAIRS + m - 1)
                else:
                    pool.wait_ge(sc_done, 3 * 2 * MLA_PAIRS)
                skewed = bass.AP(tensor=bias_t, offset=640 * P * m + P - 1, ap=[[640 - 1, P], [1, T]])
                pool.dma_start(bias[:, m % 2, :], skewed)\
                    .then_inc(bias_in[m % 2], 16)

            for hh in range(NH0):
                for it in slots_of_step(hh):
                    item_pool(pool, it)
                if hh == 2 * MLA_PAIRS - 2:
                    load_bias(0)
                    load_bias(1)
                elif 2 * MLA_PAIRS - 2 < hh < NH0 - 3:
                    load_bias(hh - 2 * MLA_PAIRS + 3)
            pool.wait_ge(rp_cos, 2 * MLA_PAIRS + 1)
            f_adds(pool, 0, N_POST_A0)
            res_pool(pool, 0, N_POST_A0, True)
            gu_pool(pool, 0)
            f_adds(pool, 1, N_POST_F0)
            for v in sv:
                ins = nc.gpsimd.memset(v[:, :, :, HD:2 * HD].bitcast(F32), 0.0)
            ins.then_inc(v1_ready, 1)
            res_pool(pool, 1, N_POST_F0, True)

            def pair(pool, p, par, first=False, last=False):
                w_pool(pool, p, 0)
                w_pool(pool, p, 1)
            sb_turns(pool, pair)
            f_adds(pool, 2, N_POST_A1)
            res_pool(pool, 2, N_POST_A1, True)
            gu_pool(pool, 1)
            f_adds(pool, 3, N_POST_F1)
            res_pool(pool, 3, N_POST_F1, False)

        @block.scalar
        def _(act):
            act.wait_ge(gains_ready, 1)
            for n in range(AHEAD):
                split_hi(act, Chunk(n))
            for k in range(KD):
                act.wait_ge(h_ready, k + 1)
                act.activation(uh[:, k, :], hT[:, k, :], ACT.Copy, scale=gains[:, k:k + 1]).then_inc(uh_ready, 1)
                if k % 2:
                    t = k // 2
                    act.wait_ge(x_in[t], 16)
                    if t:
                        act.wait_ge(ssx_ready, t)
                    act.activation(junk[:, :], xt[:, t, :], ACT.Square, accum_out=ssx[:, t:t + 1]).then_inc(ssx_ready, 1)
            act.wait_ge(consts_ready, 2)
            act.activation(negtri[:, :], tri_f[:, :], ACT.Copy, scale=-1.0)
            act.activation(negones[:, :], ones[:, :], ACT.Copy, scale=-1.0)
            act.activation(identb[:, :], ident[:, :], ACT.Copy)
            act.activation(big[:, :], tri_f[:, :], ACT.Copy, scale=-NEG).then_inc(tri_r_ready, 1)
            stat_act(act, N_X, None, D)
            for n in range(len(IN_TILES)):
                split_hi(act, Chunk(CH_IN + n + AHEAD), ukv(CH_IN + n + AHEAD))
                if n == len(IN_TILES) - 1:
                    break
                hi, _, m = lat_dst[n]
                k, first = lat_norm[n]
                act.wait_ge(in_scaled, n + 1)
                if n == 0:
                    act.wait_ge(brow_out, 16)
                act.activation(hi[:, m, :], tf[:, n % 2, :], ACT.Copy,
                               scale=gains[:, lat_gain[n]:lat_gain[n] + 1]).then_inc(lat_hi, 1)
                square(act, tf[:, n % 2, :], first, k)
            act.wait_ge(rp_done, 1)
            for b in range(3):
                ins = act.activation(mq[2][ROPE_ROWS, b, :], tf[ROPE_ROWS, 1, :], ACT.Copy)
            ins.then_inc(kr_hi, 1)
            stat_act(act, N_CQ, bank(6)[:, 0:TT], QL)
            stat_act(act, N_CKV, bank(6)[:, 0:TT], KVL)
            for it in groups[0]:
                item_act(act, it)
            exp_act(act, 0)
            for hh in range(NH0):
                a, b, c = slots_of_step(hh)
                item_act(act, a)
                probs_act(act, hh)
                item_act(act, b)
                if hh + 1 < NH0:
                    exp_act(act, hh + 1)
                item_act(act, c)
                if hh % 2:
                    o_act(act, hh // 2)
            out_act(act, CH_OUT0, N_POST_A0)
            stat_act(act, N_POST_A0, bank(0)[:, 0:TT], D)
            res_act(act, 0, N_POST_A0, G_FFN_PRE)
            gu_act(act, CH_GU0, 0, N_FFN0)
            dn_act(act, CH_DN0, N_POST_F0)
            stat_act(act, N_POST_F0, bank(0)[:, 0:TT], D)
            res_act(act, 1, N_POST_F0, G_MIX_PRE + KD)
            act.wait_ge(res_h, 2 * KD)
            stat_act(act, N_SB, bank(0)[:, 0:TT], D)
            for j in range(4):
                sb_item_act(act, 0, 0, j)
            z_act(act, 0, 0)
            ns_act(act, 0, 0, True)
            sb_turns(act, sb_pair_act)
            sb_o_act(act, SB_PAIRS - 1)
            out_act(act, CH_OUT1, N_POST_A1)
            stat_act(act, N_POST_A1, bank(0)[:, 0:TT], D)
            res_act(act, 2, N_POST_A1, G_FFN_PRE + KD)
            gu_act(act, CH_GU1, 1, N_FFN1)
            dn_act(act, CH_DN1, N_POST_F1)
            stat_act(act, N_POST_F1, bank(0)[:, 0:TT], D)
            for n in range(KD):
                act.wait_ge(y_tr, n + 1)
                act.activation(ot[:, n, :], bank(n), ACT.Copy).then_inc(y_sb, 1)

        @block.vector
        def _(dve):
            dve.wait_ge(gains_tr, 1)
            nc.vector.tensor_copy(gains[:, :], bank(7)[:, 0:G_ROWS]).then_inc(gains_ready, 1)
            dve.wait_ge(gains_ready, 1)
            for k in range(KD + 1):
                if k < KD:
                    dve.wait_ge(x_tr, k + 1)
                    nc.vector.tensor_copy(hT[:, k, :], bank(k)).then_inc(h_ready, 1)
                if k:
                    m = k - 1
                    dve.wait_ge(uh_ready, m + 1)
                    nc.vector.scalar_tensor_tensor(ul[:, m, :], hT[:, m, :], gains[:, m:m + 1],
                                                   uh[:, m, :].bitcast(F32), ALU.mult, ALU.subtract)\
                        .then_inc(u_ready, 1)
                if k == 2:
                    for n in range(AHEAD):
                        split_lo(dve, Chunk(n))
            split_lo(dve, Chunk(AHEAD))
            dve.wait_ge(brow_mm, 1)
            nc.vector.tensor_copy(brow[:, 0:T], bank(6)[0:8, :])
            nc.vector.tensor_copy(brow[:, T:640], bank(7)[0:8, 0:640 - T]).then_inc(brow_sb, 1)
            stat_dve(dve, N_X, 5, r_pre)
            dve.wait_ge(st_r, 1)
            for n in range(len(IN_TILES)):
                if n:
                    split_lo(dve, Chunk(CH_IN + n + AHEAD))
                dve.wait_ge(w_used, CH_IN + n + 1)
                rows = slice(0, P) if n < 5 else ROPE_ROWS
                if 2 <= n:
                    m = n - 2
                    k, j = lat_norm[m]
                    dve.wait_ge(sq_ready, SQ0[k] + j + 1)
                nc.vector.tensor_tensor(tf[rows, n % 2, :], bank(n)[rows, :], r_pre[rows, :], ALU.mult)\
                    .then_inc(in_scaled, 1)
                if n < 5:
                    hi, lo, m = lat_dst[n]
                    dve.wait_ge(lat_hi, n + 1)
                    nc.vector.scalar_tensor_tensor(lo[:, m, :], tf[:, n % 2, :],
                                                   gains[:, lat_gain[n]:lat_gain[n] + 1],
                                                   hi[:, m, :].bitcast(F32), ALU.mult, ALU.subtract)\
                        .then_inc(lat_ready, 1)
            dve.wait_ge(tables_in, 16)
            rope_rows_dve(dve, 1, 0, (in_scaled, 6))
            dve.wait_ge(kr_hi, 1)
            for b in range(3):
                ins = nc.vector.tensor_tensor(mq[3][ROPE_ROWS, b, :], tf[ROPE_ROWS, 1, :],
                                              mq[2][ROPE_ROWS, b, :].bitcast(F32), ALU.subtract)
            ins.then_inc(kr_lo, 1)
            stat_dve(dve, N_CQ, 6, r_q)
            stat_dve(dve, N_CKV, 6, r_kv)
            dve.wait_ge(st_r, 3)
            for it in groups[0]:
                item_dve(dve, it)
            scores_dve(dve, 0)
            den_dve(dve, 0)
            for hh in range(NH0):
                a, b, c = slots_of_step(hh)
                item_dve(dve, a)
                probs_dve(dve, hh)
                item_dve(dve, b)
                if hh + 1 < NH0:
                    scores_dve(dve, hh + 1)
                    den_dve(dve, hh + 1)
                item_dve(dve, c)
                if hh % 2:
                    o_dve(dve, hh // 2)
            out_dve(dve, CH_OUT0)
            res_dve(dve, 0, N_POST_A0, G_MIX_POST, G_FFN_PRE)
            gu_dve(dve, CH_GU0, 0, N_FFN0)
            dn_dve(dve, CH_DN0)
            res_dve(dve, 1, N_POST_F0, G_FFN_POST, G_MIX_PRE + KD)
            for j in range(4):
                sb_item_dve(dve, 0, 0, j, N_SB if j == 0 else None)
            z_dve_clamp(dve, 0, 0)
            z_dve(dve, 0, 0)
            ns_dve(dve, 0, 0)
            sb_turns(dve, sb_pair_dve)
            sb_o_dve(dve, SB_PAIRS - 1)
            out_dve(dve, CH_OUT1)
            res_dve(dve, 2, N_POST_A1, G_MIX_POST + KD, G_FFN_PRE + KD)
            gu_dve(dve, CH_GU1, 1, N_FFN1)
            dn_dve(dve, CH_DN1)
            res_dve(dve, 3, N_POST_F1, G_FFN_POST + KD, None)

        @block.tensor
        def _(pe):
            pe.wait_ge(consts_ready, 1)
            pe.wait_ge(gains_in, 16 * 6)
            nc.tensor.transpose(bank(7)[:, 0:G_ROWS], graw[:, :], ident[0:G_ROWS, 0:G_ROWS]).then_inc(gains_tr, 1)
            for k in range(KD):
                if k == KD - 1:
                    pe.wait_ge(gains_ready, 1)
                for t in range(TT):
                    if k == 0:
                        pe.wait_ge(x_in[t], 16)
                    mm = nc.tensor.transpose(bank(k)[:, t * P:(t + 1) * P], xt[:, t, k * P:(k + 1) * P], ident[:, :])
                mm.then_inc(x_tr, 1)
            for n, (_, cols) in enumerate(IN_TILES):
                c = Chunk(CH_IN + n)
                pe.wait_ge(w_lo, c.n + 1)
                project(pe, bank(n)[0:cols, :], c, KD, P, 0, cols, uh, ul,
                        x_ready=(u_ready, 0) if n == 0 else None).then_inc(w_used, 1)
                if n == 0:
                    pe.wait_ge(bias_in_sbuf, 32)
                    nc.tensor.matmul(bank(6)[0:8, :], rb[:, :], hot[:, 0:T], start=True, stop=True)
                    nc.tensor.matmul(bank(7)[0:8, 0:640 - T], rb[:, :], hot[:, T:640], start=True, stop=True)\
                        .then_inc(brow_mm, 1)
                    stat_pe_spread(pe, N_X, 5)
                if n == 4:
                    pe.wait_ge(brow_sb, 1)
                    pe.wait_ge(st_r, 1)
                    stat_pe(pe, N_CQ, 6, AD0[N_CKV])
            stat_pe_spread(pe, N_CQ, 6)
            pe.wait_ge(st_r, N_CQ + 1)
            stat_pe(pe, N_CKV, 6, AD0[N_CKV + 1])
            stat_pe_spread(pe, N_CKV, 6)
            pe.wait_ge(lat_ready, 5)
            for it in groups[0]:
                item_pe(pe, it)
            pe.wait_ge(rp_done, 1)
            scores_pe(pe, 0)
            for hh in range(NH0):
                a, b, c = slots_of_step(hh)
                item_pe(pe, a)
                probs_pe(pe, hh)
                item_pe(pe, b)
                if hh + 1 < NH0:
                    scores_pe(pe, hh + 1)
                item_pe(pe, c)
                pv_pe(pe, hh)
            out_pe(pe, CH_OUT0, 0, lambda k: (oh[k], ol[k]), (o_lo, MLA_PAIRS + MOBA_PAIRS))
            stat_pe(pe, N_POST_A0, 0, AD0[N_POST_A0 + 1])
            stat_pe_spread(pe, N_POST_A0, 0)
            gu_pe(pe, CH_GU0, 0, N_FFN0)
            dn_pe(pe, CH_DN0, 1, 0)
            stat_pe(pe, N_POST_F0, 0, AD0[N_POST_F0 + 1])
            stat_pe_spread(pe, N_POST_F0, 0)
            pe.wait_ge(tri_r_ready, 1)
            sb_item_pe(pe, 0, 0, 0)
            stat_pe(pe, N_SB, 0, AD0[N_SB + 1])
            stat_pe_spread(pe, N_SB, 0)
            for j in range(1, 4):
                sb_item_pe(pe, 0, 0, j)
            z_pe(pe, 0, 0, 0)
            sb_turns(pe, sb_pair_pe)
            sb_pv_pe(pe, SB_PAIRS - 1, 1, 1)
            out_pe(pe, CH_OUT1, 2, lambda k: (soh[:, k, :], sol[:, k, :]), (so_lo_s, SB_PAIRS))
            stat_pe(pe, N_POST_A1, 0, AD0[N_POST_A1 + 1])
            stat_pe_spread(pe, N_POST_A1, 0)
            gu_pe(pe, CH_GU1, 1, N_FFN1)
            dn_pe(pe, CH_DN1, 3, 1)
            stat_pe(pe, N_POST_F1, 0, AD0[N_POST_F1 + 1])
            stat_pe_spread(pe, N_POST_F1, 0)
            pe.wait_ge(st_r, N_POST_F1 + 1)
            for n in range(KD):
                pe.wait_ge(res_h, 3 * KD + n + 1)
                for t in range(TT):
                    mm = nc.tensor.transpose(bank(n)[:, t * P:(t + 1) * P], hT[:, n, t * P:(t + 1) * P], ident[:, :])
                mm.then_inc(y_tr, 1)


_INS = ['x', 'mix_pre_g', 'mix_post_g', 'ffn_pre_g', 'ffn_post_g', 'ab_w_in', 'mla_q_norm_g', 'mla_w_uq',
        'mla_kv_norm_g', 'mla_w_ukv', 'ab_w_out', 'rel_bias', 'sb_w_qkv', 'sb_w_out', 'ffn_w_gate_up', 'ffn_w_down']
_OUTS = [((1, T, D), 'float32')]


def kernel(**inputs):
    import numpy as _np
    import concourse.bacc as _bacc
    from concourse import mybir as _mybir
    from concourse.bass_utils import run_bass_kernel_spmd as _run

    nc = _bacc.Bacc("TRN2", target_bir_lowering=False, num_devices=1)
    arrays, args = {}, []
    for name in _INS:
        a = _np.ascontiguousarray(inputs[name])
        arrays[f"in_{name}_dram"] = a
        args.append(nc.dram_tensor(f"in_{name}_dram", a.shape, _mybir.dt.from_np(a.dtype), kind="ExternalInput").ap())
    for i, (shape, dtype) in enumerate(_OUTS):
        dt = _mybir.dt.from_np(_np.dtype(dtype))
        args.append(nc.dram_tensor(f"out_{i}_dram", shape, dt, kind="ExternalOutput").ap())
    bass_hybrid_two_layers(nc, *args)
    r = _run(nc, [arrays], core_ids=[0])
    got = tuple(r.results[0][f"out_{i}_dram"] for i in range(len(_OUTS)))
    return got[0]
```

```python
import math
from contextlib import ExitStack

import numpy as np

import concourse.bass as bass
from concourse import mybir

F32 = mybir.dt.float32
F32R = mybir.dt.float32r
BF16 = mybir.dt.bfloat16
ALU = mybir.AluOpType
ACT = mybir.ActivationFunctionType

P = 128
T = 512
TT = T // P
D = 1024
KD = D // P
FF = 2816
KF = FF // P
EPS = 1e-6
NEG = -1e30
HD = 64
ROPE = 32
QL, KVL = 384, 256
KQ, KKV = QL // P, KVL // P
MLA_QH = HD + ROPE
MLA_SCALE = float(MLA_QH) ** -0.5
SCALE = float(HD) ** -0.5
THETA = 10000.0
NBUCKET, MAXDIST = 32, 128
O1, O2, O3 = QL, QL + KVL, QL + KVL + ROPE
MLA_PAIRS, MOBA_PAIRS, SB_PAIRS = 4, 4, 8
NH0 = 2 * (MLA_PAIRS + MOBA_PAIRS)
NH1 = 2 * SB_PAIRS

ROW_AT = {3: 0, 2: 512, 0: 896, 1: 1024}
COL_AT = {0: 0, 1: 512, 3: 896, 2: 1024}
CW = 1280

NSLOT = 3
AHEAD = 2
CH_IN = 0
CH_MLA = CH_IN + 6
CH_MOBA = CH_MLA + 2 * MLA_PAIRS
CH_OUT0 = CH_MOBA + 3 * MOBA_PAIRS
CH_GU0 = CH_OUT0 + KD
CH_DN0 = CH_GU0 + 2 * KF
CH_SB = CH_DN0 + 3 * KD
CH_OUT1 = CH_SB + 3 * SB_PAIRS
CH_GU1 = CH_OUT1 + KD
CH_DN1 = CH_GU1 + 2 * KF
CH_END = CH_DN1 + 3 * KD
DN_PARTS = ((0, 8), (8, 7), (15, 7))

G_MIX_PRE, G_MIX_POST, G_FFN_PRE, G_FFN_POST, G_Q, G_KV, G_ROWS = 0, 16, 32, 48, 64, 67, 69


def rope_tables():
    half = ROPE // 2
    inv = (np.float32(THETA) ** (-np.arange(half, dtype=np.float32) / np.float32(half))).astype(np.float32)
    ang = np.arange(T, dtype=np.float32)[None, :] * inv[:, None]
    cos, sin = np.cos(ang).astype(np.float32), np.sin(ang).astype(np.float32)
    return np.stack([np.concatenate([cos, cos]), np.concatenate([-sin, sin])])


def bucket_onehot():
    rel = 511 - np.arange(640)
    exact = NBUCKET // 2
    big = exact + (np.log(np.maximum(rel, exact).astype(np.float32) / np.float32(exact))
                   / np.float32(math.log(MAXDIST / exact)) * (NBUCKET - exact)).astype(np.int32)
    bucket = np.where(np.maximum(rel, 0) < exact, np.maximum(rel, 0), np.minimum(big, NBUCKET - 1))
    hot = (bucket[None, :] == np.arange(NBUCKET + 1)[:, None]) & (rel >= 0)[None, :]
    hot[NBUCKET] = rel < 0
    return hot.astype(np.float32)


class Chunk:

    def __init__(self, c0, i=0, per=0):
        assert per % NSLOT == 0
        self.c0, self.i, self.per = c0, i, per
        self.slot = c0 % NSLOT
        self.turn = c0 // NSLOT + i * (per // NSLOT)
        self.n = c0 + i * per

    def later(self, k):
        return Chunk(self.c0 + k, self.i, self.per)


def layer0_items():
    groups = []
    for p in range(MLA_PAIRS):
        cq, ck = CH_MLA + 2 * p, CH_MLA + 2 * p + 1
        groups.append([("mq", p, 0, cq, True, False), ("mk", p, 0, ck, True, False),
                       ("mq", p, 1, cq, False, True), ("mk", p, 1, ck, False, False),
                       ("mv", p, 0, ck, False, True), ("vt", p, 0, None, False, False)])
    for m in range(MOBA_PAIRS):
        p, c = MLA_PAIRS + m, CH_MOBA + 3 * m
        groups.append([("bq", p, 0, c, True, True), ("bk", p, 0, c + 1, True, True),
                       ("bv", p, 0, c + 2, True, True), ("vt", p, 0, None, False, False)])
    return groups


def bass_hybrid_two_layers(nc, x, mix_pre_g, mix_post_g, ffn_pre_g, ffn_post_g, ab_w_in,
                           mla_q_norm_g, mla_w_uq, mla_kv_norm_g, mla_w_ukv, ab_w_out, rel_bias,
                           sb_w_qkv, sb_w_out, ffn_w_gate_up, ffn_w_down, out):
    onehot_d = nc.inline_tensor(bucket_onehot(), name="bucket_onehot").ap()
    rope_d = nc.inline_tensor(rope_tables(), name="rope_tables").ap()
    bias_t = nc.dram_tensor("bias_by_distance", [8, P, 640], F32, kind="Internal")

    groups = layer0_items()
    items = [it for g in groups for it in g]
    order = {it[:3]: n for n, it in enumerate(items)}
    split_order = {}
    for it in items:
        if it[0] not in ("mv", "bv"):
            split_order[it[:3]] = len(split_order)
    inner_order = {}
    for it in items:
        if not it[5]:
            inner_order[it[:3]] = len(inner_order)

    def slots_of_step(hh):
        p, e = hh // 2, hh % 2
        if e:
            vt = groups[p + 1][-1] if p + 1 < len(groups) else None
            return [vt] + (groups[p + 2][0:2] if p + 2 < len(groups) else [None, None])
        if p + 1 >= len(groups):
            return [None] * 3
        g = groups[p + 1]
        return g[2:5] if len(g) == 6 else [g[2], None, None]

    ctx = ExitStack()
    with ctx:
        def sem(name):
            return ctx.enter_context(nc.semaphore(name))

        def sb(stack, name, shape, dt=F32):
            return stack.enter_context(nc.sbuf_tensor(name, shape, dt))

        hT = sb(ctx, "residual", [P, KD, T])
        uh = sb(ctx, "u_hi", [P, KD, T], F32R)
        with ExitStack() as s:
            F = sb(s, "block_out", [P, KD, T])
        ul = sb(ctx, "u_lo", [P, KD, T], F32R)
        raw = sb(ctx, "w_raw", [P, NSLOT, 1024])
        wh = sb(ctx, "w_hi", [P, NSLOT, 1024], F32R)
        wl = sb(ctx, "w_lo", [P, NSLOT, 1024], F32R)
        ident = sb(ctx, "ident", [P, P])
        ones = sb(ctx, "ones", [P, P])
        tri_f = sb(ctx, "tri_f", [P, P])
        negtri = sb(ctx, "negtri", [P, P], F32R)
        negones = sb(ctx, "negones", [P, P], F32R)
        identb = sb(ctx, "identb", [P, P], BF16)
        big = sb(ctx, "big", [P, P], BF16)
        gains = sb(ctx, "gains", [P, G_ROWS])
        r_pre = sb(ctx, "r_pre", [P, T])
        r_post = sb(ctx, "r_post", [P, T])
        acc = sb(ctx, "sq_sum", [P, T])
        sqt = sb(ctx, "sq_tile", [P, T])
        diag = sb(ctx, "diag", [P, TT, P])
        tf = sb(ctx, "tf", [P, 2, T])
        rms = sb(ctx, "rms", [P, TT])
        rinv = sb(ctx, "rinv", [P, TT])
        ssx = sb(ctx, "ssx", [P, TT])
        eps_t = sb(ctx, "eps", [P, 1])
        with ExitStack() as at0:
            vh = sb(at0, "v_hi", [P, 2, TT, 192], F32R)
            vl = sb(at0, "v_lo", [P, 2, TT, 192], F32R)
            oAh = sb(at0, "oA_hi", [P, 4, T], F32R)
            oAl = sb(at0, "oA_lo", [P, 4, T], F32R)
            logits = sb(at0, "logits", [P, 2, CW])
            pth = sb(at0, "probsT_hi", [P, CW], F32R)
            ptl = sb(at0, "probsT_lo", [P, CW], F32R)
            mx = sb(at0, "row_max", [P, 2, TT])
            nmx = sb(at0, "neg_max", [P, 2, TT])
            den = sb(at0, "den", [P, 2, TT])
            rden = sb(at0, "rden", [P, 2, TT])
            with ExitStack() as s:
                xt = sb(s, "x_tokens", [P, TT, D])
                junk = sb(s, "x_squares", [P, D])
                graw = sb(s, "gain_rows", [G_ROWS, P])
            with ExitStack() as s:
                sb(s, "below_x", [P, TT * D + D + P])
                hot = sb(s, "onehot", [NBUCKET + 1, 640])
                rb = sb(s, "rel_bias_rows", [NBUCKET + 1, 8])
                brow = sb(s, "bias_rows", [8, 640])
            with ExitStack() as s:
                mq = [sb(s, f"mla_{n}", [P, 3, T], F32R) for n in ("q_hi", "q_lo", "k_hi", "k_lo")]
                cqh = sb(s, "cq_hi", [P, KQ, T], F32R)
                cql = sb(s, "cq_lo", [P, KQ, T], F32R)
                ckh = sb(s, "ckv_hi", [P, KKV, T], F32R)
                ckl = sb(s, "ckv_lo", [P, KKV, T], F32R)
                cs = sb(s, "cos_sin", [P, 2, T])
                cmask = sb(s, "causal", [P, T])
                r_q = sb(s, "r_q", [P, T])
                r_kv = sb(s, "r_kv", [P, T])
                rt = sb(s, "rope_tmp", [P, 2, T])
            with ExitStack() as s:
                oBh = sb(s, "oB_hi", [P, 4, T], F32R)
                oBl = sb(s, "oB_lo", [P, 4, T], F32R)
                bias = sb(s, "bias", [P, 2, T])
                sb(s, "below_moba_qk", [P, 2, T])
                bq = [sb(s, f"moba_{n}", [P, 2, T], F32R) for n in ("q_hi", "q_lo", "k_hi", "k_lo")]
        with ExitStack() as s:
            hidh = sb(s, "hidden_hi", [P, KF, T], F32R)
            hidl = sb(s, "hidden_lo", [P, KF, T], F32R)
            gs = sb(s, "gate", [P, 3, T])
            us = sb(s, "up", [P, 3, T])
        with ExitStack() as s:
            ot = sb(s, "out_tiles", [P, KD, T])
        with ExitStack() as s:
            sv = [sb(s, f"sb_{n}", [P, 2, TT, 192], F32R) for n in ("v_hi", "v_lo")]
            soh = sb(s, "so_hi", [P, KD, T], F32R)
            sol = sb(s, "so_lo", [P, KD, T], F32R)
            sq = [sb(s, f"sb_{n}", [P, 2, T], F32R) for n in ("q_hi", "q_lo", "k_hi", "k_lo")]
            lsp = sb(s, "softplus", [P, CW])
            nsh = sb(s, "nsp_hi", [P, CW], F32R)
            nsl = sb(s, "nsp_lo", [P, CW], F32R)
            wf = sb(s, "stick", [P, CW])
            swh = sb(s, "stick_hi", [P, 2, CW], F32R)
            swl = sb(s, "stick_lo", [P, 2, CW], F32R)

        ps = ctx.enter_context(nc.psum_tensor("banks", [P, 8, T], F32))

        def bank(b):
            return ps[:, b, :]

        def banks(b):
            return ps[:, b:b + 3, :].rearrange("p b n -> p (b n)")

        SC, PT, O_BANK, P_BANK = banks(0), banks(3), 6, 7
        ZB = [banks(0), banks(3)]
        oh = [oAh[:, n, :] for n in range(4)] + [oBh[:, n, :] for n in range(4)]
        ol = [oAl[:, n, :] for n in range(4)] + [oBl[:, n, :] for n in range(4)]

        raw_in = [sem(f"raw_in{n}") for n in range(NSLOT)]
        ukv_in = [sem(f"ukv_in{n}") for n in range(2)]
        w_hi, w_lo, w_used = sem("w_hi_done"), sem("w_lo_done"), sem("w_used")
        consts_ready = sem("consts_ready")
        tri_ready = sem("tri_ready")
        tri_r_ready = sem("tri_rounded")
        x_in = [sem(f"x_in{n}") for n in range(TT)]
        gains_in, tables_in, bias_in_sbuf = sem("gains_in"), sem("tables_in"), sem("bias_tables_in")
        gains_tr, gains_ready = sem("gains_transposed"), sem("gains_ready")
        x_tr, h_ready = sem("x_transposed"), sem("h_copied")
        uh_ready, u_ready = sem("u_hi_ready"), sem("u_ready")
        ssx_ready = sem("x_square_sums")
        st_sum, st_rms, st_rinv = sem("stat_sums"), sem("stat_rms"), sem("stat_rinv")
        st_diag, st_bc, st_r = sem("stat_diag"), sem("stat_spread"), sem("stat_r_ready")
        sq_ready, sq_added = sem("squares_ready"), sem("squares_added")
        in_scaled = sem("latent_scaled")
        lat_hi, lat_ready = sem("latent_hi"), sem("latent_ready")
        brow_mm, brow_sb, brow_out = sem("bias_rows_mm"), sem("bias_rows_sbuf"), sem("bias_rows_dram")
        bias_in = [sem(f"bias_in{n}") for n in range(2)]
        pj_mm, pj_read, pj_hi, pj_lo = sem("proj_product"), sem("proj_bank_read"), sem("proj_hi"), sem("proj_lo")
        rp_sw, rp_cos, rp_sin, rp_done = sem("rope_swapped"), sem("rope_cos"), sem("rope_sin"), sem("rope_done")
        kr_hi, kr_lo = sem("k_rope_hi"), sem("k_rope_lo")
        sc_done, sc_read, mx_neg = sem("scores_done"), sem("scores_read"), sem("max_negated")
        e_done, den_inv, p_done = sem("exp_done"), sem("den_inverted"), sem("probs_done")
        pt_done, pt_hi, pt_lo = sem("probsT_done"), sem("probsT_hi_done"), sem("probsT_lo_done")
        pv_done, o_hi, o_lo = sem("pv_done"), sem("o_hi_done"), sem("o_lo_done")
        f_read = sem("f_read")
        res_t, res_h = sem("branch_scaled"), sem("residual_added")
        gu_read = sem("gate_up_read")
        silu_done, act_mul = sem("silu_done"), sem("hidden_done")
        hid_hi, hid_lo = sem("hidden_hi_done"), sem("hidden_lo_done")
        v0_ready, v1_ready = sem("v_pad_ready"), sem("v1_pad_ready")
        qj_mm, qj_read, qj_hi, qj_lo = sem("sb_product"), sem("sb_bank_read"), sem("sb_hi"), sem("sb_lo")
        z_done, z_min, z_exp, z_ln = sem("z_done"), sem("z_clamped"), sem("z_exp"), sem("z_ln")
        ns_f, ns_hi, ns_lo = sem("softplus_ready"), sem("softplus_hi"), sem("softplus_lo")
        c_done, w_exp, sw_hi, sw_lo = sem("stick_sums"), sem("stick_exp"), sem("stick_hi"), sem("stick_lo")
        sv_done, so_hi_s, so_lo_s = sem("sb_pv_done"), sem("sb_o_hi"), sem("sb_o_lo")
        y_tr, y_sb, y_out = sem("y_transposed"), sem("y_sbuf"), sem("y_out")


        def load(sp, c, src, kt, cols, stride=None):
            if c.c0 >= NSLOT:
                sp.wait_ge(w_lo, c.n - NSLOT + 1)
            stride = stride or cols
            dst = raw[:, c.slot, 0:kt * stride].rearrange("p (k n) -> p k n", k=kt)[:, :, 0:cols]
            sp.dma_start(dst, src.rearrange("(k p) n -> p k n", p=P)).then_inc(raw_in[c.slot], 16)

        def ukv(c):
            p, j = (c - CH_MLA) // 2, (c - CH_MLA) % 2
            return (ukv_in[p % 2], 48 * (p // 2 + 1)) if 0 <= p < MLA_PAIRS and j == 1 else None

        def width(c):
            if CH_MLA <= c < CH_MOBA:
                return (KQ * 2 * MLA_QH, KKV * 2 * P)[(c - CH_MLA) % 2]
            for ch in (CH_DN0, CH_DN1):
                if ch <= c < ch + 3 * KD:
                    return DN_PARTS[(c - ch) % 3][1] * P
            return KD * P

        def split_hi(act, c, also=None):
            if c.c0 >= CH_END:
                return
            if also:
                act.wait_ge(*also)
            act.wait_ge(raw_in[c.slot], 16 * (c.turn + 1))
            if c.c0 >= NSLOT:
                act.wait_ge(w_used, c.n - NSLOT + 1)
            w = width(c.c0)
            act.activation(wh[:, c.slot, 0:w], raw[:, c.slot, 0:w], ACT.Copy).then_inc(w_hi, 1)

        def split_lo(dve, c):
            if c.c0 >= CH_END:
                return
            dve.wait_ge(w_hi, c.n + 1)
            w = width(c.c0)
            dve.tensor_tensor(wl[:, c.slot, 0:w], raw[:, c.slot, 0:w], wh[:, c.slot, 0:w].bitcast(F32),
                              ALU.subtract).then_inc(w_lo, 1)

        def mm3(o, lh, ll, rh, rl, start, stop):
            nc.tensor.matmul(o, lh, rh, start=start, stop=False, skip_group_check=True)
            nc.tensor.matmul(o, lh, rl, start=False, stop=False, skip_group_check=True)
            return nc.tensor.matmul(o, ll, rh, start=False, stop=stop, skip_group_check=True)

        def project(pe, o, c, kt, stride, at, m, xh, xl, first=0, total=None, x_ready=None):
            total = total or kt
            for k in range(kt):
                if x_ready:
                    pe.wait_ge(x_ready[0], x_ready[1] + k + 1)
                s = slice(k * stride + at, k * stride + at + m)
                last = mm3(o, wh[:, c.slot, s], wl[:, c.slot, s], xh[:, first + k, :], xl[:, first + k, :],
                           start=(first + k == 0), stop=(first + k == total - 1))
            return last

        def stat_pe(pe, k, b, adds=None):
            if adds is not None:
                pe.wait_ge(sq_added, adds)
                for t in range(TT):
                    last = nc.tensor.matmul(bank(b)[:, t:t + 1], acc[:, t * P:(t + 1) * P], ones[:, 0:1],
                                            start=True, stop=True)
                last.then_inc(st_sum, 1)

        def stat_pe_spread(pe, k, b):
            pe.wait_ge(st_diag, k + 1)
            nc.tensor.matmul(bank(b), ones[:, :], diag[:, :, :].rearrange("p t n -> p (t n)"),
                             start=True, stop=True).then_inc(st_bc, 1)

        def stat_act(act, k, src, width):
            if src is None:
                act.wait_ge(ssx_ready, TT)
                src = ssx[:, :]
            else:
                act.wait_ge(st_sum, k)
            act.activation(rms[:, :], src, ACT.Sqrt, bias=eps_t[:, 0:1], scale=1.0 / width).then_inc(st_rms, 1)

        def stat_dve(dve, k, b, dst):
            dve.wait_ge(st_rms, k + 1)
            nc.vector.reciprocal(rinv[:, :], rms[:, :]).then_inc(st_rinv, 1)
            dve.wait_ge(st_rinv, k + 1)
            if k:
                dve.wait_ge(st_bc, k)
            for t in range(TT):
                last = nc.vector.tensor_scalar(diag[:, t, :], ident[:, :], rinv[:, t:t + 1], None, ALU.mult)
            last.then_inc(st_diag, 1)
            dve.wait_ge(st_bc, k + 1)
            nc.vector.tensor_copy(dst[:, :], bank(b)).then_inc(st_r, 1)

        def square(act, src, n, k):
            if n == 0:
                if k > 1:
                    act.wait_ge(st_sum, k - 1)
                act.activation(acc[:, :], src, ACT.Square).then_inc(sq_ready, 1)
            else:
                if AD0[k] + n > 1:
                    act.wait_ge(sq_added, AD0[k] + n - 1)
                act.activation(sqt[:, :], src, ACT.Square).then_inc(sq_ready, 1)

        def add_squares(pool, n, k):
            pool.wait_ge(sq_ready, SQ0[k] + n + 1)
            if n > 1:
                pool.wait_ge(sq_added, AD0[k] + n - 1)
            nc.gpsimd.tensor_tensor(acc[:, :], acc[:, :], sqt[:, :], ALU.add).then_inc(sq_added, 1)

        N_X, N_CQ, N_CKV, N_POST_A0, N_FFN0, N_POST_F0, N_SB, N_POST_A1, N_FFN1, N_POST_F1 = range(10)
        tiles_of = [0, KQ, KKV] + [KD] * 7
        posts = (N_POST_A0, N_POST_F0, N_POST_A1, N_POST_F1)
        SQ0 = [sum(t for j, t in enumerate(tiles_of[:k]) if j not in posts) for k in range(10)]
        AD0 = [sum(t - 1 for t in tiles_of[1:k]) for k in range(11)]

        def f_pe(pe, chunks, fn, n, operands, f0, b):
            if not (f0 == 0 and n is not None and isinstance(n, int) and n < 2):
                pe.wait_ge(f_read, fn * KD + n - 1)
            at = 0
            total = sum(kt for _, kt in chunks)
            for c, kt in chunks:
                pe.wait_ge(w_lo, c.n + 1)
                for k in range(kt):
                    s = slice(k * P, (k + 1) * P)
                    xh, xl = operands(pe, at)
                    last = mm3(bank(b), wh[:, c.slot, s], wl[:, c.slot, s], xh, xl,
                               start=(at == 0), stop=(at == total - 1))
                    at += 1
                last.then_inc(w_used, 1)

        def f_act(act, last_chunk, b, n, first, k):
            act.wait_ge(w_used, last_chunk.n + 1)
            act.activation(F[:, n, :] if isinstance(n, int) else F[:, bass.ds(n, 1), :], bank(b), ACT.Copy)
            if first:
                act.wait_ge(st_sum, k - 1)
                act.activation(acc[:, :], bank(b), ACT.Square).then_inc(f_read, 1)
            else:
                act.wait_ge(sq_added, AD0[k] + n - 1)
                act.activation(sqt[:, :], bank(b), ACT.Square).then_inc(f_read, 1)

        def f_pool(pool, fn, n, k):
            pool.wait_ge(f_read, fn * KD + n + 1)
            if isinstance(n, int) and n == 1:
                pass
            else:
                pool.wait_ge(sq_added, AD0[k] + n - 1)
            nc.gpsimd.tensor_tensor(acc[:, :], acc[:, :], sqt[:, :], ALU.add).then_inc(sq_added, 1)

        def out_sp(sp, ch, w):
            for n in range(KD):
                load(sp, Chunk(ch + n), w[:, n * P:(n + 1) * P], KD, P)

        OUT_BANK = (7, 0, 1, 2, 6, 7, 0, 1)

        def out_part(pe, ch, n, o_at, k0, k1):
            c = Chunk(ch + n)
            if k0 == 0:
                pe.wait_ge(w_lo, c.n + 1)
            for k in range(k0, k1):
                s = slice(k * P, (k + 1) * P)
                last = mm3(bank(OUT_BANK[n]), wh[:, c.slot, s], wl[:, c.slot, s], *o_at(k),
                           start=(k == 0), stop=(k == KD - 1))
            if k1 == KD:
                last.then_inc(w_used, 1)

        def out_pe(pe, ch, fn, o_at, o_ready, begun):
            pe.wait_ge(*o_ready)
            for n in range(KD):
                if n >= 5:
                    pe.wait_ge(f_read, fn * KD + n - 4)
                out_part(pe, ch, n, o_at, begun[n] if n < len(begun) else 0, KD)

        def out_act(act, ch, k):
            for n in range(KD):
                if n:
                    split_hi(act, Chunk(ch + n + AHEAD))
                f_act(act, Chunk(ch + n), OUT_BANK[n], n, n == 0, k)

        def out_dve(dve, ch):
            for n in range(1, KD):
                split_lo(dve, Chunk(ch + n + AHEAD))

        def f_adds(pool, fn, k):
            for n in range(1, KD):
                f_pool(pool, fn, n, k)

        def res_sp(sp):
            pass

        def res_dve_branch(dve, r, n, g_post):
            if n >= 2:
                dve.wait_ge(res_h, KD * r + n - 1)
            nc.vector.scalar_tensor_tensor(tf[:, n % 2, :], F[:, n, :], gains[:, g_post + n:g_post + n + 1],
                                           r_post[:, :], ALU.mult, ALU.mult).then_inc(res_t, 1)

        def res_dve(dve, r, k, g_post, g_pre):
            stat_dve(dve, k, 0, r_post)
            dve.wait_ge(st_r, k + 1)
            for n in range(KD + 1):
                if n < KD:
                    res_dve_branch(dve, r, n, g_post)
                if n and g_pre is not None:
                    m = n - 1
                    dve.wait_ge(uh_ready, KD * (r + 1) + m + 1)
                    nc.vector.scalar_tensor_tensor(ul[:, m, :], hT[:, m, :], gains[:, g_pre + m:g_pre + m + 1],
                                                   uh[:, m, :].bitcast(F32), ALU.mult, ALU.subtract)\
                        .then_inc(u_ready, 1)

        def res_act(act, r, k, g_pre):
            for n in range(KD):
                act.wait_ge(res_h, KD * r + n + 1)
                act.activation(uh[:, n, :], hT[:, n, :], ACT.Copy, scale=gains[:, g_pre + n:g_pre + n + 1])\
                    .then_inc(uh_ready, 1)
                square(act, hT[:, n, :], n, k + 1)

        def res_pool(pool, r, k, more):
            for n in range(KD):
                pool.wait_ge(res_t, KD * r + n + 1)
                nc.gpsimd.tensor_tensor(hT[:, n, :], hT[:, n, :], tf[:, n % 2, :], ALU.add).then_inc(res_h, 1)
                if more and n > 1:
                    add_squares(pool, n - 1, k + 1)
            if more:
                add_squares(pool, KD - 1, k + 1)

        def gu_chunk(ch, n0, i=0):
            return Chunk(ch + 2 * n0, i, 6)

        def gu_sp(sp, ch, w):
            def tile(n0, i):
                c = gu_chunk(ch, n0, i)
                for half in range(2):
                    at = half * FF + n0 * P
                    src = w[:, at:at + P] if isinstance(i, int) and i == 0 else w[:, bass.ds(i * (3 * P) + at, P)]
                    load(sp, c.later(half), src, KD, P)
            tile(0, 0)
            with sp.Fori(0, (KF - 1) // 3) as i:
                for b in range(1, 4):
                    tile(b, i)

        def gu_pe(pe, ch, l, k):
            def tile(n0, i, k_outer=False):
                c, b = gu_chunk(ch, n0, i), 2 * (n0 % 3)
                for half in range(2):
                    cc = c.later(half)
                    pe.wait_ge(w_lo, cc.n + 1)
                    if n0 or not isinstance(i, int):
                        if n0 == 3 or not isinstance(i, int):
                            pe.wait_ge(gu_read, base_wait(l, n0, i, half))
                    project(pe, bank(b + half), cc, KD, P, 0, P, uh, ul,
                            x_ready=(u_ready, KD * (2 * l + 1)) if n0 == 0 else None).then_inc(w_used, 1)

            def base_wait(l, n0, i, half):
                return 2 * KF * l + 2 * (n0 - 3) + half + 1 + i * 6

            tile(0, 0)
            stat_pe(pe, k, 6, AD0[k + 1])
            stat_pe_spread(pe, k, 6)
            for n0 in (1, 2, 3):
                tile(n0, 0)
            with pe.Fori(1, (KF - 1) // 3) as i:
                for b in range(1, 4):
                    tile(b, i)

        def gu_act(act, ch, l, k):
            def hi(n0, i):
                act.wait_ge(act_mul, KF * l + n0 + i * 3 + 1)
                o = hidh[:, n0, :] if isinstance(i, int) else hidh[:, bass.ds(i * 3 + n0, 1), :]
                act.activation(o, us[:, n0 % 3, :], ACT.Copy).then_inc(hid_hi, 1)

            def tile(n0, i, first=False):
                c = gu_chunk(ch, n0, i)
                split_hi(act, c.later(AHEAD))
                split_hi(act, c.later(AHEAD + 1))
                if first:
                    stat_act(act, k, bank(6)[:, 0:TT], D)
                else:
                    hi(n0 - 1, i)
                act.wait_ge(gu_read, 2 * KF * l + 2 * n0 + i * 6 + 1)
                act.activation(gs[:, n0 % 3, :], gs[:, n0 % 3, :], ACT.Silu).then_inc(silu_done, 1)

            tile(0, 0, True)
            with act.Fori(0, (KF - 1) // 3) as i:
                for b in range(1, 4):
                    tile(b, i)
            hi(KF - 1, 0)

        def gu_pool(pool, l):
            def tile(n0, i):
                pool.wait_ge(silu_done, KF * l + n0 + i * 3 + 1)
                pool.wait_ge(gu_read, 2 * KF * l + 2 * n0 + i * 6 + 2)
                nc.gpsimd.tensor_tensor(us[:, n0 % 3, :], us[:, n0 % 3, :], gs[:, n0 % 3, :], ALU.mult)\
                    .then_inc(act_mul, 1)
            tile(0, 0)
            with pool.Fori(0, (KF - 1) // 3) as i:
                for b in range(1, 4):
                    tile(b, i)

        def gu_dve(dve, ch, l, k):
            def lo(n0, i):
                dve.wait_ge(hid_hi, KF * l + n0 + i * 3 + 1)
                o = hidl[:, n0, :] if isinstance(i, int) else hidl[:, bass.ds(i * 3 + n0, 1), :]
                h = hidh[:, n0, :] if isinstance(i, int) else hidh[:, bass.ds(i * 3 + n0, 1), :]
                nc.vector.tensor_tensor(o, us[:, n0 % 3, :], h.bitcast(F32), ALU.subtract).then_inc(hid_lo, 1)

            def tile(n0, i, first=False):
                c, b = gu_chunk(ch, n0, i), n0 % 3
                split_lo(dve, c.later(AHEAD))
                if first:
                    split_lo(dve, c.later(AHEAD + 1))
                    stat_dve(dve, k, 6, r_pre)
                    dve.wait_ge(st_r, k + 1)
                dve.wait_ge(w_used, c.n + 1)
                nc.vector.tensor_tensor(gs[:, b, :], bank(2 * b), r_pre[:, :], ALU.mult).then_inc(gu_read, 1)
                if not first:
                    split_lo(dve, c.later(AHEAD + 1))
                dve.wait_ge(w_used, c.n + 2)
                nc.vector.tensor_tensor(us[:, b, :], bank(2 * b + 1), r_pre[:, :], ALU.mult).then_inc(gu_read, 1)
                if not first:
                    lo(n0 - 1, i)

            tile(0, 0, True)
            with dve.Fori(0, (KF - 1) // 3) as i:
                for b in range(1, 4):
                    tile(b, i)
            lo(KF - 1, 0)

        def dn_chunks(ch, n0, i=0):
            return [(Chunk(ch + 3 * n0 + j, i, 6), kt) for j, (_, kt) in enumerate(DN_PARTS)]

        DN_TURNS = (KD - 2) // 2

        def dn_sp(sp, ch, w):
            def tile(n0, i):
                for (c, kt), (k0, _) in zip(dn_chunks(ch, n0, i), DN_PARTS):
                    rows = w[k0 * P:(k0 + kt) * P, :]
                    src = rows[:, n0 * P:(n0 + 1) * P] if isinstance(i, int) else rows[:, bass.ds(i * (2 * P) + n0 * P, P)]
                    load(sp, c, src, kt, P)
            with sp.Fori(0, DN_TURNS) as i:
                tile(0, i)
                tile(1, i)
            tile(KD - 2, 0)
            tile(KD - 1, 0)

        def dn_pe(pe, ch, fn, l):
            def operands(ready):
                def at(pe, k):
                    if ready:
                        pe.wait_ge(hid_lo, KF * l + k + 1)
                    return hidh[:, k, :], hidl[:, k, :]
                return at

            def tile(n0, i, first=False):
                f_pe(pe, dn_chunks(ch, n0, i), fn, n0 + i * 2, operands(first), 1, 6 + n0 % 2)
            tile(0, 0, True)
            tile(1, 0)
            with pe.Fori(1, DN_TURNS) as i:
                tile(0, i)
                tile(1, i)
            tile(KD - 2, 0)
            tile(KD - 1, 0)

        def dn_act(act, ch, k):
            def tile(n0, i, first=False):
                c = Chunk(ch + 3 * n0, i, 6)
                for j in range(3):
                    split_hi(act, c.later(AHEAD + j))
                f_act(act, c.later(2), 6 + n0 % 2, n0 + i * 2, first, k)
            tile(0, 0, True)
            tile(1, 0)
            with act.Fori(1, DN_TURNS) as i:
                tile(0, i)
                tile(1, i)
            tile(KD - 2, 0)
            tile(KD - 1, 0)

        def dn_dve(dve, ch):
            def tile(n0, i):
                c = Chunk(ch + 3 * n0, i, 6)
                for j in range(3):
                    split_lo(dve, c.later(AHEAD + j))
            with dve.Fori(0, DN_TURNS) as i:
                tile(0, i)
                tile(1, i)
            tile(KD - 2, 0)
            tile(KD - 1, 0)

        IN_TILES = [(0, P), (P, P), (2 * P, P), (O1, P), (O1 + P, P), (O2 - HD, MLA_QH)]
        lat_gain = [G_Q, G_Q + 1, G_Q + 2, G_KV, G_KV + 1]
        lat_dst = [(cqh, cql, 0), (cqh, cql, 1), (cqh, cql, 2), (ckh, ckl, 0), (ckh, ckl, 1)]
        lat_norm = [(N_CQ, 0), (N_CQ, 1), (N_CQ, 2), (N_CKV, 0), (N_CKV, 1)]

        def rope_dve(dve, n):
            pass

        ROPE_ROWS = slice(HD, HD + ROPE)

        def rope_rows_dve(dve, b, number, scaled):
            dve.wait_ge(*scaled)
            nc.vector.stream_shuffle(rt[ROPE_ROWS, 0, :], tf[ROPE_ROWS, b, :],
                                     [(j + ROPE // 2) % ROPE for j in range(ROPE)]).then_inc(rp_sw, 1)
            dve.wait_ge(rp_sw, number + 1)
            nc.vector.tensor_tensor(rt[ROPE_ROWS, 0, :], rt[ROPE_ROWS, 0, :], cs[ROPE_ROWS, 1, :], ALU.mult)\
                .then_inc(rp_sin, 1)
            dve.wait_ge(rp_sin, number + 1)
            dve.wait_ge(rp_cos, number + 1)
            nc.vector.tensor_tensor(tf[ROPE_ROWS, b, :], rt[ROPE_ROWS, 0, :], rt[ROPE_ROWS, 1, :], ALU.add)\
                .then_inc(rp_done, 1)

        def rope_rows_pool(pool, b, number, scaled):
            pool.wait_ge(*scaled)
            if number:
                pool.wait_ge(rp_done, number)
            nc.gpsimd.tensor_tensor(rt[ROPE_ROWS, 1, :], tf[ROPE_ROWS, b, :], cs[ROPE_ROWS, 0, :], ALU.mult)\
                .then_inc(rp_cos, 1)

        def item_done(eng, it):
            if it[5]:
                eng.wait_ge(w_used, it[3] + 1)
            else:
                eng.wait_ge(pj_mm, inner_order[it[:3]] + 1)

        def head_of(it):
            return 2 * it[1] + it[2]

        def item_pe(pe, it):
            if it is None:
                return
            kind, p, e, c, first, last = it
            n = order[it[:3]]
            c = Chunk(c) if c is not None else None
            if n:
                pe.wait_ge(pj_read, n)
            if first:
                pe.wait_ge(w_lo, c.n + 1)
            b = bank(P_BANK)
            if kind == "mq":
                mm = project(pe, b[0:MLA_QH, :], c, KQ, 2 * MLA_QH, e * MLA_QH, MLA_QH, cqh, cql)
            elif kind == "mk":
                mm = project(pe, b[0:HD, :], c, KKV, P, e * HD, HD, ckh, ckl)
            elif kind == "mv":
                mm = project(pe, b, c, KKV, P, KKV * P, P, ckh, ckl)
            elif kind == "vt":
                tb = n_tf(it) % 2
                for t in range(TT):
                    mm = nc.tensor.transpose(b[:, t * P:(t + 1) * P], tf[:, tb, t * P:(t + 1) * P], ident[:, :])
            else:
                mm = project(pe, b, c, KD, P, 0, P, uh, ul)
            mm.then_inc(w_used if last else pj_mm, 1)

        split_at = {}
        for n, it in enumerate(items):
            ended = items[n - 1][3] if n and items[n - 1][5] else CH_MLA - 1 if n == 0 else None
            ahead = ended + NSLOT if ended is not None else None
            split_at[it[:3]] = ahead if ahead is not None and ahead < CH_OUT0 + AHEAD else None

        tf_of = {}
        for it in items:
            if it[0] != "vt":
                tf_of[it[:3]] = len(tf_of) + KQ + KKV + 1

        def n_tf(it):
            if it[0] == "vt":
                return tf_of[("mv" if it[1] < MLA_PAIRS else "bv", it[1], 0)]
            return tf_of[it[:3]]

        def v_views(v, buf):
            return v[:, buf, :, 0:HD], v[:, buf, :, 2 * HD:3 * HD]

        def qk_dst(it):
            kind, p, e = it[:3]
            if kind[0] == "m":
                j = 0 if kind == "mq" else 2
                rows = slice(0, MLA_QH) if kind == "mq" else slice(0, HD)
                return [mq[j + a][rows, head_of(it) % 3, :] for a in range(2)], rows
            j = 0 if kind == "bq" else 2
            return [bq[j + a][:, p % 2, :] for a in range(2)], slice(0, P)

        def buffer_free(eng, it):
            kind, p, e = it[:3]
            if kind[0] == "m":
                h = head_of(it)
                if h >= 3 and kind in ("mq", "mk"):
                    eng.wait_ge(sc_done, 3 * (h - 2))
            elif kind in ("bq", "bk"):
                eng.wait_ge(sc_done, 3 * 2 * max(p - 1, MLA_PAIRS))
            if kind == "vt" and p >= 2:
                eng.wait_ge(pv_done, 2 * (p - 1))

        def item_split_act(act, it):
            if split_at[it[:3]] is not None:
                split_hi(act, Chunk(split_at[it[:3]]), ukv(split_at[it[:3]]))

        def item_split_dve(dve, it):
            if split_at[it[:3]] is not None:
                split_lo(dve, Chunk(split_at[it[:3]]))

        def item_act(act, it):
            if it is None:
                return
            kind, p, e, c, first, last = it
            if kind in ("mv", "bv"):
                item_split_act(act, it)
                return
            buffer_free(act, it)
            if kind == "vt":
                item_done(act, it)
                if p == 0:
                    act.wait_ge(v0_ready, 1)
                src = bank(P_BANK).rearrange("p (t h n) -> p t h n", t=TT, h=2)
                a, b = v_views(vh, p % 2)
                act.activation(a, src[:, :, 0, :], ACT.Copy)
                act.activation(b, src[:, :, 1, :], ACT.Copy).then_inc(pj_hi, 1)
                item_split_act(act, it)
                return
            (hi, _), rows = qk_dst(it)
            if kind == "mq":
                act.wait_ge(rp_done, head_of(it) + 2)
            else:
                act.wait_ge(pj_read, order[it[:3]] + 1)
            act.activation(hi, tf[rows, n_tf(it) % 2, :], ACT.Copy).then_inc(pj_hi, 1)
            item_split_act(act, it)

        def item_scale(dve, it):
            if it is None or it[0] == "vt":
                return
            kind, p, e, c, first, last = it
            n = order[it[:3]]
            tb = n_tf(it) % 2
            item_done(dve, it)
            if kind[0] == "m":
                rows = slice(0, {"mq": MLA_QH, "mk": HD, "mv": P}[kind])
                r = r_q if kind == "mq" else r_kv
                scale = MLA_SCALE if kind == "mq" else 1.0
            else:
                rows, r, scale = slice(0, P), r_pre, SCALE if kind == "bq" else 1.0
            vt_before = [i for i in items[:n] if i[0] == "vt"]
            if vt_before:
                dve.wait_ge(pj_mm, inner_order[vt_before[-1][:3]] + 1)
            for i in items[:n]:
                if i[0] != "vt" and tf_of[i[:3]] == tf_of[it[:3]] - 2 and i[:3] in lo_order:
                    dve.wait_ge(pj_lo, lo_order[i[:3]] + 1)
            nc.vector.scalar_tensor_tensor(tf[rows, tb, :], bank(P_BANK)[rows, :], scale, r[rows, :],
                                           ALU.mult, ALU.mult).then_inc(pj_read, 1)
            if kind == "mq":
                rope_rows_dve(dve, tb, head_of(it) + 1, (pj_read, n + 1))

        def item_lo(dve, it):
            if it is None:
                return
            kind, p, e, c, first, last = it
            if kind in ("mv", "bv"):
                item_split_dve(dve, it)
                return
            dve.wait_ge(pj_hi, split_order[it[:3]] + 1)
            if kind == "vt":
                src = bank(P_BANK).rearrange("p (t h n) -> p t h n", t=TT, h=2)
                for x in range(2):
                    ins = nc.vector.tensor_tensor(v_views(vl, p % 2)[x], src[:, :, x, :],
                                                  v_views(vh, p % 2)[x].bitcast(F32), ALU.subtract)
                ins.then_inc(pj_read, 1)
                item_split_dve(dve, it)
                return
            (hi, lo), rows = qk_dst(it)
            nc.vector.tensor_tensor(lo, tf[rows, n_tf(it) % 2, :], hi.bitcast(F32), ALU.subtract).then_inc(pj_lo, 1)
            item_split_dve(dve, it)

        def item_pool(pool, it):
            if it is not None and it[0] == "mq":
                rope_rows_pool(pool, n_tf(it) % 2, head_of(it) + 1, (pj_read, order[it[:3]] + 1))

        lo_order = {}
        for it in items:
            if it[0] in ("mq", "mk", "bq", "bk"):
                lo_order[it[:3]] = len(lo_order)

        def scores_pe(pe, hh):
            p, e = hh // 2, hh % 2
            pe.wait_ge(pj_lo, 1 + max(lo_order[("mk", p, e)], lo_order[("mq", p, e)]) if p < MLA_PAIRS
                       else 1 + lo_order[("bk", p, 0)])
            if hh == 0:
                pe.wait_ge(kr_lo, 1)
            if hh:
                pe.wait_ge(sc_read, hh)
            if p < MLA_PAIRS:
                rows, b, (qh, ql, kh, kl) = slice(0, MLA_QH), hh % 3, mq
            else:
                rows, b, (qh, ql, kh, kl) = slice(HD * e, HD * e + HD), p % 2, bq
            for i in (3, 1, 2, 0):
                w, at, q = P * (i + 1), ROW_AT[i], slice(i * P, (i + 1) * P)
                mm = mm3(SC[:, at:at + w], qh[rows, b, q], ql[rows, b, q], kh[rows, b, 0:w], kl[rows, b, 0:w],
                         start=(i != 0), stop=True)
                if i != 2:
                    mm.then_inc(sc_done, 1)

        def scores_dve(dve, hh):
            b = hh % 2
            if hh >= 2:
                dve.wait_ge(pt_done, hh - 1)
            if hh < 2 * MLA_PAIRS:
                add = cmask[:, :]
                if hh == 0:
                    dve.wait_ge(v0_ready, 2)
            else:
                m = hh - 2 * MLA_PAIRS
                dve.wait_ge(bias_in[m % 2], 16 * (m // 2 + 1))
                add = bias[:, m % 2, :]
            for x, i in enumerate((3, 1, 2, 0)):
                w, at = P * (i + 1), ROW_AT[i]
                if x < 3:
                    dve.wait_ge(sc_done, 3 * hh + x + 1)
                ins = nc.vector.tensor_tensor_reduce(logits[:, b, at:at + w], SC[:, at:at + w], add[:, T - w:T], 1.0,
                                                     -3.0e38, ALU.add, ALU.max, mx[:, b, i:i + 1])
            ins.then_inc(sc_read, 1)
            dve.wait_ge(sc_read, hh + 1)
            nc.vector.tensor_scalar(nmx[:, b, :], mx[:, b, :], -1.0, None, ALU.mult).then_inc(mx_neg, 1)

        def exp_act(act, hh):
            b = hh % 2
            act.wait_ge(mx_neg, hh + 1)
            for i in (3, 1, 2, 0):
                w, at = P * (i + 1), ROW_AT[i]
                ins = act.activation(logits[:, b, at:at + w], logits[:, b, at:at + w], ACT.Exp,
                                     bias=nmx[:, b, i:i + 1], accum_out=den[:, b, i:i + 1])
            ins.then_inc(e_done, 1)

        def den_dve(dve, hh):
            dve.wait_ge(e_done, hh + 1)
            nc.vector.reciprocal(rden[:, hh % 2, :], den[:, hh % 2, :]).then_inc(den_inv, 1)

        def norm_act(act, hh):
            b = hh % 2
            act.wait_ge(den_inv, hh + 1)
            for i in (3, 1, 2, 0):
                w, at = P * (i + 1), ROW_AT[i]
                ins = act.activation(logits[:, b, at:at + w], logits[:, b, at:at + w], ACT.Copy,
                                     scale=rden[:, b, i:i + 1])
            ins.then_inc(p_done, 1)

        def probs_pe(pe, hh):
            pe.wait_ge(p_done, hh + 1)
            if hh:
                pe.wait_ge(pt_lo, hh)
            for j in range(TT):
                for i in range(j, TT):
                    mm = nc.tensor.transpose(PT[:, COL_AT[j] + (i - j) * P:COL_AT[j] + (i - j + 1) * P],
                                             logits[:, hh % 2, ROW_AT[i] + j * P:ROW_AT[i] + (j + 1) * P], ident[:, :])
            mm.then_inc(pt_done, 1)

        def probs_act(act, hh):
            act.wait_ge(pt_done, hh + 1)
            if hh:
                act.wait_ge(pv_done, hh)
            act.activation(pth[:, :], PT[:, 0:CW], ACT.Copy).then_inc(pt_hi, 1)

        def probs_dve(dve, hh):
            dve.wait_ge(pt_hi, hh + 1)
            nc.vector.tensor_tensor(ptl[:, :], PT[:, 0:CW], pth[:, :].bitcast(F32), ALU.subtract)\
                .then_inc(pt_lo, 1)

        def values(out_bank, v, buf, e, xh, xl, at0):
            for j in range(TT):
                w, at, cols = T - P * j, COL_AT[j] + at0, slice(HD * e, HD * e + P)
                mm = mm3(out_bank[:, P * j:T], v[0][:, buf, j, cols], v[1][:, buf, j, cols],
                         xh[:, at:at + w], xl[:, at:at + w], start=(e == 0 and j == 0), stop=(e == 1 and j == TT - 1))
            return mm

        def pv_pe(pe, hh):
            p, e = hh // 2, hh % 2
            pe.wait_ge(pt_lo, hh + 1)
            if e == 0:
                pe.wait_ge(pj_read, order[("vt", p, 0)] + 1)
                if p:
                    pe.wait_ge(o_lo, p)
            values(bank(O_BANK), (vh, vl), p % 2, e, pth, ptl, 0).then_inc(pv_done, 1)

        def out0_at(k):
            return oh[k], ol[k]

        def o_act(act, p):
            act.wait_ge(pv_done, 2 * p + 2)
            act.activation(oh[p], bank(O_BANK), ACT.Copy).then_inc(o_hi, 1)

        def o_dve(dve, p):
            dve.wait_ge(o_hi, p + 1)
            nc.vector.tensor_tensor(ol[p], bank(O_BANK), oh[p].bitcast(F32), ALU.subtract).then_inc(o_lo, 1)

        def sb_item_pe(pe, p, par, j):
            first = isinstance(p, int) and p == 0 and j == 0
            if not first:
                pe.wait_ge(qj_read, p * 4 + j)
            if j < 3:
                c = sb_chunk(p, j)
                pe.wait_ge(w_lo, c.n + 1)
                x_ready = (u_ready, KD * 2) if first else None
                project(pe, bank(P_BANK), c, KD, P, 0, P, uh, ul, x_ready=x_ready).then_inc(w_used, 1)
            else:
                tb = tf_sb(par, 2)
                for t in range(TT):
                    mm = nc.tensor.transpose(bank(P_BANK)[:, t * P:(t + 1) * P], tf[:, tb, t * P:(t + 1) * P],
                                             ident[:, :])
                mm.then_inc(qj_mm, 1)

        def tf_sb(par, j):
            return (par * 3 + j) % 2

        def sb_chunk(p, j):
            c = Chunk(CH_SB + j)
            c.turn, c.n = c.turn + p, c.n + p * 3
            return c

        def sb_later(p, j, k):
            c = Chunk(CH_SB + j + k)
            c.turn, c.n = c.turn + p, c.n + p * 3
            return c

        def sb_split_act(act, p, j):
            split_hi(act, sb_later(p, j, AHEAD))

        def sb_split_dve(dve, p, j):
            split_lo(dve, sb_later(p, j, AHEAD))

        def sb_item_act(act, p, par, j):
            if j == 3:
                act.wait_ge(qj_mm, p + 1)
                if not isinstance(p, int) or p >= 2:
                    act.wait_ge(sv_done, 2 * p - 2)
                elif p == 0:
                    act.wait_ge(v1_ready, 1)
                src = bank(P_BANK).rearrange("p (t h n) -> p t h n", t=TT, h=2)
                a, b = v_views(sv[0], par)
                act.activation(a, src[:, :, 0, :], ACT.Copy)
                act.activation(b, src[:, :, 1, :], ACT.Copy).then_inc(qj_hi, 1)
                return
            act.wait_ge(qj_read, p * 4 + j + 1)
            if not isinstance(p, int) or p >= 2:
                act.wait_ge(z_done, 2 * p - 2)
            act.activation(sq[2 * j][:, par, :], tf[:, tf_sb(par, j), :], ACT.Copy).then_inc(qj_hi, 1)

        def sb_scale(dve, p, par, j):
            dve.wait_ge(w_used, sb_chunk(p, j).n + 1)
            if not (isinstance(p, int) and p == 0):
                dve.wait_ge(qj_mm, p)
            nc.vector.scalar_tensor_tensor(tf[:, tf_sb(par, j), :], bank(P_BANK), -SCALE if j == 0 else 1.0,
                                           r_pre[:, :], ALU.mult, ALU.mult).then_inc(qj_read, 1)

        def sb_item_dve(dve, p, par, j):
            if j < 2:
                dve.wait_ge(qj_hi, p * 3 + j + 1)
                nc.vector.tensor_tensor(sq[2 * j + 1][:, par, :], tf[:, tf_sb(par, j), :],
                                        sq[2 * j][:, par, :].bitcast(F32), ALU.subtract).then_inc(qj_lo, 1)
                return
            dve.wait_ge(qj_hi, p * 3 + 3)
            src = bank(P_BANK).rearrange("p (t h n) -> p t h n", t=TT, h=2)
            for x in range(2):
                ins = nc.vector.tensor_tensor(v_views(sv[1], par)[x], src[:, :, x, :],
                                              v_views(sv[0], par)[x].bitcast(F32), ALU.subtract)
            ins.then_inc(qj_read, 1)

        def z_pe(pe, p, par, e, first=False):
            hh = p * 2 + e
            pe.wait_ge(qj_lo, p * 2 + 2)
            if not (isinstance(p, int) and hh < 2):
                pe.wait_ge(w_exp, hh - 1)
            rows = slice(HD * e, HD * e + HD)
            Z = ZB[e]
            for j in (0, 1, 3, 2):
                w, at = T - P * j, COL_AT[j]
                k = slice(j * P, (j + 1) * P)
                mm3(Z[:, at:at + w], sq[2][rows, par, k], sq[3][rows, par, k],
                    sq[0][rows, par, P * j:T], sq[1][rows, par, P * j:T], start=(j != 3), stop=False)
                mm = nc.tensor.matmul(Z[:, at:at + P], identb[:, :], big[:, :], start=False, stop=False,
                                      skip_group_check=True)
            mm.then_inc(z_done, 1)

        def z_act_exp(act, p, e):
            hh = p * 2 + e
            act.wait_ge(z_done, hh + 1)
            if not (isinstance(p, int) and hh == 0):
                act.wait_ge(ns_lo, hh)
            act.activation(lsp[:, :], ZB[e][:, 0:CW], ACT.Exp, scale=-1.0).then_inc(z_exp, 1)

        def z_dve_clamp(dve, p, e):
            dve.wait_ge(z_exp, p * 2 + e + 1)
            nc.vector.tensor_scalar(lsp[:, :], lsp[:, :], 1e17, None, ALU.min).then_inc(z_min, 1)

        def z_act_ln(act, p, e):
            act.wait_ge(z_min, p * 2 + e + 1)
            act.activation(lsp[:, :], lsp[:, :], ACT.Ln, bias=1.0).then_inc(z_ln, 1)

        def z_dve(dve, p, e):
            hh = p * 2 + e
            dve.wait_ge(z_ln, hh + 1)
            nc.vector.scalar_tensor_tensor(lsp[:, :], lsp[:, :], -1.0, ZB[e][:, 0:CW], ALU.mult, ALU.min)\
                .then_inc(ns_f, 1)

        def ns_dve_hi(dve, p, e, first=False):
            hh = p * 2 + e
            dve.wait_ge(ns_f, hh + 1)
            if not first:
                dve.wait_ge(c_done, hh)
            nc.vector.tensor_copy(nsh[:, :], lsp[:, :]).then_inc(ns_hi, 1)

        def ns_dve_lo(dve, p, e):
            dve.wait_ge(ns_hi, p * 2 + e + 1)
            nc.vector.tensor_tensor(nsl[:, :], lsp[:, :], nsh[:, :].bitcast(F32), ALU.subtract).then_inc(ns_lo, 1)

        def c_pe(pe, p, e):
            hh = p * 2 + e
            pe.wait_ge(ns_lo, hh + 1)
            Z = ZB[e]
            for j in range(TT):
                for jj in range(j, TT):
                    at, w = COL_AT[j] + (jj - j) * P, T - P * jj
                    lt = negtri if jj == j else negones
                    for n in (nsh, nsl):
                        mm = nc.tensor.matmul(Z[:, at:at + w], lt[:, :], n[:, COL_AT[jj]:COL_AT[jj] + w],
                                              start=False, stop=False, skip_group_check=True)
            mm.then_inc(c_done, 1)

        def w_act(act, p, e, first=False):
            hh = p * 2 + e
            act.wait_ge(c_done, hh + 1)
            if not first:
                act.wait_ge(sw_lo, hh)
            act.activation(wf[:, :], ZB[e][:, 0:CW], ACT.Exp, scale=-1.0).then_inc(w_exp, 1)

        def w_dve(dve, p, e, first=False):
            hh = p * 2 + e
            dve.wait_ge(w_exp, hh + 1)
            if not first:
                dve.wait_ge(sv_done, hh - 1)
            nc.vector.tensor_copy(swh[:, e, :], wf[:, :]).then_inc(sw_hi, 1)

        def w_pool(pool, p, e):
            pool.wait_ge(sw_hi, p * 2 + e + 1)
            nc.gpsimd.tensor_tensor(swl[:, e, :], wf[:, :], swh[:, e, :].bitcast(F32), ALU.subtract)\
                .then_inc(sw_lo, 1)

        def sb_pv_pe(pe, p, par, e):
            hh = p * 2 + e
            pe.wait_ge(sw_lo, hh + 1)
            if e == 0:
                pe.wait_ge(qj_read, p * 4 + 4)
                if not (isinstance(p, int) and p == 0):
                    pe.wait_ge(so_lo_s, p)
            values(bank(O_BANK), sv, par, e, swh[:, e, :], swl[:, e, :], 0).then_inc(sv_done, 1)

        def sb_o_act(act, p):
            act.wait_ge(sv_done, p * 2 + 2)
            o = soh[:, p, :] if isinstance(p, int) else soh[:, bass.ds(p, 1), :]
            act.activation(o, bank(O_BANK), ACT.Copy).then_inc(so_hi_s, 1)

        def sb_o_dve(dve, p):
            dve.wait_ge(so_hi_s, p + 1)
            h = soh[:, p, :] if isinstance(p, int) else soh[:, bass.ds(p, 1), :]
            o = sol[:, p, :] if isinstance(p, int) else sol[:, bass.ds(p, 1), :]
            nc.vector.tensor_tensor(o, bank(O_BANK), h.bitcast(F32), ALU.subtract).then_inc(so_lo_s, 1)

        def out1_at(k):
            return soh[:, k, :], sol[:, k, :]

        def sb_pair_pe(pe, p, par, first=False, last=False):
            q = 1 - par
            if not last:
                sb_item_pe(pe, p + 1, q, 0)
            z_pe(pe, p, par, 1)
            if last:
                pe.wait_ge(qj_read, 4 * SB_PAIRS)
                out_part(pe, CH_OUT1, 0, out1_at, 0, 6)
            c_pe(pe, p, 0)
            if not last:
                sb_item_pe(pe, p + 1, q, 1)
            if not first:
                sb_pv_pe(pe, p - 1, q, 1)
            if last:
                pe.wait_ge(w_exp, 2 * SB_PAIRS - 1)
                out_part(pe, CH_OUT1, 1, out1_at, 0, 6)
            if not last:
                sb_item_pe(pe, p + 1, q, 2)
                z_pe(pe, p + 1, q, 0)
            c_pe(pe, p, 1)
            if not last:
                sb_item_pe(pe, p + 1, q, 3)
            sb_pv_pe(pe, p, par, 0)
            if last:
                out_part(pe, CH_OUT1, 2, out1_at, 0, 6)

        def sb_pair_act(act, p, par, first=False, last=False):
            q = 1 - par
            if not last:
                sb_split_act(act, p + 1, 0)
                sb_item_act(act, p + 1, q, 0)
            z_act_exp(act, p, 1)
            z_act_ln(act, p, 1)
            w_act(act, p, 0, first)
            if not last:
                sb_split_act(act, p + 1, 1)
                sb_item_act(act, p + 1, q, 1)
            if not first:
                sb_o_act(act, p - 1)
            if last:
                split_hi(act, Chunk(CH_OUT1 + AHEAD))
            if not last:
                sb_split_act(act, p + 1, 2)
                z_act_exp(act, p + 1, 0)
                z_act_ln(act, p + 1, 0)
                sb_item_act(act, p + 1, q, 3)
            w_act(act, p, 1)

        def sb_pair_dve(dve, p, par, first=False, last=False):
            q = 1 - par
            if not last:
                sb_split_dve(dve, p + 1, 0)
                sb_scale(dve, p + 1, q, 0)
                sb_item_dve(dve, p + 1, q, 0)
            z_dve_clamp(dve, p, 1)
            z_dve(dve, p, 1)
            ns_dve_hi(dve, p, 1)
            w_dve(dve, p, 0, first)
            ns_dve_lo(dve, p, 1)
            if not last:
                sb_scale(dve, p + 1, q, 1)
                sb_item_dve(dve, p + 1, q, 1)
            if not first:
                sb_o_dve(dve, p - 1)
            if last:
                split_lo(dve, Chunk(CH_OUT1 + AHEAD))
            if not last:
                sb_split_dve(dve, p + 1, 1)
                sb_split_dve(dve, p + 1, 2)
                sb_scale(dve, p + 1, q, 2)
                z_dve_clamp(dve, p + 1, 0)
                sb_item_dve(dve, p + 1, q, 3)
                z_dve(dve, p + 1, 0)
                ns_dve_hi(dve, p + 1, 0)
                ns_dve_lo(dve, p + 1, 0)
            w_dve(dve, p, 1, first)

        def sb_turns(eng, pair):
            pair(eng, 0, 0, first=True)
            with eng.Fori(0, (SB_PAIRS - 2) // 2) as i:
                pair(eng, i * 2 + 1, 1)
                pair(eng, i * 2 + 2, 0)
            pair(eng, SB_PAIRS - 1, 1, last=True)

        block = ctx.enter_context(nc.Block())

        @block.sync
        def _(sp):
            for v, (g, r0, n) in enumerate(((mix_pre_g, G_MIX_PRE, 16), (mix_post_g, G_MIX_POST, 16),
                                            (ffn_pre_g, G_FFN_PRE, 16), (ffn_post_g, G_FFN_POST, 16),
                                            (mla_q_norm_g, G_Q, KQ), (mla_kv_norm_g, G_KV, KKV))):
                sp.dma_start(graw[r0:r0 + n, :], g.rearrange("l (k p) -> (l k) p", p=P)).then_inc(gains_in, 16)
            for t in range(TT):
                sp.dma_start(xt[:, t, :], x[0, t * P:(t + 1) * P, :]).then_inc(x_in[t], 16)
            for n, (at, cols) in enumerate(IN_TILES):
                load(sp, Chunk(CH_IN + n), ab_w_in[0][:, at:at + cols], KD, cols, P)
                if n == 2:
                    sp.dma_start(hot[:, :], onehot_d).then_inc(bias_in_sbuf, 16)
                    sp.dma_start(rb[0:NBUCKET, :], rel_bias).then_inc(bias_in_sbuf, 16)
            sp.wait_ge(brow_sb, 1)
            sp.dma_start(bias_t.ap(), brow[:, :].unsqueeze(1).to_broadcast([8, P, 640])).then_inc(brow_out, 16)
            sp.wait_ge(brow_out, 16)
            sp.wait_ge(h_ready, KD)
            sp.wait_ge(ssx_ready, TT)
            sp.dma_start(cs[ROPE_ROWS, :, :], rope_d.rearrange("a r t -> r a t")).then_inc(tables_in, 16)
            for p in range(MLA_PAIRS):
                load(sp, Chunk(CH_MLA + 2 * p), mla_w_uq[0][:, 2 * p * MLA_QH:2 * (p + 1) * MLA_QH], KQ, 2 * MLA_QH)
                c = Chunk(CH_MLA + 2 * p + 1)
                sp.wait_ge(w_lo, c.n - NSLOT + 1)
                for kv in range(2):
                    for h in range(2):
                        at = (2 * p + h) * 2 * HD + kv * HD
                        dst = raw[:, c.slot, kv * KKV * P:(kv + 1) * KKV * P].rearrange("p (k h n) -> p k h n", k=KKV, h=2)
                        sp.dma_start(dst[:, :, h, :], mla_w_ukv[0][:, at:at + HD].rearrange("(k p) n -> p k n", p=P))\
                            .then_inc(ukv_in[p % 2] if 2 * kv + h < 3 else raw_in[c.slot], 16)
            for m in range(MOBA_PAIRS):
                for j in range(3):
                    load(sp, Chunk(CH_MOBA + 3 * m + j),
                         ab_w_in[0][:, O3 + 512 * j + P * m:O3 + 512 * j + P * (m + 1)], KD, P)
            out_sp(sp, CH_OUT0, ab_w_out[0])
            gu_sp(sp, CH_GU0, ffn_w_gate_up[0])
            dn_sp(sp, CH_DN0, ffn_w_down[0])
            with sp.Fori(0, SB_PAIRS) as p:
                for j in range(3):
                    load(sp, sb_chunk(p, j), sb_w_qkv[0][:, bass.ds(p * P + D * j, P)], KD, P)
            out_sp(sp, CH_OUT1, sb_w_out[0])
            gu_sp(sp, CH_GU1, ffn_w_gate_up[1])
            dn_sp(sp, CH_DN1, ffn_w_down[1])
            y = out[0].rearrange("(t p) d -> p t d", p=P)
            for n in range(KD):
                sp.wait_ge(y_sb, n + 1)
                sp.dma_start(y[:, :, n * P:(n + 1) * P], ot[:, n, :].rearrange("p (t d) -> p t d", t=TT))\
                    .then_inc(y_out, 16)
            sp.wait_ge(y_out, 16 * KD)
            sp.wait_ge(brow_out, 16)

        @block.gpsimd
        def _(pool):
            nc.gpsimd.memset(ones[:, :], 1.0).then_inc(tri_ready, 1)
            pool.wait_ge(tri_ready, 1)
            nc.gpsimd.memset(eps_t[:, :], EPS).then_inc(tri_ready, 1)
            pool.wait_ge(tri_ready, 2)
            nc.gpsimd.memset(rb[NBUCKET:NBUCKET + 1, :], NEG).then_inc(tri_ready, 1)
            pool.wait_ge(tri_ready, 3)
            nc.gpsimd.affine_select(out=ident[:, :], in_=ones[:, :], compare_op=ALU.is_equal, fill=0.0, base=0,
                                    pattern=[[-1, P]], channel_multiplier=1).then_inc(consts_ready, 1)
            nc.gpsimd.affine_select(out=tri_f[:, :], in_=ones[:, :], compare_op=ALU.is_ge, fill=0.0, base=0,
                                    pattern=[[-1, P]], channel_multiplier=1).then_inc(consts_ready, 1)
            pool.wait_ge(consts_ready, 2)
            for v in (vh, vl):
                nc.gpsimd.memset(v[:, :, :, HD:2 * HD].bitcast(F32), 0.0)
            pool.wait_ge(h_ready, KD)
            pool.wait_ge(ssx_ready, TT)
            pool.wait_ge(brow_out, 16)
            nc.gpsimd.memset(cmask[:, :], 0.0).then_inc(v0_ready, 1)
            pool.wait_ge(v0_ready, 1)
            nc.gpsimd.affine_select(out=cmask[:, :], in_=cmask[:, :], compare_op=ALU.is_ge, fill=NEG, base=T - P,
                                    pattern=[[-1, T]], channel_multiplier=1).then_inc(v0_ready, 1)
            for n in (1, 2):
                add_squares(pool, n, N_CQ)
            add_squares(pool, 1, N_CKV)
            pool.wait_ge(tables_in, 16)
            pool.wait_ge(sq_added, AD0[N_CKV + 1])
            rope_rows_pool(pool, 1, 0, (in_scaled, 6))
            for it in items[0:8]:
                item_pool(pool, it)

            def load_bias(m):
                if m >= 2:
                    pool.wait_ge(sc_read, 2 * MLA_PAIRS + m - 1)
                else:
                    pool.wait_ge(sc_done, 3 * 2 * MLA_PAIRS)
                skewed = bass.AP(tensor=bias_t, offset=640 * P * m + P - 1, ap=[[640 - 1, P], [1, T]])
                pool.dma_start(bias[:, m % 2, :], skewed)\
                    .then_inc(bias_in[m % 2], 16)

            for hh in range(NH0):
                for it in slots_of_step(hh):
                    item_pool(pool, it)
                if hh == 2 * MLA_PAIRS - 3:
                    load_bias(0)
                    load_bias(1)
                elif 2 * MLA_PAIRS - 3 < hh < NH0 - 4:
                    load_bias(hh - 2 * MLA_PAIRS + 4)
            pool.wait_ge(rp_cos, 2 * MLA_PAIRS + 1)
            f_adds(pool, 0, N_POST_A0)
            res_pool(pool, 0, N_POST_A0, True)
            gu_pool(pool, 0)
            f_adds(pool, 1, N_POST_F0)
            for v in sv:
                ins = nc.gpsimd.memset(v[:, :, :, HD:2 * HD].bitcast(F32), 0.0)
            ins.then_inc(v1_ready, 1)
            res_pool(pool, 1, N_POST_F0, True)

            def pair(pool, p, par, first=False, last=False):
                w_pool(pool, p, 0)
                w_pool(pool, p, 1)
            sb_turns(pool, pair)
            f_adds(pool, 2, N_POST_A1)
            res_pool(pool, 2, N_POST_A1, True)
            gu_pool(pool, 1)
            f_adds(pool, 3, N_POST_F1)
            res_pool(pool, 3, N_POST_F1, False)

        @block.scalar
        def _(act):
            act.wait_ge(gains_ready, 1)
            for n in range(AHEAD):
                split_hi(act, Chunk(n))
            for k in range(KD):
                act.wait_ge(h_ready, k + 1)
                act.activation(uh[:, k, :], hT[:, k, :], ACT.Copy, scale=gains[:, k:k + 1]).then_inc(uh_ready, 1)
                if k % 2:
                    t = k // 2
                    act.wait_ge(x_in[t], 16)
                    if t:
                        act.wait_ge(ssx_ready, t)
                    act.activation(junk[:, :], xt[:, t, :], ACT.Square, accum_out=ssx[:, t:t + 1]).then_inc(ssx_ready, 1)
            act.wait_ge(consts_ready, 2)
            act.activation(negtri[:, :], tri_f[:, :], ACT.Copy, scale=-1.0)
            act.activation(negones[:, :], ones[:, :], ACT.Copy, scale=-1.0)
            act.activation(identb[:, :], ident[:, :], ACT.Copy)
            act.activation(big[:, :], tri_f[:, :], ACT.Copy, scale=-NEG).then_inc(tri_r_ready, 1)
            stat_act(act, N_X, None, D)
            for n in range(len(IN_TILES)):
                split_hi(act, Chunk(CH_IN + n + AHEAD), ukv(CH_IN + n + AHEAD))
                if n == len(IN_TILES) - 1:
                    break
                hi, _, m = lat_dst[n]
                k, first = lat_norm[n]
                act.wait_ge(in_scaled, n + 1)
                if n == 0:
                    act.wait_ge(brow_out, 16)
                act.activation(hi[:, m, :], tf[:, n % 2, :], ACT.Copy,
                               scale=gains[:, lat_gain[n]:lat_gain[n] + 1]).then_inc(lat_hi, 1)
                square(act, tf[:, n % 2, :], first, k)
            act.wait_ge(rp_done, 1)
            for b in range(3):
                ins = act.activation(mq[2][ROPE_ROWS, b, :], tf[ROPE_ROWS, 1, :], ACT.Copy)
            ins.then_inc(kr_hi, 1)
            stat_act(act, N_CQ, bank(6)[:, 0:TT], QL)
            stat_act(act, N_CKV, bank(6)[:, 0:TT], KVL)
            for n, it in enumerate(items[0:8]):
                item_act(act, it)
                if n == 2:
                    exp_act(act, 0)
                if n == 3:
                    norm_act(act, 0)
                if n == 4:
                    exp_act(act, 1)
            for hh in range(NH0):
                a, b, c = slots_of_step(hh)
                if hh % 2:
                    item_act(act, a)
                probs_act(act, hh)
                if hh + 1 < NH0:
                    norm_act(act, hh + 1)
                if hh % 2 == 0:
                    item_act(act, a)
                if hh == NH0 - 2:
                    split_hi(act, Chunk(CH_OUT0 + AHEAD))
                if hh + 2 < NH0:
                    exp_act(act, hh + 2)
                item_act(act, b)
                item_act(act, c)
                if hh % 2:
                    o_act(act, hh // 2)
            out_act(act, CH_OUT0, N_POST_A0)
            stat_act(act, N_POST_A0, bank(0)[:, 0:TT], D)
            res_act(act, 0, N_POST_A0, G_FFN_PRE)
            gu_act(act, CH_GU0, 0, N_FFN0)
            dn_act(act, CH_DN0, N_POST_F0)
            stat_act(act, N_POST_F0, bank(0)[:, 0:TT], D)
            res_act(act, 1, N_POST_F0, G_MIX_PRE + KD)
            act.wait_ge(res_h, 2 * KD)
            stat_act(act, N_SB, bank(0)[:, 0:TT], D)
            for j in range(4):
                if j < 3:
                    sb_split_act(act, 0, j)
                if j != 2:
                    sb_item_act(act, 0, 0, j)
            act.add_instruction(mybir.InstLoadActFuncSet(name=nc.get_next_instruction_name(), act_func_set_id=6,
                                                         engine=mybir.EngineType.Activation))
            z_act_exp(act, 0, 0)
            z_act_ln(act, 0, 0)
            sb_turns(act, sb_pair_act)
            sb_o_act(act, SB_PAIRS - 1)
            out_act(act, CH_OUT1, N_POST_A1)
            stat_act(act, N_POST_A1, bank(0)[:, 0:TT], D)
            res_act(act, 2, N_POST_A1, G_FFN_PRE + KD)
            gu_act(act, CH_GU1, 1, N_FFN1)
            dn_act(act, CH_DN1, N_POST_F1)
            stat_act(act, N_POST_F1, bank(0)[:, 0:TT], D)
            for n in range(KD):
                act.wait_ge(y_tr, n + 1)
                act.activation(ot[:, n, :], bank(n), ACT.Copy).then_inc(y_sb, 1)

        @block.vector
        def _(dve):
            dve.wait_ge(gains_tr, 1)
            nc.vector.tensor_copy(gains[:, :], bank(7)[:, 0:G_ROWS]).then_inc(gains_ready, 1)
            dve.wait_ge(gains_ready, 1)
            for k in range(KD + 1):
                if k < KD:
                    dve.wait_ge(x_tr, k + 1)
                    nc.vector.tensor_copy(hT[:, k, :], bank(k)).then_inc(h_ready, 1)
                if k:
                    m = k - 1
                    dve.wait_ge(uh_ready, m + 1)
                    nc.vector.scalar_tensor_tensor(ul[:, m, :], hT[:, m, :], gains[:, m:m + 1],
                                                   uh[:, m, :].bitcast(F32), ALU.mult, ALU.subtract)\
                        .then_inc(u_ready, 1)
                if k == 2:
                    for n in range(AHEAD):
                        split_lo(dve, Chunk(n))
            split_lo(dve, Chunk(AHEAD))
            dve.wait_ge(brow_mm, 1)
            nc.vector.tensor_copy(brow[:, 0:T], bank(6)[0:8, :])
            nc.vector.tensor_copy(brow[:, T:640], bank(7)[0:8, 0:640 - T]).then_inc(brow_sb, 1)
            stat_dve(dve, N_X, 5, r_pre)
            dve.wait_ge(st_r, 1)
            for n in range(len(IN_TILES)):
                if n:
                    split_lo(dve, Chunk(CH_IN + n + AHEAD))
                dve.wait_ge(w_used, CH_IN + n + 1)
                rows = slice(0, P) if n < 5 else ROPE_ROWS
                if 2 <= n:
                    m = n - 2
                    k, j = lat_norm[m]
                    dve.wait_ge(sq_ready, SQ0[k] + j + 1)
                nc.vector.tensor_tensor(tf[rows, n % 2, :], bank(n)[rows, :], r_pre[rows, :], ALU.mult)\
                    .then_inc(in_scaled, 1)
                if n < 5:
                    hi, lo, m = lat_dst[n]
                    dve.wait_ge(lat_hi, n + 1)
                    nc.vector.scalar_tensor_tensor(lo[:, m, :], tf[:, n % 2, :],
                                                   gains[:, lat_gain[n]:lat_gain[n] + 1],
                                                   hi[:, m, :].bitcast(F32), ALU.mult, ALU.subtract)\
                        .then_inc(lat_ready, 1)
            dve.wait_ge(tables_in, 16)
            rope_rows_dve(dve, 1, 0, (in_scaled, 6))
            dve.wait_ge(kr_hi, 1)
            for b in range(3):
                ins = nc.vector.tensor_tensor(mq[3][ROPE_ROWS, b, :], tf[ROPE_ROWS, 1, :],
                                              mq[2][ROPE_ROWS, b, :].bitcast(F32), ALU.subtract)
            ins.then_inc(kr_lo, 1)
            stat_dve(dve, N_CQ, 6, r_q)
            stat_dve(dve, N_CKV, 6, r_kv)
            dve.wait_ge(st_r, 3)
            for n, it in enumerate(items[0:8]):
                item_scale(dve, it)
                item_lo(dve, it)
                if n == 2:
                    scores_dve(dve, 0)
                if n == 3:
                    den_dve(dve, 0)
                if n == 4:
                    scores_dve(dve, 1)
            for hh in range(NH0):
                a, b, c = slots_of_step(hh)
                if hh % 2:
                    item_lo(dve, a)
                if hh + 1 < NH0:
                    den_dve(dve, hh + 1)
                probs_dve(dve, hh)
                if hh % 2 == 0:
                    if hh:
                        o_dve(dve, hh // 2 - 1)
                    item_scale(dve, a)
                if hh + 2 < NH0:
                    scores_dve(dve, hh + 2)
                item_scale(dve, b)
                if hh % 2 == 0:
                    item_lo(dve, a)
                item_lo(dve, b)
                item_scale(dve, c)
                item_lo(dve, c)
                if hh == NH0 - 2:
                    split_lo(dve, Chunk(CH_OUT0 + AHEAD))
            o_dve(dve, NH0 // 2 - 1)
            out_dve(dve, CH_OUT0)
            res_dve(dve, 0, N_POST_A0, G_MIX_POST, G_FFN_PRE)
            gu_dve(dve, CH_GU0, 0, N_FFN0)
            dn_dve(dve, CH_DN0)
            res_dve(dve, 1, N_POST_F0, G_FFN_POST, G_MIX_PRE + KD)
            for j in range(3):
                sb_split_dve(dve, 0, j)
                if j == 0:
                    stat_dve(dve, N_SB, 0, r_pre)
                    dve.wait_ge(st_r, N_SB + 1)
                sb_scale(dve, 0, 0, j)
                if j < 2:
                    sb_item_dve(dve, 0, 0, j)
            sb_item_dve(dve, 0, 0, 3)
            z_dve_clamp(dve, 0, 0)
            z_dve(dve, 0, 0)
            ns_dve_hi(dve, 0, 0, True)
            ns_dve_lo(dve, 0, 0)
            sb_turns(dve, sb_pair_dve)
            sb_o_dve(dve, SB_PAIRS - 1)
            out_dve(dve, CH_OUT1)
            res_dve(dve, 2, N_POST_A1, G_MIX_POST + KD, G_FFN_PRE + KD)
            gu_dve(dve, CH_GU1, 1, N_FFN1)
            dn_dve(dve, CH_DN1)
            res_dve(dve, 3, N_POST_F1, G_FFN_POST + KD, None)

        @block.tensor
        def _(pe):
            pe.wait_ge(consts_ready, 1)
            pe.wait_ge(gains_in, 16 * 6)
            nc.tensor.transpose(bank(7)[:, 0:G_ROWS], graw[:, :], ident[0:G_ROWS, 0:G_ROWS]).then_inc(gains_tr, 1)
            for k in range(KD):
                if k == KD - 1:
                    pe.wait_ge(gains_ready, 1)
                for t in range(TT):
                    if k == 0:
                        pe.wait_ge(x_in[t], 16)
                    mm = nc.tensor.transpose(bank(k)[:, t * P:(t + 1) * P], xt[:, t, k * P:(k + 1) * P], ident[:, :])
                mm.then_inc(x_tr, 1)
            for n, (_, cols) in enumerate(IN_TILES):
                c = Chunk(CH_IN + n)
                pe.wait_ge(w_lo, c.n + 1)
                project(pe, bank(n)[0:cols, :], c, KD, P, 0, cols, uh, ul,
                        x_ready=(u_ready, 0) if n == 0 else None).then_inc(w_used, 1)
                if n == 0:
                    pe.wait_ge(bias_in_sbuf, 32)
                    nc.tensor.matmul(bank(6)[0:8, :], rb[:, :], hot[:, 0:T], start=True, stop=True)
                    nc.tensor.matmul(bank(7)[0:8, 0:640 - T], rb[:, :], hot[:, T:640], start=True, stop=True)\
                        .then_inc(brow_mm, 1)
                    stat_pe_spread(pe, N_X, 5)
                if n == 4:
                    pe.wait_ge(brow_sb, 1)
                    pe.wait_ge(st_r, 1)
                    stat_pe(pe, N_CQ, 6, AD0[N_CKV])
            stat_pe_spread(pe, N_CQ, 6)
            pe.wait_ge(st_r, N_CQ + 1)
            stat_pe(pe, N_CKV, 6, AD0[N_CKV + 1])
            stat_pe_spread(pe, N_CKV, 6)
            pe.wait_ge(lat_ready, 5)
            for n, it in enumerate(items[0:8]):
                item_pe(pe, it)
                if n == 2:
                    scores_pe(pe, 0)
                if n == 4:
                    scores_pe(pe, 1)
            for hh in range(NH0):
                a, b, c = slots_of_step(hh)
                probs_pe(pe, hh)
                item_pe(pe, a)
                if hh + 2 < NH0:
                    scores_pe(pe, hh + 2)
                item_pe(pe, b)
                if hh == NH0 - 3:
                    pe.wait_ge(pj_read, len(items))
                    out_part(pe, CH_OUT0, 0, out0_at, 0, 6)
                elif hh == NH0 - 2:
                    pe.wait_ge(sc_read, NH0)
                    out_part(pe, CH_OUT0, 1, out0_at, 0, 6)
                elif hh == NH0 - 1:
                    out_part(pe, CH_OUT0, 2, out0_at, 0, 6)
                pv_pe(pe, hh)
                item_pe(pe, c)
            pe.wait_ge(o_lo, NH0 // 2 - 1)
            for n in range(3):
                out_part(pe, CH_OUT0, n, out0_at, 6, 7)
            out_pe(pe, CH_OUT0, 0, out0_at, (o_lo, MLA_PAIRS + MOBA_PAIRS), (7, 7, 7))
            stat_pe(pe, N_POST_A0, 0, AD0[N_POST_A0 + 1])
            stat_pe_spread(pe, N_POST_A0, 0)
            gu_pe(pe, CH_GU0, 0, N_FFN0)
            dn_pe(pe, CH_DN0, 1, 0)
            stat_pe(pe, N_POST_F0, 0, AD0[N_POST_F0 + 1])
            stat_pe_spread(pe, N_POST_F0, 0)
            pe.wait_ge(tri_r_ready, 1)
            sb_item_pe(pe, 0, 0, 0)
            stat_pe(pe, N_SB, 0, AD0[N_SB + 1])
            stat_pe_spread(pe, N_SB, 0)
            for j in range(1, 4):
                sb_item_pe(pe, 0, 0, j)
            z_pe(pe, 0, 0, 0)
            sb_turns(pe, sb_pair_pe)
            sb_pv_pe(pe, SB_PAIRS - 1, 1, 1)
            pe.wait_ge(so_lo_s, SB_PAIRS - 1)
            for n in range(3):
                out_part(pe, CH_OUT1, n, out1_at, 6, 7)
            out_pe(pe, CH_OUT1, 2, out1_at, (so_lo_s, SB_PAIRS), (7, 7, 7))
            stat_pe(pe, N_POST_A1, 0, AD0[N_POST_A1 + 1])
            stat_pe_spread(pe, N_POST_A1, 0)
            gu_pe(pe, CH_GU1, 1, N_FFN1)
            dn_pe(pe, CH_DN1, 3, 1)
            stat_pe(pe, N_POST_F1, 0, AD0[N_POST_F1 + 1])
            stat_pe_spread(pe, N_POST_F1, 0)
            pe.wait_ge(st_r, N_POST_F1 + 1)
            for n in range(KD):
                pe.wait_ge(res_h, 3 * KD + n + 1)
                for t in range(TT):
                    mm = nc.tensor.transpose(bank(n)[:, t * P:(t + 1) * P], hT[:, n, t * P:(t + 1) * P], ident[:, :])
                mm.then_inc(y_tr, 1)


_INS = ['x', 'mix_pre_g', 'mix_post_g', 'ffn_pre_g', 'ffn_post_g', 'ab_w_in', 'mla_q_norm_g', 'mla_w_uq',
        'mla_kv_norm_g', 'mla_w_ukv', 'ab_w_out', 'rel_bias', 'sb_w_qkv', 'sb_w_out', 'ffn_w_gate_up', 'ffn_w_down']
_OUTS = [((1, T, D), 'float32')]


def kernel(**inputs):
    import numpy as _np
    import concourse.bacc as _bacc
    from concourse import mybir as _mybir
    from concourse.bass_utils import run_bass_kernel_spmd as _run

    nc = _bacc.Bacc("TRN2", target_bir_lowering=False, num_devices=1)
    arrays, args = {}, []
    for name in _INS:
        a = _np.ascontiguousarray(inputs[name])
        arrays[f"in_{name}_dram"] = a
        args.append(nc.dram_tensor(f"in_{name}_dram", a.shape, _mybir.dt.from_np(a.dtype), kind="ExternalInput").ap())
    for i, (shape, dtype) in enumerate(_OUTS):
        dt = _mybir.dt.from_np(_np.dtype(dtype))
        args.append(nc.dram_tensor(f"out_{i}_dram", shape, dt, kind="ExternalOutput").ap())
    bass_hybrid_two_layers(nc, *args)
    r = _run(nc, [arrays], core_ids=[0])
    got = tuple(r.results[0][f"out_{i}_dram"] for i in range(len(_OUTS)))
    return got[0]
```

```python
import math
from contextlib import ExitStack

import numpy as np

import concourse.bass as bass
from concourse import mybir

F32 = mybir.dt.float32
F32R = mybir.dt.float32r
BF16 = mybir.dt.bfloat16
ALU = mybir.AluOpType
ACT = mybir.ActivationFunctionType

P = 128
T = 512
TT = T // P
D = 1024
KD = D // P
FF = 2816
KF = FF // P
EPS = 1e-6
NEG = -1e30
HD = 64
ROPE = 32
QL, KVL = 384, 256
KQ, KKV = QL // P, KVL // P
MLA_QH = HD + ROPE
MLA_SCALE = float(MLA_QH) ** -0.5
SCALE = float(HD) ** -0.5
THETA = 10000.0
NBUCKET, MAXDIST = 32, 128
O1, O2, O3 = QL, QL + KVL, QL + KVL + ROPE
MLA_PAIRS, MOBA_PAIRS, SB_PAIRS = 4, 4, 8
NH0 = 2 * (MLA_PAIRS + MOBA_PAIRS)

ROW_AT = {3: 0, 2: 512, 0: 896, 1: 1024}
COL_AT = {0: 0, 1: 512, 3: 896, 2: 1024}
CW = 1280

NSLOT = 3
AHEAD = 2
CH_IN = 0
CH_MLA = CH_IN + 6
CH_MOBA = CH_MLA + 2 * MLA_PAIRS
CH_OUT0 = CH_MOBA + 3 * MOBA_PAIRS
CH_GU0 = CH_OUT0 + KD
CH_DN0 = CH_GU0 + 2 * KF
CH_SB = CH_DN0 + 3 * KD
CH_OUT1 = CH_SB + 3 * SB_PAIRS
CH_GU1 = CH_OUT1 + KD
CH_DN1 = CH_GU1 + 2 * KF
CH_END = CH_DN1 + KF
DN_PARTS = ((0, 8), (8, 7), (15, 7))

G_MIX_PRE, G_MIX_POST, G_FFN_PRE, G_FFN_POST, G_Q, G_KV, G_ROWS = 0, 16, 32, 48, 64, 67, 69


def rope_tables():
    half = ROPE // 2
    inv = (np.float32(THETA) ** (-np.arange(half, dtype=np.float32) / np.float32(half))).astype(np.float32)
    ang = np.arange(T, dtype=np.float32)[None, :] * inv[:, None]
    cos, sin = np.cos(ang).astype(np.float32), np.sin(ang).astype(np.float32)
    return np.stack([np.concatenate([cos, cos]), np.concatenate([-sin, sin])])


def bucket_onehot():
    rel = 511 - np.arange(640)
    exact = NBUCKET // 2
    big = exact + (np.log(np.maximum(rel, exact).astype(np.float32) / np.float32(exact))
                   / np.float32(math.log(MAXDIST / exact)) * (NBUCKET - exact)).astype(np.int32)
    bucket = np.where(np.maximum(rel, 0) < exact, np.maximum(rel, 0), np.minimum(big, NBUCKET - 1))
    hot = (bucket[None, :] == np.arange(NBUCKET + 1)[:, None]) & (rel >= 0)[None, :]
    hot[NBUCKET] = rel < 0
    return hot.astype(np.float32)


class Chunk:

    def __init__(self, c0, i=0, per=0):
        assert per % NSLOT == 0
        self.c0, self.i, self.per = c0, i, per
        self.slot = c0 % NSLOT
        self.turn = c0 // NSLOT + i * (per // NSLOT)
        self.n = c0 + i * per

    def later(self, k):
        return Chunk(self.c0 + k, self.i, self.per)


def layer0_items():
    groups = []
    for p in range(MLA_PAIRS):
        cq, ck = CH_MLA + 2 * p, CH_MLA + 2 * p + 1
        groups.append([("mq", p, 0, cq, True, False), ("mk", p, 0, ck, True, False),
                       ("mq", p, 1, cq, False, True), ("mk", p, 1, ck, False, False),
                       ("mv", p, 0, ck, False, True), ("vt", p, 0, None, False, False)])
    for m in range(MOBA_PAIRS):
        p, c = MLA_PAIRS + m, CH_MOBA + 3 * m
        groups.append([("bq", p, 0, c, True, True), ("bk", p, 0, c + 1, True, True),
                       ("bv", p, 0, c + 2, True, True), ("vt", p, 0, None, False, False)])
    return groups


def bass_hybrid_two_layers(nc, x, mix_pre_g, mix_post_g, ffn_pre_g, ffn_post_g, ab_w_in,
                           mla_q_norm_g, mla_w_uq, mla_kv_norm_g, mla_w_ukv, ab_w_out, rel_bias,
                           sb_w_qkv, sb_w_out, ffn_w_gate_up, ffn_w_down, out):
    onehot_d = nc.inline_tensor(bucket_onehot(), name="bucket_onehot").ap()
    rope_d = nc.inline_tensor(rope_tables(), name="rope_tables").ap()
    bias_t = nc.dram_tensor("bias_by_distance", [8, P, 640], F32, kind="Internal")

    groups = layer0_items()
    items = [it for g in groups for it in g]
    order = {it[:3]: n for n, it in enumerate(items)}
    split_order = {}
    for it in items:
        if it[0] not in ("mv", "bv"):
            split_order[it[:3]] = len(split_order)
    inner_order = {}
    for it in items:
        if not it[5]:
            inner_order[it[:3]] = len(inner_order)

    def slots_of_step(hh):
        p, e = hh // 2, hh % 2
        if e:
            vt = groups[p + 1][-1] if p + 1 < len(groups) else None
            return [vt] + (groups[p + 2][0:2] if p + 2 < len(groups) else [None, None])
        if p + 1 >= len(groups):
            return [None] * 3
        g = groups[p + 1]
        return g[2:5] if len(g) == 6 else [g[2], None, None]

    ctx = ExitStack()
    with ctx:
        def sem(name):
            return ctx.enter_context(nc.semaphore(name))

        def sb(stack, name, shape, dt=F32):
            return stack.enter_context(nc.sbuf_tensor(name, shape, dt))

        hT = sb(ctx, "residual", [P, KD, T])
        with ExitStack() as s:
            h_tok = sb(s, "h_tokens", [P, KD, T])
        uh = sb(ctx, "u_hi", [P, KD, T], F32R)
        with ExitStack() as s:
            F = sb(s, "block_out", [P, KD, T])
        ul = sb(ctx, "u_lo", [P, KD, T], F32R)
        raw = sb(ctx, "w_raw", [P, NSLOT, 1024])
        wh = sb(ctx, "w_hi", [P, NSLOT, 1024], F32R)
        wl = sb(ctx, "w_lo", [P, NSLOT, 1024], F32R)
        ident = sb(ctx, "ident", [P, P])
        ones = sb(ctx, "ones", [P, P])
        tri_f = sb(ctx, "tri_f", [P, P])
        negtri = sb(ctx, "negtri", [P, P], F32R)
        negones = sb(ctx, "negones", [P, P], F32R)
        identb = sb(ctx, "identb", [P, P], BF16)
        big = sb(ctx, "big", [P, P], BF16)
        gains = sb(ctx, "gains", [P, G_ROWS])
        r_pre = sb(ctx, "r_pre", [P, T])
        r_post = sb(ctx, "r_post", [P, T])
        acc = sb(ctx, "sq_sum", [P, T])
        sqt = sb(ctx, "sq_tile", [P, T])
        diag = sb(ctx, "diag", [P, TT, P])
        tf = sb(ctx, "tf", [P, 2, T])
        rms = sb(ctx, "rms", [P, TT])
        rinv = sb(ctx, "rinv", [P, TT])
        ssx = sb(ctx, "ssx", [P, TT])
        eps_t = sb(ctx, "eps", [P, 1])
        with ExitStack() as at0:
            vh = sb(at0, "v_hi", [P, 2, TT, 192], F32R)
            vl = sb(at0, "v_lo", [P, 2, TT, 192], F32R)
            oAh = sb(at0, "oA_hi", [P, 4, T], F32R)
            oAl = sb(at0, "oA_lo", [P, 4, T], F32R)
            logits = sb(at0, "logits", [P, 2, CW])
            pth = sb(at0, "probsT_hi", [P, CW], F32R)
            ptl = sb(at0, "probsT_lo", [P, CW], F32R)
            mx = sb(at0, "row_max", [P, 2, TT])
            nmx = sb(at0, "neg_max", [P, 2, TT])
            den = sb(at0, "den", [P, 2, TT])
            rden = sb(at0, "rden", [P, 2, TT])
            with ExitStack() as s:
                xt = sb(s, "x_tokens", [P, TT, D])
                junk = sb(s, "x_squares", [P, D])
                graw = sb(s, "gain_rows", [G_ROWS, P])
            with ExitStack() as s:
                sb(s, "below_x", [P, TT * D + D + P])
                hot = sb(s, "onehot", [NBUCKET + 1, 640])
                rb = sb(s, "rel_bias_rows", [NBUCKET + 1, 8])
            with ExitStack() as s:
                mq = [sb(s, f"mla_{n}", [P, 3, T], F32R) for n in ("q_hi", "q_lo", "k_hi", "k_lo")]
                cqh = sb(s, "cq_hi", [P, KQ, T], F32R)
                cql = sb(s, "cq_lo", [P, KQ, T], F32R)
                ckh = sb(s, "ckv_hi", [P, KKV, T], F32R)
                ckl = sb(s, "ckv_lo", [P, KKV, T], F32R)
                cs = sb(s, "cos_sin", [P, 2, T])
                cmask = sb(s, "causal", [P, T])
                r_q = sb(s, "r_q", [P, T])
                r_kv = sb(s, "r_kv", [P, T])
                rt = sb(s, "rope_tmp", [P, 2, T])
            with ExitStack() as s:
                oBh = sb(s, "oB_hi", [P, 4, T], F32R)
                oBl = sb(s, "oB_lo", [P, 4, T], F32R)
                bias = sb(s, "bias", [P, 2, T])
                sb(s, "below_moba_qk", [P, 2, T])
                bq = [sb(s, f"moba_{n}", [P, 2, T], F32R) for n in ("q_hi", "q_lo", "k_hi", "k_lo")]
        with ExitStack() as s:
            hidh = sb(s, "hidden_hi", [P, KF, T], F32R)
            hidl = sb(s, "hidden_lo", [P, KF, T], F32R)
            gs = sb(s, "gate", [P, 3, T])
            us = sb(s, "up", [P, 3, T])
        with ExitStack() as s:
            sv = [sb(s, f"sb_{n}", [P, 2, TT, 192], F32R) for n in ("v_hi", "v_lo")]
            soh = sb(s, "so_hi", [P, KD, T], F32R)
            sol = sb(s, "so_lo", [P, KD, T], F32R)
            sq = [sb(s, f"sb_{n}", [P, 2, T], F32R) for n in ("q_hi", "q_lo", "k_hi", "k_lo")]
            lsp = sb(s, "softplus", [P, CW])
            nsh = sb(s, "nsp_hi", [P, CW], F32R)
            nsl = sb(s, "nsp_lo", [P, CW], F32R)
            wf = sb(s, "stick", [P, CW])
            swh = sb(s, "stick_hi", [P, 2, CW], F32R)
            swl = sb(s, "stick_lo", [P, 2, CW], F32R)

        ps = ctx.enter_context(nc.psum_tensor("banks", [P, 8, T], F32))

        brow = logits[0:8, 0, 0:640]

        def bank(b):
            return ps[:, b, :]

        def banks(b):
            return ps[:, b:b + 3, :].rearrange("p b n -> p (b n)")

        SC, PT, O_BANK, P_BANK = banks(0), banks(3), 6, 7
        ZB = [banks(0), banks(3)]
        oh = [oAh[:, n, :] for n in range(4)] + [oBh[:, n, :] for n in range(4)]
        ol = [oAl[:, n, :] for n in range(4)] + [oBl[:, n, :] for n in range(4)]

        raw_in = [sem(f"raw_in{n}") for n in range(NSLOT)]
        ukv_in = [sem(f"ukv_in{n}") for n in range(2)]
        w_hi, w_lo, w_used = sem("w_hi_done"), sem("w_lo_done"), sem("w_used")
        consts_ready = sem("consts_ready")
        tri_ready = sem("tri_ready")
        tri_r_ready = sem("tri_rounded")
        x_in = [sem(f"x_in{n}") for n in range(TT)]
        gains_in, tables_in, bias_in_sbuf = sem("gains_in"), sem("tables_in"), sem("bias_tables_in")
        gains_tr, gains_ready = sem("gains_transposed"), sem("gains_ready")
        x_tr, h_ready = sem("x_transposed"), sem("h_copied")
        uh_ready, u_ready = sem("u_hi_ready"), sem("u_ready")
        ssx_ready = sem("x_square_sums")
        sq_last = sem("last_squares")
        st_sum, st_rms, st_rinv = sem("stat_sums"), sem("stat_rms"), sem("stat_rinv")
        st_diag, st_bc, st_r = sem("stat_diag"), sem("stat_spread"), sem("stat_r_ready")
        sq_ready, sq_added = sem("squares_ready"), sem("squares_added")
        in_scaled = sem("latent_scaled")
        lat_hi, lat_ready = sem("latent_hi"), sem("latent_ready")
        brow_mm, brow_sb, brow_out = sem("bias_rows_mm"), sem("bias_rows_sbuf"), sem("bias_rows_dram")
        bias_in = [sem(f"bias_in{n}") for n in range(2)]
        pj_mm, pj_read, pj_hi, pj_lo = sem("proj_product"), sem("proj_bank_read"), sem("proj_hi"), sem("proj_lo")
        rp_sw, rp_cos, rp_sin, rp_done = sem("rope_swapped"), sem("rope_cos"), sem("rope_sin"), sem("rope_done")
        kr_hi, kr_lo = sem("k_rope_hi"), sem("k_rope_lo")
        sc_done, sc_read, mx_neg = sem("scores_done"), sem("scores_read"), sem("max_negated")
        e_done, den_inv, p_done = sem("exp_done"), sem("den_inverted"), sem("probs_done")
        pt_done, pt_hi, pt_lo = sem("probsT_done"), sem("probsT_hi_done"), sem("probsT_lo_done")
        pv_done, o_hi, o_lo = sem("pv_done"), sem("o_hi_done"), sem("o_lo_done")
        f_read = sem("f_read")
        res_t, res_h = sem("branch_scaled"), sem("residual_added")
        gu_read = sem("gate_up_read")
        silu_done, act_mul = sem("silu_done"), sem("hidden_done")
        hid_hi, hid_lo = sem("hidden_hi_done"), sem("hidden_lo_done")
        v0_ready, v1_ready = sem("v_pad_ready"), sem("v1_pad_ready")
        qj_mm, qj_read, qj_hi, qj_lo = sem("sb_product"), sem("sb_bank_read"), sem("sb_hi"), sem("sb_lo")
        z_done, z_min, z_exp, z_ln = sem("z_done"), sem("z_clamped"), sem("z_exp"), sem("z_ln")
        ns_f, ns_hi, ns_lo = sem("softplus_ready"), sem("softplus_hi"), sem("softplus_lo")
        c_done, w_exp, sw_hi, sw_lo = sem("stick_sums"), sem("stick_exp"), sem("stick_hi"), sem("stick_lo")
        sv_done, so_hi_s, so_lo_s = sem("sb_pv_done"), sem("sb_o_hi"), sem("sb_o_lo")
        ht_mm, ht_even, ht_odd = sem("h_transposed"), sem("h_even_banks"), sem("h_odd_banks")
        gain_in, y_mm, y_ss, y_rms = sem("gain_rows_in"), sem("y_product"), sem("y_square_sums"), sem("y_rms")
        y_rinv, y_scaled = sem("y_rms_inverted"), sem("y_scaled")
        y_even, y_odd, y_out = sem("y_even_half"), sem("y_odd_half"), sem("y_out")


        EXP_SET, SQRT_SET, EXP_LN_SET, SILU_SET = 0, 3, 6, 18

        def load_functions(act, n):
            act.add_instruction(mybir.InstLoadActFuncSet(name=nc.get_next_instruction_name(), act_func_set_id=n,
                                                         engine=mybir.EngineType.Activation))

        def load(sp, c, src, kt, cols, stride=None):
            if c.c0 >= NSLOT:
                sp.wait_ge(w_lo, c.n - NSLOT + 1)
            stride = stride or cols
            dst = raw[:, c.slot, 0:kt * stride].rearrange("p (k n) -> p k n", k=kt)[:, :, 0:cols]
            sp.dma_start(dst, src.rearrange("(k p) n -> p k n", p=P)).then_inc(raw_in[c.slot], 16)

        def ukv(c):
            p, j = (c - CH_MLA) // 2, (c - CH_MLA) % 2
            return (ukv_in[p % 2], 48 * (p // 2 + 1)) if 0 <= p < MLA_PAIRS and j == 1 else None

        def width(c):
            if CH_MLA <= c < CH_MOBA:
                return (KQ * 2 * MLA_QH, KKV * 2 * P)[(c - CH_MLA) % 2]
            if CH_DN0 <= c < CH_DN0 + 3 * KD:
                return DN_PARTS[(c - CH_DN0) % 3][1] * P
            return KD * P

        def split_hi(act, c, also=None):
            if c.c0 >= CH_END:
                return
            if also:
                act.wait_ge(*also)
            act.wait_ge(raw_in[c.slot], 16 * (c.turn + 1))
            if c.c0 >= NSLOT:
                act.wait_ge(w_used, c.n - NSLOT + 1)
            w = width(c.c0)
            act.activation(wh[:, c.slot, 0:w], raw[:, c.slot, 0:w], ACT.Copy).then_inc(w_hi, 1)

        def split_lo(dve, c):
            if c.c0 >= CH_END:
                return
            dve.wait_ge(w_hi, c.n + 1)
            w = width(c.c0)
            dve.tensor_tensor(wl[:, c.slot, 0:w], raw[:, c.slot, 0:w], wh[:, c.slot, 0:w].bitcast(F32),
                              ALU.subtract).then_inc(w_lo, 1)

        def mm3(o, lh, ll, rh, rl, start, stop):
            nc.tensor.matmul(o, lh, rh, start=start, stop=False, skip_group_check=True)
            nc.tensor.matmul(o, lh, rl, start=False, stop=False, skip_group_check=True)
            return nc.tensor.matmul(o, ll, rh, start=False, stop=stop, skip_group_check=True)

        def project(pe, o, c, kt, stride, at, m, xh, xl, first=0, total=None, x_ready=None):
            total = total or kt
            for k in range(kt):
                if x_ready:
                    pe.wait_ge(x_ready[0], x_ready[1] + k + 1)
                s = slice(k * stride + at, k * stride + at + m)
                last = mm3(o, wh[:, c.slot, s], wl[:, c.slot, s], xh[:, first + k, :], xl[:, first + k, :],
                           start=(first + k == 0), stop=(first + k == total - 1))
            return last

        def stat_pe(pe, k, b, adds, last=None):
            pe.wait_ge(sq_added, adds)
            for t in range(TT):
                mm = nc.tensor.matmul(bank(b)[:, t:t + 1], acc[:, t * P:(t + 1) * P], ones[:, 0:1],
                                      start=(t == 0), stop=last is None, skip_group_check=True)
            if last is not None:
                pe.wait_ge(sq_last, last)
                for t in range(TT):
                    mm = nc.tensor.matmul(bank(b)[:, t:t + 1], sqt[:, t * P:(t + 1) * P], ones[:, 0:1],
                                          start=False, stop=True, skip_group_check=True)
            mm.then_inc(st_sum, 1)

        def spread_pe(pe, k, b):
            pe.wait_ge(st_diag, k + 1)
            nc.tensor.matmul(bank(b), ones[:, :], diag[:, :, :].rearrange("p t n -> p (t n)"),
                             start=True, stop=True).then_inc(st_bc, 1)

        def stat_act(act, k, b, width):
            if k:
                act.wait_ge(st_sum, k)
            else:
                act.wait_ge(ssx_ready, TT)
            act.activation(rms[:, :], bank(b)[:, 0:TT] if k else ssx[:, :], ACT.Sqrt, bias=eps_t[:, 0:1],
                           scale=1.0 / width).then_inc(st_rms, 1)

        def stat_dve(dve, k, b, dst):
            dve.wait_ge(st_rms, k + 1)
            nc.vector.reciprocal(rinv[:, :], rms[:, :]).then_inc(st_rinv, 1)
            dve.wait_ge(st_rinv, k + 1)
            if k:
                dve.wait_ge(st_bc, k)
            for t in range(TT):
                last = nc.vector.tensor_scalar(diag[:, t, :], ident[:, :], rinv[:, t:t + 1], None, ALU.mult)
            last.then_inc(st_diag, 1)
            if dst is not None:
                stat_copy_dve(dve, k, b, dst)

        def stat_copy_dve(dve, k, b, dst):
            dve.wait_ge(st_bc, k + 1)
            nc.vector.tensor_copy(dst[:, :], bank(b)).then_inc(st_r, 1)

        def square(act, src, n, k):
            if n == 0:
                if k > 1:
                    act.wait_ge(st_sum, k - 1)
                act.activation(acc[:, :], src, ACT.Square).then_inc(sq_ready, 1)
            else:
                if AD0[k] + n > 1:
                    act.wait_ge(sq_added, AD0[k] + n - 1)
                act.activation(sqt[:, :], src, ACT.Square).then_inc(sq_ready, 1)

        def add_squares(pool, n, k):
            pool.wait_ge(sq_ready, SQ0[k] + n + 1)
            if n > 1:
                pool.wait_ge(sq_added, AD0[k] + n - 1)
            nc.gpsimd.tensor_tensor(acc[:, :], acc[:, :], sqt[:, :], ALU.add).then_inc(sq_added, 1)

        def square_h(act, n, k):
            if n == 0:
                act.wait_ge(st_sum, k - 1)
                dst = acc[:, :]
            else:
                if n > 2:
                    act.wait_ge(sq_added, AD0[k] + n - 2)
                dst = tf[:, n % 2, :]
            act.activation(dst, hT[:, n, :], ACT.Square).then_inc(sq_ready, 1)

        def add_h_squares(dve, n, k):
            dve.wait_ge(sq_ready, SQ0[k] + n + 1)
            if n > 1:
                dve.wait_ge(sq_added, AD0[k] + n - 1)
            nc.vector.tensor_tensor(acc[:, :], acc[:, :], tf[:, n % 2, :], ALU.add).then_inc(sq_added, 1)

        N_X, N_CQ, N_CKV, N_POST_A0, N_FFN0, N_POST_F0, N_SB, N_POST_A1, N_FFN1 = range(9)
        tiles_of = [0, KQ, KKV] + [KD] * 6
        posts = (N_POST_A0, N_POST_F0, N_POST_A1)
        SQ0 = [sum(t for j, t in enumerate(tiles_of[:k]) if j not in posts) for k in range(9)]
        AD0 = [sum(t - (2 if j in posts else 1) for j, t in enumerate(tiles_of[:k]) if j) for k in range(10)]

        def f_pe(pe, chunks, fn, n, operands, b):
            pe.wait_ge(f_read, fn * KD + n - 1)
            at = 0
            total = sum(kt for _, kt in chunks)
            for c, kt in chunks:
                pe.wait_ge(w_lo, c.n + 1)
                for k in range(kt):
                    s = slice(k * P, (k + 1) * P)
                    xh, xl = operands(pe, at)
                    last = mm3(bank(b), wh[:, c.slot, s], wl[:, c.slot, s], xh, xl,
                               start=(at == 0), stop=(at == total - 1))
                    at += 1
                last.then_inc(w_used, 1)

        def f_act(act, last_chunk, b, n, first, k, final=False):
            act.wait_ge(w_used, last_chunk.n + 1)
            if first:
                act.wait_ge(st_sum, k - 1)
                act.activation(acc[:, :], bank(b), ACT.Square)
            else:
                act.wait_ge(sq_added, AD0[k] + n - 1)
                sq = act.activation(sqt[:, :], bank(b), ACT.Square)
                if final:
                    sq.then_inc(sq_last, 1)
            act.activation(F[:, n, :] if isinstance(n, int) else F[:, bass.ds(n, 1), :], bank(b), ACT.Copy)\
                .then_inc(f_read, 1)

        def f_pool(pool, fn, n, k):
            pool.wait_ge(f_read, fn * KD + n + 1)
            if n > 1:
                pool.wait_ge(sq_added, AD0[k] + n - 1)
            nc.gpsimd.tensor_tensor(acc[:, :], acc[:, :], sqt[:, :], ALU.add).then_inc(sq_added, 1)

        def out_sp(sp, ch, w):
            for n in range(KD):
                load(sp, Chunk(ch + n), w[:, n * P:(n + 1) * P], KD, P)

        OUT_BANK = (7, 0, 1, 2, 6, 7, 0, 1)

        def out_part(pe, ch, n, o_at, k0, k1):
            c = Chunk(ch + n)
            if k0 == 0:
                pe.wait_ge(w_lo, c.n + 1)
            for k in range(k0, k1):
                s = slice(k * P, (k + 1) * P)
                last = mm3(bank(OUT_BANK[n]), wh[:, c.slot, s], wl[:, c.slot, s], *o_at(k),
                           start=(k == 0), stop=(k == KD - 1))
            if k1 == KD:
                last.then_inc(w_used, 1)

        def out_pe(pe, ch, fn, o_at, o_ready, begun):
            pe.wait_ge(*o_ready)
            for n in range(KD):
                if n >= 5:
                    pe.wait_ge(f_read, fn * KD + n - 4)
                out_part(pe, ch, n, o_at, begun[n] if n < len(begun) else 0, KD)

        def out_act(act, ch, k):
            for n in range(KD):
                if n:
                    split_hi(act, Chunk(ch + n + AHEAD))
                if n == KD - 1:
                    load_functions(act, SQRT_SET)
                f_act(act, Chunk(ch + n), OUT_BANK[n], n, n == 0, k, n == KD - 1)

        def out_dve(dve, ch):
            for n in range(1, KD):
                split_lo(dve, Chunk(ch + n + AHEAD))

        def f_adds(pool, fn, k):
            for n in range(1, KD - 1):
                f_pool(pool, fn, n, k)

        def res_dve(dve, r, k, g_post, g_pre, c):
            def lo(m):
                dve.wait_ge(uh_ready, KD * (r + 1) + m + 1)
                nc.vector.scalar_tensor_tensor(ul[:, m, :], hT[:, m, :], gains[:, g_pre + m:g_pre + m + 1],
                                               uh[:, m, :].bitcast(F32), ALU.mult, ALU.subtract).then_inc(u_ready, 1)

            stat_dve(dve, k, 0, None)
            for n in range(KD + 1):
                if n < KD:
                    if n >= 2:
                        dve.wait_ge(res_h, KD * r + n - 1)
                    if n == KD - 1:
                        dve.wait_ge(f_read, KD * (r + 1))
                    dve.wait_ge(*((st_r, k + 1) if n else (st_bc, k + 1)))
                    nc.vector.scalar_tensor_tensor(tf[:, n % 2, :], F[:, n, :], gains[:, g_post + n:g_post + n + 1],
                                                   r_post[:, :] if n else bank(0), ALU.mult, ALU.mult)\
                        .then_inc(res_t, 1)
                if n == 0:
                    dve.wait_ge(res_t, KD * r + 1)
                    nc.vector.tensor_tensor(hT[:, 0, :], hT[:, 0, :], tf[:, 0, :], ALU.add).then_inc(res_h, 1)
                    nc.vector.tensor_copy(r_post[:, :], bank(0)).then_inc(st_r, 1)
                if n == 0 or n >= 2:
                    lo(n if n == 0 else n - 1)
                    if n == KD - 1:
                        split_lo(dve, Chunk(c + 2))
            for n in range(1, KD):
                add_h_squares(dve, n, k + 1)
                if n == 3:
                    split_lo(dve, Chunk(c + 3))
            split_lo(dve, Chunk(c + 4))

        def res_act(act, r, k, g_pre, c):
            split_hi(act, Chunk(c + 2))
            for n in range(KD):
                act.wait_ge(res_h, KD * r + n + 1)
                act.activation(uh[:, n, :], hT[:, n, :], ACT.Copy, scale=gains[:, g_pre + n:g_pre + n + 1])\
                    .then_inc(uh_ready, 1)
            for n in range(KD):
                square_h(act, n, k + 1)
                if n == 3:
                    split_hi(act, Chunk(c + 3))
            split_hi(act, Chunk(c + 4))

        def res_pool(pool, r):
            for n in range(1, KD):
                pool.wait_ge(res_t, KD * r + n + 1)
                nc.gpsimd.tensor_tensor(hT[:, n, :], hT[:, n, :], tf[:, n % 2, :], ALU.add).then_inc(res_h, 1)

        def two_products(pe, c, b0, b1, x_ready, r_copied):
            for n in range(2):
                pe.wait_ge(w_lo, c.n + n + 1)
            if r_copied:
                pe.wait_ge(st_r, r_copied)
            for k in range(KD):
                pe.wait_ge(u_ready, x_ready + k + 1)
                s = slice(k * P, (k + 1) * P)
                for cc, b in ((c, b0), (c.later(1), b1)):
                    mm = mm3(bank(b), wh[:, cc.slot, s], wl[:, cc.slot, s], uh[:, k, :], ul[:, k, :],
                             start=(k == 0), stop=(k == KD - 1))
                    if k == KD - 1:
                        mm.then_inc(w_used, 1)

        def gu_chunk(ch, n0, i=0):
            return Chunk(ch + 2 * n0, i, 6)

        def gu_sp(sp, ch, w):
            def tile(n0, i):
                c = gu_chunk(ch, n0, i)
                for half in range(2):
                    at = half * FF + n0 * P
                    src = w[:, at:at + P] if isinstance(i, int) and i == 0 else w[:, bass.ds(i * (3 * P) + at, P)]
                    load(sp, c.later(half), src, KD, P)
            tile(0, 0)
            with sp.Fori(0, (KF - 1) // 3) as i:
                for b in range(1, 4):
                    tile(b, i)

        def gu_pe(pe, ch, l, k):
            def tile(n0, i, halves=(0, 1)):
                c, b = gu_chunk(ch, n0, i), 2 * (n0 % 3)
                for half in halves:
                    cc = c.later(half)
                    pe.wait_ge(w_lo, cc.n + 1)
                    if n0 == 3 or not isinstance(i, int):
                        pe.wait_ge(gu_read, base_wait(l, n0, i, half))
                    project(pe, bank(b + half), cc, KD, P, 0, P, uh, ul).then_inc(w_used, 1)

            def base_wait(l, n0, i, half):
                return 2 * KF * l + 2 * (n0 - 3) + half + 1 + i * 6

            two_products(pe, gu_chunk(ch, 0), 0, 1, KD * (2 * l + 1), k)
            tile(1, 0, (0,))
            stat_pe(pe, k, 6, AD0[k + 1])
            tile(1, 0, (1,))
            spread_pe(pe, k, 6)
            tile(2, 0)
            tile(3, 0)
            with pe.Fori(1, (KF - 1) // 3) as i:
                for b in range(1, 4):
                    tile(b, i)

        def gu_act(act, ch, l, k):
            def hi(n0, i):
                act.wait_ge(act_mul, KF * l + n0 + i * 3 + 1)
                o = hidh[:, n0, :] if isinstance(i, int) else hidh[:, bass.ds(i * 3 + n0, 1), :]
                act.activation(o, us[:, n0 % 3, :], ACT.Copy).then_inc(hid_hi, 1)

            def tile(n0, i, first=False):
                c = gu_chunk(ch, n0, i)
                if first:
                    stat_act(act, k, 6, D)
                    load_functions(act, SILU_SET)
                act.wait_ge(gu_read, 2 * KF * l + 2 * n0 + i * 6 + 1)
                act.activation(gs[:, n0 % 3, :], gs[:, n0 % 3, :], ACT.Silu).then_inc(silu_done, 1)
                if not first:
                    split_hi(act, c.later(3))
                    hi(n0 - 1, i)
                    split_hi(act, c.later(4))

            tile(0, 0, True)
            with act.Fori(0, (KF - 1) // 3) as i:
                for b in range(1, 4):
                    tile(b, i)
            hi(KF - 1, 0)

        def gu_pool(pool, l):
            def tile(n0, i):
                pool.wait_ge(silu_done, KF * l + n0 + i * 3 + 1)
                pool.wait_ge(gu_read, 2 * KF * l + 2 * n0 + i * 6 + 2)
                nc.gpsimd.tensor_tensor(us[:, n0 % 3, :], us[:, n0 % 3, :], gs[:, n0 % 3, :], ALU.mult)\
                    .then_inc(act_mul, 1)
            tile(0, 0)
            with pool.Fori(0, (KF - 1) // 3) as i:
                for b in range(1, 4):
                    tile(b, i)

        def gu_dve(dve, ch, l, k):
            def lo(n0, i):
                dve.wait_ge(hid_hi, KF * l + n0 + i * 3 + 1)
                o = hidl[:, n0, :] if isinstance(i, int) else hidl[:, bass.ds(i * 3 + n0, 1), :]
                h = hidh[:, n0, :] if isinstance(i, int) else hidh[:, bass.ds(i * 3 + n0, 1), :]
                nc.vector.tensor_tensor(o, us[:, n0 % 3, :], h.bitcast(F32), ALU.subtract).then_inc(hid_lo, 1)

            def tile(n0, i, first=False):
                c, b = gu_chunk(ch, n0, i), n0 % 3
                if first:
                    stat_dve(dve, k, 6, r_pre)
                    dve.wait_ge(st_r, k + 1)
                dve.wait_ge(w_used, c.n + 1)
                nc.vector.tensor_tensor(gs[:, b, :], bank(2 * b), r_pre[:, :], ALU.mult).then_inc(gu_read, 1)
                if not first:
                    split_lo(dve, c.later(3))
                dve.wait_ge(w_used, c.n + 2)
                nc.vector.tensor_tensor(us[:, b, :], bank(2 * b + 1), r_pre[:, :], ALU.mult).then_inc(gu_read, 1)
                if not first:
                    lo(n0 - 1, i)
                    split_lo(dve, c.later(4))

            tile(0, 0, True)
            with dve.Fori(0, (KF - 1) // 3) as i:
                for b in range(1, 4):
                    tile(b, i)
            lo(KF - 1, 0)

        def dn_chunks(ch, n0, i=0):
            return [(Chunk(ch + 3 * n0 + j, i, 6), kt) for j, (_, kt) in enumerate(DN_PARTS)]

        DN_TURNS = (KD - 2) // 2

        def dn_sp(sp, ch, w):
            def tile(n0, i):
                for (c, kt), (k0, _) in zip(dn_chunks(ch, n0, i), DN_PARTS):
                    rows = w[k0 * P:(k0 + kt) * P, :]
                    src = rows[:, n0 * P:(n0 + 1) * P] if isinstance(i, int) else rows[:, bass.ds(i * (2 * P) + n0 * P, P)]
                    load(sp, c, src, kt, P)
            with sp.Fori(0, DN_TURNS) as i:
                tile(0, i)
                tile(1, i)
            tile(KD - 2, 0)
            tile(KD - 1, 0)

        def dn_pe(pe, ch, fn, l):
            def operands(ready):
                def at(pe, k):
                    if ready:
                        pe.wait_ge(hid_lo, KF * l + k + 1)
                    return hidh[:, k, :], hidl[:, k, :]
                return at

            def tile(n0, i, first=False):
                f_pe(pe, dn_chunks(ch, n0, i), fn, n0 + i * 2, operands(first), 6 + n0 % 2)
            tile(0, 0, True)
            tile(1, 0)
            with pe.Fori(1, DN_TURNS) as i:
                tile(0, i)
                tile(1, i)
            tile(KD - 2, 0)
            tile(KD - 1, 0)

        def dn_act(act, ch, k):
            def tile(n0, i, first=False):
                c = Chunk(ch + 3 * n0, i, 6)
                final = n0 == KD - 1
                split_hi(act, c.later(3))
                split_hi(act, c.later(4))
                if final:
                    load_functions(act, SQRT_SET)
                f_act(act, c.later(2), 6 + n0 % 2, n0 + i * 2, first, k, final)
                if not final:
                    split_hi(act, c.later(5))
            tile(0, 0, True)
            tile(1, 0)
            with act.Fori(1, DN_TURNS) as i:
                tile(0, i)
                tile(1, i)
            tile(KD - 2, 0)
            tile(KD - 1, 0)

        def dn_dve(dve, ch):
            def tile(n0, i):
                c = Chunk(ch + 3 * n0, i, 6)
                for j in range(3 if n0 < KD - 1 else 2):
                    split_lo(dve, c.later(3 + j))
            with dve.Fori(0, DN_TURNS) as i:
                tile(0, i)
                tile(1, i)
            tile(KD - 2, 0)
            tile(KD - 1, 0)

        BANK_ORDER = (6, 7, 2, 3, 4, 5, 0, 1)

        def last_chunk(n0, i=0):
            return Chunk(CH_DN1 + n0, i, 3)

        def last_sp(sp, w):
            sp.wait_ge(sq_added, AD0[N_FFN1 + 1])
            sp.dma_start(tf[:, :, :].rearrange("p a n -> p (a n)"), ffn_post_g[1:2, :].to_broadcast([P, D]))\
                .then_inc(gain_in, 16)
            load(sp, last_chunk(0), w[0:P, :], 1, D)
            with sp.Fori(0, (KF - 1) // 3) as i:
                for b in range(1, 4):
                    load(sp, last_chunk(b, i), w[bass.ds(i * (3 * P) + b * P, P), :], 1, D)

        def last_splits(eng, split):
            with eng.Fori(0, (KF - 4) // 3) as i:
                for b in range(3):
                    split(eng, last_chunk(b + 3, i))
            split(eng, last_chunk(KF - 1))

        def last_pe(pe):
            for n, b in enumerate(BANK_ORDER):
                t, half = b // 2, b % 2
                if b < 6:
                    pe.wait_ge(gu_read, 4 * KF - 2 * (0, 2, 1)[t] - 1 + half)
                for m in range(4):
                    mm = nc.tensor.transpose(bank(b)[:, m * P:(m + 1) * P], hT[:, 4 * half + m, t * P:(t + 1) * P],
                                             ident[:, :])
                mm.then_inc(ht_mm, 1)
            def products(k, b):
                c, t, half = last_chunk(k), b // 2, b % 2
                tok, cols = slice(t * P, (t + 1) * P), slice(half * T, (half + 1) * T)
                return mm3(bank(b), hidh[:, k, tok], hidl[:, k, tok], wh[:, c.slot, cols], wl[:, c.slot, cols],
                           start=(k == 0), stop=(k == KF - 1))

            for k in range(KF - NSLOT):
                pe.wait_ge(w_lo, last_chunk(k).n + 1)
                pe.wait_ge(hid_lo, KF + k + 1)
                for n, b in enumerate(BANK_ORDER if k == 0 else range(8)):
                    if k == 0:
                        pe.wait_ge(ht_odd if b % 2 else ht_even, n // 2 + 1)
                    mm = products(k, b)
                mm.then_inc(w_used, 1)
            for t in range(TT):
                for k in range(KF - NSLOT, KF):
                    if t == 0:
                        pe.wait_ge(w_lo, last_chunk(k).n + 1)
                        pe.wait_ge(hid_lo, KF + k + 1)
                    products(k, 2 * t)
                    mm = products(k, 2 * t + 1)
                mm.then_inc(y_mm, 1)

        y_tok = F

        def two_banks(x, t):
            return x[:, 2 * t:2 * t + 2, :].rearrange("p a n -> p (a n)")

        def last_act(act):
            for n, b in enumerate(BANK_ORDER):
                if b % 2 == 0:
                    act.wait_ge(ht_mm, n + 1)
                    act.activation(h_tok[:, b, :], bank(b), ACT.Copy).then_inc(ht_even, 1)
            load_functions(act, SQRT_SET)
            last_splits(act, split_hi)
            for t in range(TT):
                act.wait_ge(y_mm, t + 1)
                act.activation(two_banks(y_tok, t), two_banks(ps, t), ACT.Square, accum_out=ssx[:, t:t + 1])\
                    .then_inc(y_ss, 1)
                act.wait_ge(y_ss, t + 1)
                act.activation(rms[:, t:t + 1], ssx[:, t:t + 1], ACT.Sqrt, bias=eps_t[:, 0:1], scale=1.0 / D)\
                    .then_inc(y_rms, 1)

        def last_dve(dve):
            for n, b in enumerate(BANK_ORDER):
                if b % 2:
                    dve.wait_ge(ht_mm, n + 1)
                    nc.vector.tensor_copy(h_tok[:, b, :], bank(b)).then_inc(ht_odd, 1)
            last_splits(dve, split_lo)
            dve.wait_ge(gain_in, 16)
            for t in range(TT):
                dve.wait_ge(y_rms, t + 1)
                nc.vector.reciprocal(rinv[:, t:t + 1], rms[:, t:t + 1]).then_inc(y_rinv, 1)
                dve.wait_ge(y_rinv, t + 1)
                nc.vector.scalar_tensor_tensor(two_banks(y_tok, t), two_banks(ps, t), rinv[:, t:t + 1],
                                               tf[:, :, :].rearrange("p a n -> p (a n)"), ALU.mult, ALU.mult)\
                    .then_inc(y_scaled, 1)
                dve.wait_ge(y_scaled, t + 1)
                dve.wait_ge(ht_even, TT)
                nc.vector.tensor_tensor(y_tok[:, 2 * t, :], y_tok[:, 2 * t, :], h_tok[:, 2 * t, :], ALU.add)\
                    .then_inc(y_even, 1)

        def last_pool(pool):
            for t in range(TT):
                pool.wait_ge(y_scaled, t + 1)
                nc.gpsimd.tensor_tensor(y_tok[:, 2 * t + 1, :], y_tok[:, 2 * t + 1, :], h_tok[:, 2 * t + 1, :], ALU.add)\
                    .then_inc(y_odd, 1)

        IN_TILES = [(0, P), (P, P), (2 * P, P), (O1, P), (O1 + P, P), (O2 - HD, MLA_QH)]
        lat_gain = [G_Q, G_Q + 1, G_Q + 2, G_KV, G_KV + 1]
        lat_dst = [(cqh, cql, 0), (cqh, cql, 1), (cqh, cql, 2), (ckh, ckl, 0), (ckh, ckl, 1)]
        lat_norm = [(N_CQ, 0), (N_CQ, 1), (N_CQ, 2), (N_CKV, 0), (N_CKV, 1)]

        ROPE_ROWS = slice(HD, HD + ROPE)

        def rope_rows_dve(dve, x, number, scaled):
            dve.wait_ge(*scaled)
            if number:
                dve.wait_ge(rp_done, number)
            nc.vector.stream_shuffle(rt[ROPE_ROWS, 0, :], x[ROPE_ROWS, :],
                                     [(j + ROPE // 2) % ROPE for j in range(ROPE)]).then_inc(rp_sw, 1)

        def rope_rows_pool(pool, x, number, scaled):
            pool.wait_ge(*scaled)
            if number:
                pool.wait_ge(rp_done, number)
            nc.gpsimd.tensor_tensor(rt[ROPE_ROWS, 1, :], x[ROPE_ROWS, :], cs[ROPE_ROWS, 0, :], ALU.mult)\
                .then_inc(rp_cos, 1)
            pool.wait_ge(rp_sw, number + 1)
            nc.gpsimd.tensor_tensor(rt[ROPE_ROWS, 0, :], rt[ROPE_ROWS, 0, :], cs[ROPE_ROWS, 1, :], ALU.mult)\
                .then_inc(rp_sin, 1)
            pool.wait_ge(rp_cos, number + 1)
            pool.wait_ge(rp_sin, number + 1)
            nc.gpsimd.tensor_tensor(x[ROPE_ROWS, :], rt[ROPE_ROWS, 0, :], rt[ROPE_ROWS, 1, :], ALU.add)\
                .then_inc(rp_done, 1)

        tiles = [tf[:, 0, :], tf[:, 1, :], diag[:, :, :].rearrange("p t n -> p (t n)")]

        def scaled_tile(it):
            return tiles[n_tf(it) % 3]

        def item_done(eng, it):
            if it[5]:
                eng.wait_ge(w_used, it[3] + 1)
            else:
                eng.wait_ge(pj_mm, inner_order[it[:3]] + 1)

        def item_bank(it):
            n = order[it[:3]]
            return (7, 3, 4, 5, 6, 3, 4, 5)[n] if n < 8 else P_BANK

        def head_of(it):
            return 2 * it[1] + it[2]

        def item_pe(pe, it):
            if it is None:
                return
            kind, p, e, c, first, last = it
            n = order[it[:3]]
            c = Chunk(c) if c is not None else None
            if n >= 8:
                pe.wait_ge(pj_read, n)
            elif n >= 5:
                pe.wait_ge(pj_read, n - 3)
            elif n == 4:
                pe.wait_ge(st_r, N_CKV + 1)
            if n == 7 or kind == "vt":
                pe.wait_ge(pj_read, n)
            if first:
                pe.wait_ge(w_lo, c.n + 1)
            b = bank(item_bank(it))
            if kind == "mq":
                mm = project(pe, b[0:MLA_QH, :], c, KQ, 2 * MLA_QH, e * MLA_QH, MLA_QH, cqh, cql)
            elif kind == "mk":
                mm = project(pe, b[0:HD, :], c, KKV, P, e * HD, HD, ckh, ckl)
            elif kind == "mv":
                mm = project(pe, b, c, KKV, P, KKV * P, P, ckh, ckl)
            elif kind == "vt":
                for t in range(TT):
                    mm = nc.tensor.transpose(b[:, t * P:(t + 1) * P], scaled_tile(it)[:, t * P:(t + 1) * P], ident[:, :])
            else:
                mm = project(pe, b, c, KD, P, 0, P, uh, ul)
            mm.then_inc(w_used if last else pj_mm, 1)

        split_at = {}
        for n, it in enumerate(items):
            ended = items[n - 1][3] if n and items[n - 1][5] else CH_MLA - 1 if n == 0 else None
            ahead = ended + NSLOT if ended is not None else None
            split_at[it[:3]] = ahead if ahead is not None and ahead < CH_OUT0 + AHEAD else None

        tf_of = {}
        for it in items:
            if it[0] != "vt":
                tf_of[it[:3]] = len(tf_of) + KQ + KKV + 1

        def n_tf(it):
            if it[0] == "vt":
                return tf_of[("mv" if it[1] < MLA_PAIRS else "bv", it[1], 0)]
            return tf_of[it[:3]]

        def v_views(v, buf):
            return v[:, buf, :, 0:HD], v[:, buf, :, 2 * HD:3 * HD]

        def qk_dst(it):
            kind, p, e = it[:3]
            if kind[0] == "m":
                j = 0 if kind == "mq" else 2
                rows = slice(0, MLA_QH) if kind == "mq" else slice(0, HD)
                return [mq[j + a][rows, head_of(it) % 3, :] for a in range(2)], rows
            j = 0 if kind == "bq" else 2
            return [bq[j + a][:, p % 2, :] for a in range(2)], slice(0, P)

        def buffer_free(eng, it):
            kind, p, e = it[:3]
            if kind[0] == "m":
                h = head_of(it)
                if h >= 3 and kind in ("mq", "mk"):
                    eng.wait_ge(sc_done, 3 * (h - 2))
            elif kind in ("bq", "bk"):
                eng.wait_ge(sc_done, 3 * 2 * max(p - 1, MLA_PAIRS))
            if kind == "vt" and p >= 2:
                eng.wait_ge(pv_done, 2 * (p - 1))

        def item_split_act(act, it):
            if it is not None and split_at[it[:3]] is not None:
                split_hi(act, Chunk(split_at[it[:3]]), ukv(split_at[it[:3]]))

        def item_split_dve(dve, it):
            if it is not None and split_at[it[:3]] is not None:
                split_lo(dve, Chunk(split_at[it[:3]]))

        def item_act(act, it):
            if it is None:
                return
            kind, p, e, c, first, last = it
            if kind in ("mv", "bv"):
                return
            buffer_free(act, it)
            if kind == "vt":
                item_done(act, it)
                if p == 0:
                    act.wait_ge(v0_ready, 1)
                src = bank(item_bank(it)).rearrange("p (t h n) -> p t h n", t=TT, h=2)
                a, b = v_views(vh, p % 2)
                act.activation(a, src[:, :, 0, :], ACT.Copy)
                act.activation(b, src[:, :, 1, :], ACT.Copy).then_inc(pj_hi, 1)
                return
            (hi, _), rows = qk_dst(it)
            if kind == "mq":
                act.wait_ge(rp_done, head_of(it) + 2)
            else:
                act.wait_ge(pj_read, order[it[:3]] + 1)
            act.activation(hi, scaled_tile(it)[rows, :], ACT.Copy).then_inc(pj_hi, 1)

        def item_scale(dve, it, swap=True):
            if it is None or it[0] == "vt":
                return
            kind, p, e, c, first, last = it
            n = order[it[:3]]
            item_done(dve, it)
            if kind[0] == "m":
                rows = slice(0, {"mq": MLA_QH, "mk": HD, "mv": P}[kind])
                r = r_q if kind == "mq" else r_kv
                scale = MLA_SCALE if kind == "mq" else 1.0
            else:
                rows, r, scale = slice(0, P), r_pre, SCALE if kind == "bq" else 1.0
            vt_before = [i for i in items[:n] if i[0] == "vt"]
            if vt_before:
                dve.wait_ge(pj_mm, inner_order[vt_before[-1][:3]] + 1)
            for i in items[:n]:
                if i[0] != "vt" and tf_of[i[:3]] == tf_of[it[:3]] - 3 and i[:3] in lo_order:
                    dve.wait_ge(pj_lo, lo_order[i[:3]] + 1)
            nc.vector.scalar_tensor_tensor(scaled_tile(it)[rows, :], bank(item_bank(it))[rows, :], scale, r[rows, :],
                                           ALU.mult, ALU.mult).then_inc(pj_read, 1)
            if swap:
                item_swap(dve, it)

        def item_swap(dve, it):
            if it[0] == "mq":
                rope_rows_dve(dve, scaled_tile(it), head_of(it) + 1, (pj_read, order[it[:3]] + 1))

        def item_lo(dve, it):
            if it is None:
                return
            kind, p, e, c, first, last = it
            if kind in ("mv", "bv"):
                return
            dve.wait_ge(pj_hi, split_order[it[:3]] + 1)
            if kind == "vt":
                src = bank(item_bank(it)).rearrange("p (t h n) -> p t h n", t=TT, h=2)
                for x in range(2):
                    ins = nc.vector.tensor_tensor(v_views(vl, p % 2)[x], src[:, :, x, :],
                                                  v_views(vh, p % 2)[x].bitcast(F32), ALU.subtract)
                ins.then_inc(pj_read, 1)
                return
            (hi, lo), rows = qk_dst(it)
            nc.vector.tensor_tensor(lo, scaled_tile(it)[rows, :], hi.bitcast(F32), ALU.subtract).then_inc(pj_lo, 1)

        def item_pool(pool, it):
            if it is not None and it[0] == "mq":
                rope_rows_pool(pool, scaled_tile(it), head_of(it) + 1, (pj_read, order[it[:3]] + 1))

        lo_order = {}
        for it in items:
            if it[0] in ("mq", "mk", "bq", "bk"):
                lo_order[it[:3]] = len(lo_order)

        def scores_pe(pe, hh):
            p, e = hh // 2, hh % 2
            pe.wait_ge(pj_lo, 1 + max(lo_order[("mk", p, e)], lo_order[("mq", p, e)]) if p < MLA_PAIRS
                       else 1 + lo_order[("bk", p, 0)])
            if hh == 0:
                pe.wait_ge(kr_lo, 1)
            if hh:
                pe.wait_ge(sc_read, hh)
            if p < MLA_PAIRS:
                rows, b, (qh, ql, kh, kl) = slice(0, MLA_QH), hh % 3, mq
            else:
                rows, b, (qh, ql, kh, kl) = slice(HD * e, HD * e + HD), p % 2, bq
            for i in (3, 1, 2, 0):
                w, at, q = P * (i + 1), ROW_AT[i], slice(i * P, (i + 1) * P)
                mm = mm3(SC[:, at:at + w], qh[rows, b, q], ql[rows, b, q], kh[rows, b, 0:w], kl[rows, b, 0:w],
                         start=(i != 0), stop=True)
                if i != 2:
                    mm.then_inc(sc_done, 1)

        def scores_dve(dve, hh):
            b = hh % 2
            if hh >= 2:
                dve.wait_ge(pt_done, hh - 1)
            if hh < 2 * MLA_PAIRS:
                add = cmask[:, :]
                if hh == 0:
                    dve.wait_ge(v0_ready, 2)
                    dve.wait_ge(brow_out, 16)
            else:
                m = hh - 2 * MLA_PAIRS
                dve.wait_ge(bias_in[m % 2], 16 * (m // 2 + 1))
                add = bias[:, m % 2, :]
            for x, i in enumerate((3, 1, 2, 0)):
                w, at = P * (i + 1), ROW_AT[i]
                if x < 3:
                    dve.wait_ge(sc_done, 3 * hh + x + 1)
                ins = nc.vector.tensor_tensor_reduce(logits[:, b, at:at + w], SC[:, at:at + w], add[:, T - w:T], 1.0,
                                                     -3.0e38, ALU.add, ALU.max, mx[:, b, i:i + 1])
            ins.then_inc(sc_read, 1)
            dve.wait_ge(sc_read, hh + 1)
            nc.vector.tensor_scalar(nmx[:, b, :], mx[:, b, :], -1.0, None, ALU.mult).then_inc(mx_neg, 1)

        def exp_act(act, hh):
            b = hh % 2
            act.wait_ge(mx_neg, hh + 1)
            for i in (3, 1, 2, 0):
                w, at = P * (i + 1), ROW_AT[i]
                ins = act.activation(logits[:, b, at:at + w], logits[:, b, at:at + w], ACT.Exp,
                                     bias=nmx[:, b, i:i + 1], accum_out=den[:, b, i:i + 1])
            ins.then_inc(e_done, 1)

        def den_dve(dve, hh):
            dve.wait_ge(e_done, hh + 1)
            nc.vector.reciprocal(rden[:, hh % 2, :], den[:, hh % 2, :]).then_inc(den_inv, 1)

        def norm_act(act, hh):
            b = hh % 2
            act.wait_ge(den_inv, hh + 1)
            for i in (3, 1, 2, 0):
                w, at = P * (i + 1), ROW_AT[i]
                ins = act.activation(logits[:, b, at:at + w], logits[:, b, at:at + w], ACT.Copy,
                                     scale=rden[:, b, i:i + 1])
            ins.then_inc(p_done, 1)

        def probs_pe(pe, hh):
            pe.wait_ge(p_done, hh + 1)
            if hh == 0:
                pe.wait_ge(pj_read, 8)
            if hh:
                pe.wait_ge(pt_lo, hh)
            for j in range(TT):
                for i in range(j, TT):
                    mm = nc.tensor.transpose(PT[:, COL_AT[j] + (i - j) * P:COL_AT[j] + (i - j + 1) * P],
                                             logits[:, hh % 2, ROW_AT[i] + j * P:ROW_AT[i] + (j + 1) * P], ident[:, :])
            mm.then_inc(pt_done, 1)

        def probs_act(act, hh):
            act.wait_ge(pt_done, hh + 1)
            if hh:
                act.wait_ge(pv_done, hh)
            act.activation(pth[:, :], PT[:, 0:CW], ACT.Copy).then_inc(pt_hi, 1)

        def probs_dve(dve, hh):
            dve.wait_ge(pt_hi, hh + 1)
            nc.vector.tensor_tensor(ptl[:, :], PT[:, 0:CW], pth[:, :].bitcast(F32), ALU.subtract)\
                .then_inc(pt_lo, 1)

        def values(out_bank, v, buf, e, xh, xl):
            for j in range(TT):
                w, at, cols = T - P * j, COL_AT[j], slice(HD * e, HD * e + P)
                mm = mm3(out_bank[:, P * j:T], v[0][:, buf, j, cols], v[1][:, buf, j, cols],
                         xh[:, at:at + w], xl[:, at:at + w], start=(e == 0 and j == 0), stop=(e == 1 and j == TT - 1))
            return mm

        def pv_pe(pe, hh):
            p, e = hh // 2, hh % 2
            pe.wait_ge(pt_lo, hh + 1)
            if e == 0:
                pe.wait_ge(pj_read, order[("vt", p, 0)] + 1)
                if p:
                    pe.wait_ge(o_lo, p)
            values(bank(O_BANK), (vh, vl), p % 2, e, pth, ptl).then_inc(pv_done, 1)

        def out0_at(k):
            return oh[k], ol[k]

        def o_act(act, p):
            act.wait_ge(pv_done, 2 * p + 2)
            act.activation(oh[p], bank(O_BANK), ACT.Copy).then_inc(o_hi, 1)

        def o_dve(dve, p):
            dve.wait_ge(o_hi, p + 1)
            nc.vector.tensor_tensor(ol[p], bank(O_BANK), oh[p].bitcast(F32), ALU.subtract).then_inc(o_lo, 1)

        def sb_bank(p, j):
            return {(0, 0): 6, (0, 1): 7, (0, 2): 5, (1, 0): 4, (1, 1): 3}.get((p, j), P_BANK) \
                if isinstance(p, int) else P_BANK

        def sb_item_pe(pe, p, par, j):
            if sb_bank(p, j) == P_BANK:
                pe.wait_ge(qj_read, p * 4 + j)
            if j < 3:
                c = sb_chunk(p, j)
                pe.wait_ge(w_lo, c.n + 1)
                project(pe, bank(sb_bank(p, j)), c, KD, P, 0, P, uh, ul).then_inc(w_used, 1)
            else:
                tb = tf_sb(par, 2)
                for t in range(TT):
                    mm = nc.tensor.transpose(bank(P_BANK)[:, t * P:(t + 1) * P], tf[:, tb, t * P:(t + 1) * P],
                                             ident[:, :])
                mm.then_inc(qj_mm, 1)

        def tf_sb(par, j):
            return (par * 3 + j) % 2

        def sb_chunk(p, j):
            c = Chunk(CH_SB + j)
            c.turn, c.n = c.turn + p, c.n + p * 3
            return c

        def sb_split_act(act, p, j):
            split_hi(act, sb_chunk(p, j + AHEAD))

        def sb_split_dve(dve, p, j):
            split_lo(dve, sb_chunk(p, j + AHEAD))

        def sb_item_act(act, p, par, j):
            if j == 3:
                act.wait_ge(qj_mm, p + 1)
                if not isinstance(p, int) or p >= 2:
                    act.wait_ge(sv_done, 2 * p - 2)
                elif p == 0:
                    act.wait_ge(v1_ready, 1)
                src = bank(P_BANK).rearrange("p (t h n) -> p t h n", t=TT, h=2)
                a, b = v_views(sv[0], par)
                act.activation(a, src[:, :, 0, :], ACT.Copy)
                act.activation(b, src[:, :, 1, :], ACT.Copy).then_inc(qj_hi, 1)
                return
            act.wait_ge(qj_read, p * 4 + j + 1)
            if not isinstance(p, int) or p >= 2:
                act.wait_ge(z_done, 2 * p - 2)
            act.activation(sq[2 * j][:, par, :], tf[:, tf_sb(par, j), :], ACT.Copy).then_inc(qj_hi, 1)

        def sb_scale(dve, p, par, j):
            dve.wait_ge(w_used, sb_chunk(p, j).n + 1)
            if not (isinstance(p, int) and p == 0):
                dve.wait_ge(qj_mm, p)
            b = sb_bank(p, j)
            nc.vector.scalar_tensor_tensor(tf[:, tf_sb(par, j), :], bank(b), -SCALE if j == 0 else 1.0,
                                           r_pre[:, :], ALU.mult, ALU.mult).then_inc(qj_read, 1)

        def sb_item_dve(dve, p, par, j):
            if j < 2:
                dve.wait_ge(qj_hi, p * 3 + j + 1)
                nc.vector.tensor_tensor(sq[2 * j + 1][:, par, :], tf[:, tf_sb(par, j), :],
                                        sq[2 * j][:, par, :].bitcast(F32), ALU.subtract).then_inc(qj_lo, 1)
                return
            dve.wait_ge(qj_hi, p * 3 + 3)
            src = bank(P_BANK).rearrange("p (t h n) -> p t h n", t=TT, h=2)
            for x in range(2):
                ins = nc.vector.tensor_tensor(v_views(sv[1], par)[x], src[:, :, x, :],
                                              v_views(sv[0], par)[x].bitcast(F32), ALU.subtract)
            ins.then_inc(qj_read, 1)

        def z_pe(pe, p, par, e):
            hh = p * 2 + e
            pe.wait_ge(qj_lo, p * 2 + 2)
            if not (isinstance(p, int) and hh < 2):
                pe.wait_ge(w_exp, hh - 1)
            rows = slice(HD * e, HD * e + HD)
            Z = ZB[e]
            for j in (0, 1, 3, 2):
                w, at = T - P * j, COL_AT[j]
                k = slice(j * P, (j + 1) * P)
                mm3(Z[:, at:at + w], sq[2][rows, par, k], sq[3][rows, par, k],
                    sq[0][rows, par, P * j:T], sq[1][rows, par, P * j:T], start=(j != 3), stop=False)
                mm = nc.tensor.matmul(Z[:, at:at + P], identb[:, :], big[:, :], start=False, stop=False,
                                      skip_group_check=True)
            mm.then_inc(z_done, 1)

        def z_act_exp(act, p, e):
            hh = p * 2 + e
            act.wait_ge(z_done, hh + 1)
            if not (isinstance(p, int) and hh == 0):
                act.wait_ge(ns_lo, hh)
            act.activation(lsp[:, :], ZB[e][:, 0:CW], ACT.Exp, scale=-1.0).then_inc(z_exp, 1)

        def z_dve_clamp(dve, p, e):
            dve.wait_ge(z_exp, p * 2 + e + 1)
            nc.vector.tensor_scalar(lsp[:, :], lsp[:, :], 1e17, None, ALU.min).then_inc(z_min, 1)

        def z_act_ln(act, p, e):
            act.wait_ge(z_min, p * 2 + e + 1)
            act.activation(lsp[:, :], lsp[:, :], ACT.Ln, bias=1.0).then_inc(z_ln, 1)

        def z_dve(dve, p, e):
            hh = p * 2 + e
            dve.wait_ge(z_ln, hh + 1)
            nc.vector.scalar_tensor_tensor(lsp[:, :], lsp[:, :], -1.0, ZB[e][:, 0:CW], ALU.mult, ALU.min)\
                .then_inc(ns_f, 1)

        def ns_dve_hi(dve, p, e, first=False):
            hh = p * 2 + e
            dve.wait_ge(ns_f, hh + 1)
            if not first:
                dve.wait_ge(c_done, hh)
            nc.vector.tensor_copy(nsh[:, :], lsp[:, :]).then_inc(ns_hi, 1)

        def ns_dve_lo(dve, p, e):
            dve.wait_ge(ns_hi, p * 2 + e + 1)
            nc.vector.tensor_tensor(nsl[:, :], lsp[:, :], nsh[:, :].bitcast(F32), ALU.subtract).then_inc(ns_lo, 1)

        def c_pe(pe, p, e):
            hh = p * 2 + e
            pe.wait_ge(ns_lo, hh + 1)
            Z = ZB[e]
            for j in range(TT):
                for jj in range(j, TT):
                    at, w = COL_AT[j] + (jj - j) * P, T - P * jj
                    lt = negtri if jj == j else negones
                    for n in (nsh, nsl):
                        mm = nc.tensor.matmul(Z[:, at:at + w], lt[:, :], n[:, COL_AT[jj]:COL_AT[jj] + w],
                                              start=False, stop=False, skip_group_check=True)
            mm.then_inc(c_done, 1)

        def w_act(act, p, e, first=False):
            hh = p * 2 + e
            act.wait_ge(c_done, hh + 1)
            if not first:
                act.wait_ge(sw_lo, hh)
            act.activation(wf[:, :], ZB[e][:, 0:CW], ACT.Exp, scale=-1.0).then_inc(w_exp, 1)

        def w_dve(dve, p, e, first=False):
            hh = p * 2 + e
            dve.wait_ge(w_exp, hh + 1)
            if not first:
                dve.wait_ge(sv_done, hh - 1)
            nc.vector.tensor_copy(swh[:, e, :], wf[:, :]).then_inc(sw_hi, 1)

        def w_pool(pool, p, e):
            pool.wait_ge(sw_hi, p * 2 + e + 1)
            nc.gpsimd.tensor_tensor(swl[:, e, :], wf[:, :], swh[:, e, :].bitcast(F32), ALU.subtract)\
                .then_inc(sw_lo, 1)

        def sb_pv_pe(pe, p, par, e):
            hh = p * 2 + e
            pe.wait_ge(sw_lo, hh + 1)
            if e == 0:
                pe.wait_ge(qj_read, p * 4 + 4)
                if not (isinstance(p, int) and p == 0):
                    pe.wait_ge(so_lo_s, p)
            values(bank(O_BANK), sv, par, e, swh[:, e, :], swl[:, e, :]).then_inc(sv_done, 1)

        def sb_o_act(act, p):
            act.wait_ge(sv_done, p * 2 + 2)
            o = soh[:, p, :] if isinstance(p, int) else soh[:, bass.ds(p, 1), :]
            act.activation(o, bank(O_BANK), ACT.Copy).then_inc(so_hi_s, 1)

        def sb_o_dve(dve, p):
            dve.wait_ge(so_hi_s, p + 1)
            h = soh[:, p, :] if isinstance(p, int) else soh[:, bass.ds(p, 1), :]
            o = sol[:, p, :] if isinstance(p, int) else sol[:, bass.ds(p, 1), :]
            nc.vector.tensor_tensor(o, bank(O_BANK), h.bitcast(F32), ALU.subtract).then_inc(so_lo_s, 1)

        def out1_at(k):
            return soh[:, k, :], sol[:, k, :]

        def sb_pair_pe(pe, p, par, first=False, last=False):
            q = 1 - par
            if first:
                pe.wait_ge(qj_read, 6)
            elif not last:
                sb_item_pe(pe, p + 1, q, 0)
            z_pe(pe, p, par, 1)
            if last:
                pe.wait_ge(qj_read, 4 * SB_PAIRS)
                out_part(pe, CH_OUT1, 0, out1_at, 0, 6)
            if first:
                sb_item_pe(pe, p + 1, q, 2)
            c_pe(pe, p, 0)
            if not last and not first:
                sb_item_pe(pe, p + 1, q, 1)
            if not first:
                sb_pv_pe(pe, p - 1, q, 1)
            if last:
                pe.wait_ge(w_exp, 2 * SB_PAIRS - 1)
                out_part(pe, CH_OUT1, 1, out1_at, 0, 6)
            if not last and not first:
                sb_item_pe(pe, p + 1, q, 2)
            if not last:
                z_pe(pe, p + 1, q, 0)
            c_pe(pe, p, 1)
            if not last:
                sb_item_pe(pe, p + 1, q, 3)
            sb_pv_pe(pe, p, par, 0)
            if last:
                out_part(pe, CH_OUT1, 2, out1_at, 0, 4)

        def sb_pair_act(act, p, par, first=False, last=False):
            q = 1 - par
            if not last and not first:
                sb_split_act(act, p + 1, 0)
                sb_item_act(act, p + 1, q, 0)
            z_act_exp(act, p, 1)
            z_act_ln(act, p, 1)
            w_act(act, p, 0, first)
            if not last:
                sb_split_act(act, p + 1, 1)
                if not first:
                    sb_item_act(act, p + 1, q, 1)
            if not first:
                sb_o_act(act, p - 1)
            if last:
                split_hi(act, Chunk(CH_OUT1 + AHEAD))
            if not last:
                sb_split_act(act, p + 1, 2)
                z_act_exp(act, p + 1, 0)
                z_act_ln(act, p + 1, 0)
                sb_item_act(act, p + 1, q, 3)
            w_act(act, p, 1)

        def sb_pair_dve(dve, p, par, first=False, last=False):
            q = 1 - par
            if not last and not first:
                sb_scale(dve, p + 1, q, 0)
                sb_item_dve(dve, p + 1, q, 0)
                sb_split_dve(dve, p + 1, 0)
            z_dve_clamp(dve, p, 1)
            z_dve(dve, p, 1)
            ns_dve_hi(dve, p, 1)
            w_dve(dve, p, 0, first)
            ns_dve_lo(dve, p, 1)
            if not last and not first:
                sb_scale(dve, p + 1, q, 1)
                sb_item_dve(dve, p + 1, q, 1)
            if not first:
                sb_o_dve(dve, p - 1)
            if last:
                split_lo(dve, Chunk(CH_OUT1 + AHEAD))
            if not last:
                sb_split_dve(dve, p + 1, 1)
                sb_split_dve(dve, p + 1, 2)
                sb_scale(dve, p + 1, q, 2)
                z_dve_clamp(dve, p + 1, 0)
                sb_item_dve(dve, p + 1, q, 3)
                z_dve(dve, p + 1, 0)
                ns_dve_hi(dve, p + 1, 0)
                ns_dve_lo(dve, p + 1, 0)
            w_dve(dve, p, 1, first)

        def sb_turns(eng, pair):
            pair(eng, 0, 0, first=True)
            with eng.Fori(0, (SB_PAIRS - 2) // 2) as i:
                pair(eng, i * 2 + 1, 1)
                pair(eng, i * 2 + 2, 0)
            pair(eng, SB_PAIRS - 1, 1, last=True)

        block = ctx.enter_context(nc.Block())

        @block.sync
        def _(sp):
            def load_in(n):
                at, cols = IN_TILES[n]
                load(sp, Chunk(CH_IN + n), ab_w_in[0][:, at:at + cols], KD, cols, P)
            load_in(0)
            for t in range(TT):
                sp.dma_start(xt[:, t, :], x[0, t * P:(t + 1) * P, :]).then_inc(x_in[t], 16)
            load_in(1)
            sp.dma_start(hot[:, :], onehot_d).then_inc(bias_in_sbuf, 16)
            sp.dma_start(rb[0:NBUCKET, :], rel_bias).then_inc(bias_in_sbuf, 16)
            for n in range(2, len(IN_TILES)):
                load_in(n)
            sp.wait_ge(brow_sb, 1)
            sp.dma_start(bias_t.ap(), brow.unsqueeze(1).to_broadcast([8, P, 640])).then_inc(brow_out, 16)
            sp.wait_ge(brow_mm, 1)
            sp.wait_ge(h_ready, KD)
            sp.wait_ge(ssx_ready, TT)
            sp.dma_start(cs[ROPE_ROWS, :, :], rope_d.rearrange("a r t -> r a t")).then_inc(tables_in, 16)
            for p in range(MLA_PAIRS):
                load(sp, Chunk(CH_MLA + 2 * p), mla_w_uq[0][:, 2 * p * MLA_QH:2 * (p + 1) * MLA_QH], KQ, 2 * MLA_QH)
                c = Chunk(CH_MLA + 2 * p + 1)
                sp.wait_ge(w_lo, c.n - NSLOT + 1)
                for kv in range(2):
                    for h in range(2):
                        at = (2 * p + h) * 2 * HD + kv * HD
                        dst = raw[:, c.slot, kv * KKV * P:(kv + 1) * KKV * P].rearrange("p (k h n) -> p k h n", k=KKV, h=2)
                        sp.dma_start(dst[:, :, h, :], mla_w_ukv[0][:, at:at + HD].rearrange("(k p) n -> p k n", p=P))\
                            .then_inc(ukv_in[p % 2] if 2 * kv + h < 3 else raw_in[c.slot], 16)
            for m in range(MOBA_PAIRS):
                for j in range(3):
                    load(sp, Chunk(CH_MOBA + 3 * m + j),
                         ab_w_in[0][:, O3 + 512 * j + P * m:O3 + 512 * j + P * (m + 1)], KD, P)
            out_sp(sp, CH_OUT0, ab_w_out[0])
            gu_sp(sp, CH_GU0, ffn_w_gate_up[0])
            dn_sp(sp, CH_DN0, ffn_w_down[0])
            with sp.Fori(0, SB_PAIRS) as p:
                for j in range(3):
                    load(sp, sb_chunk(p, j), sb_w_qkv[0][:, bass.ds(p * P + D * j, P)], KD, P)
            out_sp(sp, CH_OUT1, sb_w_out[0])
            gu_sp(sp, CH_GU1, ffn_w_gate_up[1])
            last_sp(sp, ffn_w_down[1])
            for t in range(TT):
                sp.wait_ge(y_even, t + 1)
                sp.wait_ge(y_odd, t + 1)
                sp.dma_start(out[0, t * P:(t + 1) * P, :], two_banks(y_tok, t)).then_inc(y_out, 16)
            sp.wait_ge(y_out, 16 * TT)
            sp.wait_ge(brow_out, 16)

        @block.gpsimd
        def _(pool):
            nc.gpsimd.memset(ones[:, :], 1.0).then_inc(tri_ready, 1)
            pool.wait_ge(tri_ready, 1)
            nc.gpsimd.memset(eps_t[:, :], EPS).then_inc(tri_ready, 1)
            pool.wait_ge(tri_ready, 2)
            nc.gpsimd.memset(rb[NBUCKET:NBUCKET + 1, :], NEG).then_inc(tri_ready, 1)
            pool.wait_ge(tri_ready, 3)
            nc.gpsimd.affine_select(out=ident[:, :], in_=ones[:, :], compare_op=ALU.is_equal, fill=0.0, base=0,
                                    pattern=[[-1, P]], channel_multiplier=1).then_inc(consts_ready, 1)
            nc.gpsimd.affine_select(out=tri_f[:, :], in_=ones[:, :], compare_op=ALU.is_ge, fill=0.0, base=0,
                                    pattern=[[-1, P]], channel_multiplier=1).then_inc(consts_ready, 1)
            pool.wait_ge(consts_ready, 2)
            for v in (vh, vl):
                nc.gpsimd.memset(v[:, :, :, HD:2 * HD].bitcast(F32), 0.0)
            pool.wait_ge(h_ready, KD)
            pool.wait_ge(ssx_ready, TT)
            pool.wait_ge(brow_mm, 1)
            nc.gpsimd.memset(cmask[:, :], 0.0).then_inc(v0_ready, 1)
            pool.wait_ge(v0_ready, 1)
            nc.gpsimd.affine_select(out=cmask[:, :], in_=cmask[:, :], compare_op=ALU.is_ge, fill=NEG, base=T - P,
                                    pattern=[[-1, T]], channel_multiplier=1).then_inc(v0_ready, 1)
            for n in (1, 2):
                add_squares(pool, n, N_CQ)
            add_squares(pool, 1, N_CKV)
            pool.wait_ge(tables_in, 16)
            pool.wait_ge(sq_added, AD0[N_CKV + 1])
            rope_rows_pool(pool, tf[:, 1, :], 0, (in_scaled, 6))
            for it in items[0:8]:
                item_pool(pool, it)

            def load_bias(m):
                if m >= 2:
                    pool.wait_ge(sc_read, 2 * MLA_PAIRS + m - 1)
                else:
                    pool.wait_ge(sc_done, 3 * 2 * MLA_PAIRS)
                skewed = bass.AP(tensor=bias_t, offset=640 * P * m + P - 1, ap=[[640 - 1, P], [1, T]])
                pool.dma_start(bias[:, m % 2, :], skewed).then_inc(bias_in[m % 2], 16)

            for hh in range(NH0):
                for it in slots_of_step(hh):
                    item_pool(pool, it)
                if hh == 2 * MLA_PAIRS - 3:
                    load_bias(0)
                    load_bias(1)
                elif 2 * MLA_PAIRS - 3 < hh < NH0 - 4:
                    load_bias(hh - 2 * MLA_PAIRS + 4)
            pool.wait_ge(rp_done, 2 * MLA_PAIRS + 1)
            f_adds(pool, 0, N_POST_A0)
            res_pool(pool, 0)
            gu_pool(pool, 0)
            f_adds(pool, 1, N_POST_F0)
            res_pool(pool, 1)
            for v in sv:
                ins = nc.gpsimd.memset(v[:, :, :, HD:2 * HD].bitcast(F32), 0.0)
            ins.then_inc(v1_ready, 1)

            def pair(pool, p, par, first=False, last=False):
                w_pool(pool, p, 0)
                w_pool(pool, p, 1)
            sb_turns(pool, pair)
            f_adds(pool, 2, N_POST_A1)
            res_pool(pool, 2)
            gu_pool(pool, 1)
            last_pool(pool)

        @block.scalar
        def _(act):
            for g, r0, n in ((mix_pre_g, G_MIX_PRE, 16), (mix_post_g, G_MIX_POST, 16), (ffn_pre_g, G_FFN_PRE, 16),
                             (ffn_post_g, G_FFN_POST, 16), (mla_q_norm_g, G_Q, KQ), (mla_kv_norm_g, G_KV, KKV)):
                act.dma_start(graw[r0:r0 + n, :], g.rearrange("l (k p) -> (l k) p", p=P)).then_inc(gains_in, 16)
            split_hi(act, Chunk(0))
            act.wait_ge(gains_ready, 1)
            for k in range(KD):
                act.wait_ge(h_ready, k + 1)
                act.activation(uh[:, k, :], hT[:, k, :], ACT.Copy, scale=gains[:, k:k + 1]).then_inc(uh_ready, 1)
                if k in (1, KD - 1):
                    split_hi(act, Chunk(1 if k == 1 else 2))
            for t in range(TT):
                act.wait_ge(x_in[t], 16)
                if t:
                    act.wait_ge(ssx_ready, t)
                act.activation(junk[:, :], xt[:, t, :], ACT.Square, accum_out=ssx[:, t:t + 1]).then_inc(ssx_ready, 1)
                if t == 1:
                    split_hi(act, Chunk(3))
            act.wait_ge(consts_ready, 2)
            act.activation(negtri[:, :], tri_f[:, :], ACT.Copy, scale=-1.0)
            act.activation(negones[:, :], ones[:, :], ACT.Copy, scale=-1.0)
            act.activation(identb[:, :], ident[:, :], ACT.Copy)
            act.activation(big[:, :], tri_f[:, :], ACT.Copy, scale=-NEG).then_inc(tri_r_ready, 1)
            stat_act(act, N_X, None, D)
            split_hi(act, Chunk(4))
            split_hi(act, Chunk(5))
            for n in range(len(IN_TILES)):
                if n > 3:
                    split_hi(act, Chunk(CH_IN + n + AHEAD), ukv(CH_IN + n + AHEAD))
                if n == len(IN_TILES) - 1:
                    break
                hi, _, m = lat_dst[n]
                k, first = lat_norm[n]
                if n == KQ + 1:
                    stat_act(act, N_CQ, 6, QL)
                act.wait_ge(in_scaled, n + 1)
                if n == 0:
                    act.wait_ge(brow_mm, 1)
                act.activation(hi[:, m, :], tf[:, n % 2, :], ACT.Copy,
                               scale=gains[:, lat_gain[n]:lat_gain[n] + 1]).then_inc(lat_hi, 1)
                square(act, tf[:, n % 2, :], first, k)
            stat_act(act, N_CKV, 6, KVL)
            act.wait_ge(rp_done, 1)
            for b in range(3):
                ins = act.activation(mq[2][ROPE_ROWS, b, :], tf[ROPE_ROWS, 1, :], ACT.Copy)
            ins.then_inc(kr_hi, 1)
            load_functions(act, EXP_SET)
            for n, it in enumerate(items[0:6]):
                item_act(act, it)
                item_split_act(act, it)
                if n == 3:
                    exp_act(act, 0)
            norm_act(act, 0)
            exp_act(act, 1)
            before = items[6:8]
            for hh in range(NH0):
                a, b, c = slots_of_step(hh)
                for it in before:
                    item_act(act, it)
                if hh % 2:
                    item_act(act, a)
                probs_act(act, hh)
                if hh % 2:
                    item_split_act(act, a)
                if hh + 1 < NH0:
                    norm_act(act, hh + 1)
                if hh % 2 == 0:
                    item_split_act(act, a)
                if hh + 2 < NH0:
                    exp_act(act, hh + 2)
                if hh % 2 == 0:
                    item_act(act, a)
                    item_act(act, b)
                item_split_act(act, b)
                item_split_act(act, c)
                before = (b, c) if hh % 2 else ()
                if hh == NH0 - 2:
                    split_hi(act, Chunk(CH_OUT0 + AHEAD))
                if hh % 2:
                    o_act(act, hh // 2)
            out_act(act, CH_OUT0, N_POST_A0)
            stat_act(act, N_POST_A0, 0, D)
            res_act(act, 0, N_POST_A0, G_FFN_PRE, CH_GU0)
            gu_act(act, CH_GU0, 0, N_FFN0)
            dn_act(act, CH_DN0, N_POST_F0)
            stat_act(act, N_POST_F0, 0, D)
            res_act(act, 1, N_POST_F0, G_MIX_PRE + KD, CH_SB)
            stat_act(act, N_SB, 0, D)
            load_functions(act, EXP_LN_SET)
            sb_split_act(act, 1, 0)
            sb_item_act(act, 0, 0, 0)
            sb_item_act(act, 0, 0, 1)
            z_act_exp(act, 0, 0)
            sb_item_act(act, 0, 0, 3)
            z_act_ln(act, 0, 0)
            sb_item_act(act, 1, 1, 0)
            sb_item_act(act, 1, 1, 1)
            sb_turns(act, sb_pair_act)
            sb_o_act(act, SB_PAIRS - 1)
            out_act(act, CH_OUT1, N_POST_A1)
            stat_act(act, N_POST_A1, 0, D)
            res_act(act, 2, N_POST_A1, G_FFN_PRE + KD, CH_GU1)
            gu_act(act, CH_GU1, 1, N_FFN1)
            last_act(act)

        @block.vector
        def _(dve):
            split_lo(dve, Chunk(0))
            dve.wait_ge(x_tr, 1)
            nc.vector.tensor_copy(hT[:, 0, :], bank(0)).then_inc(h_ready, 1)
            dve.wait_ge(gains_tr, 1)
            nc.vector.tensor_copy(gains[:, :], bank(7)[:, 0:G_ROWS]).then_inc(gains_ready, 1)
            dve.wait_ge(gains_ready, 1)
            for k in range(KD + 1):
                if 0 < k < KD:
                    dve.wait_ge(x_tr, k + 1)
                    nc.vector.tensor_copy(hT[:, k, :], bank(k)).then_inc(h_ready, 1)
                if k:
                    m = k - 1
                    dve.wait_ge(uh_ready, m + 1)
                    nc.vector.scalar_tensor_tensor(ul[:, m, :], hT[:, m, :], gains[:, m:m + 1],
                                                   uh[:, m, :].bitcast(F32), ALU.mult, ALU.subtract)\
                        .then_inc(u_ready, 1)
                if k == 2:
                    split_lo(dve, Chunk(1))
            split_lo(dve, Chunk(2))
            dve.wait_ge(brow_mm, 1)
            nc.vector.tensor_copy(logits[0:8, 0, 0:T], bank(6)[0:8, :])
            nc.vector.tensor_copy(logits[0:8, 0, T:640], bank(7)[0:8, 0:640 - T]).then_inc(brow_sb, 1)
            split_lo(dve, Chunk(3))
            stat_dve(dve, N_X, 5, None)
            split_lo(dve, Chunk(4))
            stat_copy_dve(dve, N_X, 5, r_pre)
            dve.wait_ge(st_r, 1)
            for n in range(len(IN_TILES)):
                if n == 1:
                    split_lo(dve, Chunk(5))
                if n > 3:
                    split_lo(dve, Chunk(CH_IN + n + AHEAD))
                dve.wait_ge(w_used, CH_IN + n + 1)
                rows = slice(0, P) if n < 5 else ROPE_ROWS
                if 2 <= n:
                    m = n - 2
                    k, j = lat_norm[m]
                    dve.wait_ge(sq_ready, SQ0[k] + j + 1)
                nc.vector.tensor_tensor(tf[rows, n % 2, :], bank(n)[rows, :], r_pre[rows, :], ALU.mult)\
                    .then_inc(in_scaled, 1)
                if n < 5:
                    hi, lo, m = lat_dst[n]
                    if n == KQ + 1:
                        stat_dve(dve, N_CQ, 6, None)
                    dve.wait_ge(lat_hi, n + 1)
                    nc.vector.scalar_tensor_tensor(lo[:, m, :], tf[:, n % 2, :],
                                                   gains[:, lat_gain[n]:lat_gain[n] + 1],
                                                   hi[:, m, :].bitcast(F32), ALU.mult, ALU.subtract)\
                        .then_inc(lat_ready, 1)
            dve.wait_ge(tables_in, 16)
            rope_rows_dve(dve, tf[:, 1, :], 0, (in_scaled, 6))
            stat_copy_dve(dve, N_CQ, 6, r_q)
            dve.wait_ge(st_r, 2)
            item_scale(dve, items[0], False)
            stat_dve(dve, N_CKV, 6, r_kv)
            dve.wait_ge(st_r, 3)
            item_swap(dve, items[0])
            item_scale(dve, items[1])
            dve.wait_ge(kr_hi, 1)
            for b in range(3):
                ins = nc.vector.tensor_tensor(mq[3][ROPE_ROWS, b, :], tf[ROPE_ROWS, 1, :],
                                              mq[2][ROPE_ROWS, b, :].bitcast(F32), ALU.subtract)
            ins.then_inc(kr_lo, 1)
            for n in (0, 2, 4):
                if n == 2:
                    for it in items[2:5]:
                        item_scale(dve, it)
                    scores_dve(dve, 0)
                for it in items[n:n + 2]:
                    item_lo(dve, it)
                if n == 4:
                    den_dve(dve, 0)
                for it in items[n:n + 2]:
                    item_split_dve(dve, it)
            scores_dve(dve, 1)
            for it in items[6:8]:
                item_scale(dve, it)
            before = items[6:8]
            for hh in range(NH0):
                a, b, c = slots_of_step(hh)
                for it in before:
                    item_lo(dve, it)
                if hh % 2:
                    item_lo(dve, a)
                if hh + 1 < NH0:
                    den_dve(dve, hh + 1)
                probs_dve(dve, hh)
                if hh % 2:
                    item_split_dve(dve, a)
                else:
                    if hh:
                        o_dve(dve, hh // 2 - 1)
                    item_split_dve(dve, a)
                    item_scale(dve, a)
                if hh + 2 < NH0:
                    scores_dve(dve, hh + 2)
                item_scale(dve, b)
                item_scale(dve, c)
                if hh % 2 == 0:
                    item_lo(dve, a)
                    item_lo(dve, b)
                item_split_dve(dve, b)
                item_split_dve(dve, c)
                before = (b, c) if hh % 2 else ()
                if hh == NH0 - 2:
                    split_lo(dve, Chunk(CH_OUT0 + AHEAD))
            o_dve(dve, NH0 // 2 - 1)
            out_dve(dve, CH_OUT0)
            res_dve(dve, 0, N_POST_A0, G_MIX_POST, G_FFN_PRE, CH_GU0)
            gu_dve(dve, CH_GU0, 0, N_FFN0)
            dn_dve(dve, CH_DN0)
            res_dve(dve, 1, N_POST_F0, G_FFN_POST, G_MIX_PRE + KD, CH_SB)
            stat_dve(dve, N_SB, 0, None)
            sb_split_dve(dve, 1, 0)
            stat_copy_dve(dve, N_SB, 0, r_pre)
            dve.wait_ge(st_r, N_SB + 1)
            sb_scale(dve, 0, 0, 0)
            sb_scale(dve, 0, 0, 1)
            sb_item_dve(dve, 0, 0, 0)
            sb_item_dve(dve, 0, 0, 1)
            dve.wait_ge(qj_lo, 1)
            sb_scale(dve, 0, 0, 2)
            z_dve_clamp(dve, 0, 0)
            sb_item_dve(dve, 0, 0, 3)
            sb_scale(dve, 1, 1, 0)
            sb_scale(dve, 1, 1, 1)
            z_dve(dve, 0, 0)
            ns_dve_hi(dve, 0, 0, True)
            ns_dve_lo(dve, 0, 0)
            sb_item_dve(dve, 1, 1, 0)
            sb_item_dve(dve, 1, 1, 1)
            sb_turns(dve, sb_pair_dve)
            sb_o_dve(dve, SB_PAIRS - 1)
            out_dve(dve, CH_OUT1)
            res_dve(dve, 2, N_POST_A1, G_MIX_POST + KD, G_FFN_PRE + KD, CH_GU1)
            gu_dve(dve, CH_GU1, 1, N_FFN1)
            last_dve(dve)

        @block.tensor
        def _(pe):
            pe.wait_ge(consts_ready, 1)
            for t in range(TT):
                pe.wait_ge(x_in[t], 16)
                for k in range(KD - 1):
                    mm = nc.tensor.transpose(bank(k)[:, t * P:(t + 1) * P], xt[:, t, k * P:(k + 1) * P], ident[:, :])
                    if t == TT - 1:
                        mm.then_inc(x_tr, 1)
            pe.wait_ge(gains_in, 16 * 6)
            nc.tensor.transpose(bank(7)[:, 0:G_ROWS], graw[:, :], ident[0:G_ROWS, 0:G_ROWS]).then_inc(gains_tr, 1)
            pe.wait_ge(gains_ready, 1)
            for t in range(TT):
                mm = nc.tensor.transpose(bank(7)[:, t * P:(t + 1) * P], xt[:, t, (KD - 1) * P:], ident[:, :])
            mm.then_inc(x_tr, 1)
            pe.wait_ge(h_ready, 2)
            two_products(pe, Chunk(CH_IN), 0, 1, 0, 0)
            pe.wait_ge(bias_in_sbuf, 32)
            nc.tensor.matmul(bank(6)[0:8, :], rb[:, :], hot[:, 0:T], start=True, stop=True)
            nc.tensor.matmul(bank(7)[0:8, 0:640 - T], rb[:, :], hot[:, T:640], start=True, stop=True)\
                .then_inc(brow_mm, 1)
            for n in range(2, len(IN_TILES)):
                cols = IN_TILES[n][1]
                c = Chunk(CH_IN + n)
                pe.wait_ge(w_lo, c.n + 1)
                project(pe, bank(n)[0:cols, :], c, KD, P, 0, cols, uh, ul).then_inc(w_used, 1)
                if n == 2:
                    spread_pe(pe, N_X, 5)
                if n == 4:
                    pe.wait_ge(brow_sb, 1)
                    pe.wait_ge(st_r, 1)
                    stat_pe(pe, N_CQ, 6, AD0[N_CKV])
            spread_pe(pe, N_CQ, 6)
            pe.wait_ge(lat_ready, 3)
            item_pe(pe, items[0])
            pe.wait_ge(st_r, N_CQ + 1)
            stat_pe(pe, N_CKV, 6, AD0[N_CKV + 1])
            pe.wait_ge(lat_ready, 5)
            item_pe(pe, items[1])
            spread_pe(pe, N_CKV, 6)
            for n in range(2, 8):
                item_pe(pe, items[n])
                if n == 4:
                    scores_pe(pe, 0)
                if n == 5:
                    scores_pe(pe, 1)
            for hh in range(NH0):
                a, b, c = slots_of_step(hh)
                probs_pe(pe, hh)
                item_pe(pe, a)
                if hh + 2 < NH0:
                    scores_pe(pe, hh + 2)
                item_pe(pe, b)
                if hh == NH0 - 3:
                    pe.wait_ge(pj_read, len(items))
                    out_part(pe, CH_OUT0, 0, out0_at, 0, 6)
                elif hh == NH0 - 2:
                    pe.wait_ge(sc_read, NH0)
                    out_part(pe, CH_OUT0, 1, out0_at, 0, 6)
                elif hh == NH0 - 1:
                    out_part(pe, CH_OUT0, 2, out0_at, 0, 4)
                pv_pe(pe, hh)
                item_pe(pe, c)
            pe.wait_ge(o_lo, NH0 // 2 - 1)
            for n in range(3):
                out_part(pe, CH_OUT0, n, out0_at, *((6, 7) if n < 2 else (4, 5)))
            out_pe(pe, CH_OUT0, 0, out0_at, (o_lo, MLA_PAIRS + MOBA_PAIRS), (7, 7, 5))
            stat_pe(pe, N_POST_A0, 0, AD0[N_POST_A0 + 1], 1)
            spread_pe(pe, N_POST_A0, 0)
            gu_pe(pe, CH_GU0, 0, N_FFN0)
            dn_pe(pe, CH_DN0, 1, 0)
            stat_pe(pe, N_POST_F0, 0, AD0[N_POST_F0 + 1], 2)
            spread_pe(pe, N_POST_F0, 0)
            pe.wait_ge(tri_r_ready, 1)
            two_products(pe, Chunk(CH_SB), 6, 7, 2 * KD, N_SB)
            sb_item_pe(pe, 0, 0, 2)
            stat_pe(pe, N_SB, 0, AD0[N_SB + 1])
            sb_item_pe(pe, 1, 1, 0)
            spread_pe(pe, N_SB, 0)
            sb_item_pe(pe, 1, 1, 1)
            pe.wait_ge(st_r, N_SB + 1)
            z_pe(pe, 0, 0, 0)
            sb_item_pe(pe, 0, 0, 3)
            sb_turns(pe, sb_pair_pe)
            sb_pv_pe(pe, SB_PAIRS - 1, 1, 1)
            pe.wait_ge(so_lo_s, SB_PAIRS - 1)
            for n in range(3):
                out_part(pe, CH_OUT1, n, out1_at, *((6, 7) if n < 2 else (4, 5)))
            out_pe(pe, CH_OUT1, 2, out1_at, (so_lo_s, SB_PAIRS), (7, 7, 5))
            stat_pe(pe, N_POST_A1, 0, AD0[N_POST_A1 + 1], 3)
            spread_pe(pe, N_POST_A1, 0)
            gu_pe(pe, CH_GU1, 1, N_FFN1)
            last_pe(pe)


_INS = ['x', 'mix_pre_g', 'mix_post_g', 'ffn_pre_g', 'ffn_post_g', 'ab_w_in', 'mla_q_norm_g', 'mla_w_uq',
        'mla_kv_norm_g', 'mla_w_ukv', 'ab_w_out', 'rel_bias', 'sb_w_qkv', 'sb_w_out', 'ffn_w_gate_up', 'ffn_w_down']
_OUTS = [((1, T, D), 'float32')]


def kernel(**inputs):
    import numpy as _np
    import concourse.bacc as _bacc
    from concourse import mybir as _mybir
    from concourse.bass_utils import run_bass_kernel_spmd as _run

    nc = _bacc.Bacc("TRN2", target_bir_lowering=False, num_devices=1)
    arrays, args = {}, []
    for name in _INS:
        a = _np.ascontiguousarray(inputs[name])
        arrays[f"in_{name}_dram"] = a
        args.append(nc.dram_tensor(f"in_{name}_dram", a.shape, _mybir.dt.from_np(a.dtype), kind="ExternalInput").ap())
    for i, (shape, dtype) in enumerate(_OUTS):
        dt = _mybir.dt.from_np(_np.dtype(dtype))
        args.append(nc.dram_tensor(f"out_{i}_dram", shape, dt, kind="ExternalOutput").ap())
    bass_hybrid_two_layers(nc, *args)
    r = _run(nc, [arrays], core_ids=[0])
    got = tuple(r.results[0][f"out_{i}_dram"] for i in range(len(_OUTS)))
    return got[0]
```
